# Optimizing a Trainium2 kernel written in Bass

```python
import jax, jax.numpy as jnp
from jax import lax
import numpy as np

D_MODEL = 1024
BATCH = 1
SEQ = 256
DEPTH = 2

HEAD_DIM = 64
D_MIX = D_MODEL
RET_HEADS = D_MIX // 4 // HEAD_DIM
RET_W = RET_HEADS * HEAD_DIM
SWA_HEADS = D_MIX // 2 // HEAD_DIM
SWA_KV_HEADS = 2
SWA_GROUP = SWA_HEADS // SWA_KV_HEADS
SWA_W = SWA_HEADS * HEAD_DIM
SWA_KV_W = SWA_KV_HEADS * HEAD_DIM
CONV_CH = D_MIX - RET_W - SWA_W
CONV_GROUPS = 4
CONV_GROUP_DIM = CONV_CH // CONV_GROUPS
CONV_WIDTH = 31
WINDOW = 128
BLOCK = 128
RET_CHUNK = 128
ROPE_THETA = 500000.0
ROPE_DIM = HEAD_DIM // 4
RET_ROPE_THETA = 10000.0
D_FF = 256 * ((8 * D_MODEL // 3 + 255) // 256)
N_EXPERTS = 8
TOP_K = 2
D_FF_EXPERT = 7 * D_MODEL // 2
EPS = 1e-6
NEG_INF = -1e30
N_DENSE = (DEPTH + 1) // 2
N_MOE = DEPTH // 2
D_IN = 4 * RET_W + SWA_W + 2 * SWA_KV_W + 2 * CONV_CH
SPLITS = [RET_W, 2 * RET_W, 3 * RET_W, 4 * RET_W, 4 * RET_W + SWA_W,
          4 * RET_W + SWA_W + SWA_KV_W, 4 * RET_W + SWA_W + 2 * SWA_KV_W]

kernel_name = "hymba_style_retention_swa_conformer_moe"

def rmsnorm(x, g):
    xf = x.astype(jnp.float32)
    y = xf * lax.rsqrt(jnp.mean(xf * xf, axis=-1, keepdims=True) + EPS)
    return (y * g.astype(jnp.float32)).astype(x.dtype)

def rope(x, theta, rot_dim):
    S = x.shape[1]
    half = rot_dim // 2
    inv = 1.0 / (theta ** (jnp.arange(half, dtype=jnp.float32) / half))
    ang = jnp.arange(S, dtype=jnp.float32)[:, None] * inv[None, :]
    cos = jnp.cos(ang)[None, :, None, :]
    sin = jnp.sin(ang)[None, :, None, :]
    xr = x[..., :rot_dim].astype(jnp.float32)
    x1, x2 = xr[..., :half], xr[..., half:]
    rot = jnp.concatenate([x1 * cos - x2 * sin, x2 * cos + x1 * sin], axis=-1).astype(x.dtype)
    return jnp.concatenate([rot, x[..., rot_dim:]], axis=-1)

def retention(q, k, v, g, gn_g):
    B, S, H, D = q.shape
    C = RET_CHUNK
    N = S // C
    dt = q.dtype
    qf = rope(q, RET_ROPE_THETA, D).astype(jnp.float32).reshape(B, N, C, H, D)
    kf = (rope(k, RET_ROPE_THETA, D).astype(jnp.float32) * D ** -0.5).reshape(B, N, C, H, D)
    vf = v.astype(jnp.float32).reshape(B, N, C, H, D)
    lg = jnp.log(1.0 - 2.0 ** (-5.0 - jnp.arange(H, dtype=jnp.float32)))
    idx = jnp.arange(C)
    rel = idx[:, None] - idx[None, :]
    dmask = jnp.where(rel[None] >= 0, jnp.exp(jnp.maximum(rel, 0)[None].astype(jnp.float32) * lg[:, None, None]), 0.0)
    scores = jnp.einsum('bnihd,bnjhd->bnhij', qf, kf) * dmask[None, None]
    intra = jnp.einsum('bnhij,bnjhd->bnihd', scores, vf)
    k_decay = jnp.exp((C - 1 - idx)[:, None].astype(jnp.float32) * lg[None, :])
    kv = jnp.einsum('bnjhd,jh,bnjhe->bnhde', kf, k_decay, vf)
    chunk_decay = jnp.exp(C * lg)[None, :, None, None]

    def step(state, kv_n):
        return state * chunk_decay + kv_n, state

    _, prev = lax.scan(step, jnp.zeros((B, H, D, D), jnp.float32), jnp.moveaxis(kv, 1, 0))
    prev = jnp.moveaxis(prev, 0, 1)
    q_decay = jnp.exp((idx + 1)[:, None].astype(jnp.float32) * lg[None, :])
    cross = jnp.einsum('bnihd,bnhde,ih->bnihe', qf, prev, q_decay)
    o = (intra + cross).reshape(B, S, H, D)
    mu = jnp.mean(o, axis=-1, keepdims=True)
    var = jnp.mean(jnp.square(o - mu), axis=-1, keepdims=True)
    o = ((o - mu) * lax.rsqrt(var + EPS)).reshape(B, S, H * D) * gn_g.astype(jnp.float32)
    return (jax.nn.silu(g.astype(jnp.float32)) * o).astype(dt)

def sliding_window_attention(q, k, v, sinks):
    B, S, _, D = q.shape
    NB = S // BLOCK
    q = rope(q, ROPE_THETA, ROPE_DIM)
    k = rope(k, ROPE_THETA, ROPE_DIM)
    qb = q.reshape(B, NB, BLOCK, SWA_KV_HEADS, SWA_GROUP, D)
    kb = k.reshape(B, NB, BLOCK, SWA_KV_HEADS, D)
    vb = v.reshape(B, NB, BLOCK, SWA_KV_HEADS, D)
    pad = ((0, 0), (1, 0), (0, 0), (0, 0), (0, 0))
    kband = jnp.concatenate([jnp.pad(kb, pad)[:, :-1], kb], axis=2)
    vband = jnp.concatenate([jnp.pad(vb, pad)[:, :-1], vb], axis=2)
    s = jnp.einsum('bnqhgd,bnkhd->bnhgqk', qb, kband).astype(jnp.float32) * D ** -0.5
    qi = jnp.arange(BLOCK)[:, None] + BLOCK
    kj = jnp.arange(2 * BLOCK)[None, :]
    rel = qi - kj
    allowed = (rel >= 0) & (rel < WINDOW)
    nb = jnp.arange(NB)[:, None, None]
    valid = allowed[None] & ((nb > 0) | (kj[None] >= BLOCK))
    s = jnp.where(valid[None, :, None, None], s, NEG_INF)
    sink = sinks.astype(jnp.float32).reshape(1, 1, SWA_KV_HEADS, SWA_GROUP, 1, 1)
    m = jnp.maximum(jnp.max(s, axis=-1, keepdims=True), sink)
    p = jnp.exp(s - m)
    p = p / (jnp.sum(p, axis=-1, keepdims=True) + jnp.exp(sink - m))
    o = jnp.einsum('bnhgqk,bnkhd->bnqhgd', p.astype(v.dtype), vband)
    return o.reshape(B, S, SWA_W)

def conformer_conv(u, dw_w, dw_b, ln_g, ln_b, pw_w):
    B, S, _ = u.shape
    a, gate = u[..., :CONV_CH], u[..., CONV_CH:]
    h = a * jax.nn.sigmoid(gate)
    h = lax.conv_general_dilated(h, dw_w[:, None, :], window_strides=(1,),
                                 padding=[(CONV_WIDTH - 1, 0)],
                                 dimension_numbers=('NWC', 'WIO', 'NWC'),
                                 feature_group_count=CONV_CH) + dw_b
    hf = h.astype(jnp.float32)
    mu = jnp.mean(hf, axis=-1, keepdims=True)
    var = jnp.mean(jnp.square(hf - mu), axis=-1, keepdims=True)
    hf = (hf - mu) * lax.rsqrt(var + EPS) * ln_g.astype(jnp.float32) + ln_b.astype(jnp.float32)
    h = jax.nn.silu(hf).astype(u.dtype).reshape(B, S, CONV_GROUPS, CONV_GROUP_DIM)
    return jnp.einsum('bsgc,gcd->bsgd', h, pw_w).reshape(B, S, CONV_CH)

def mixer(h, w_in, ret_gn_g, sinks, dw_w, dw_b, ln_g, ln_b, pw_w, w_out):
    B, S, _ = h.shape
    z = h @ w_in
    rq, rk, rv, rg, sq, sk, sv, cu = jnp.split(z, SPLITS, axis=-1)
    hd = (B, S, -1, HEAD_DIM)
    y_ret = retention(rq.reshape(hd), rk.reshape(hd), rv.reshape(hd), rg, ret_gn_g)
    y_swa = sliding_window_attention(sq.reshape(hd), sk.reshape(hd), sv.reshape(hd), sinks)
    y_conv = conformer_conv(cu, dw_w, dw_b, ln_g, ln_b, pw_w)
    return jnp.concatenate([y_ret, y_swa, y_conv], axis=-1) @ w_out

def swiglu(h, w_gate, w_up, w_down):
    return (jax.nn.silu(h @ w_gate) * (h @ w_up)) @ w_down

def moe(h, w_router, w_gate, w_up, w_down):
    B, S, D = h.shape
    t = h.reshape(B * S, D)
    logits = (t @ w_router).astype(jnp.float32)
    top_vals, top_idx = lax.top_k(logits, TOP_K)
    weights = jax.nn.softmax(top_vals, axis=-1)
    gates = jnp.sum(jax.nn.one_hot(top_idx, N_EXPERTS, dtype=jnp.float32) * weights[..., None], axis=1)
    y = jnp.zeros_like(t)
    for e in range(N_EXPERTS):
        y = y + gates[:, e:e + 1].astype(t.dtype) * swiglu(t, w_gate[e], w_up[e], w_down[e])
    return y.reshape(B, S, D)

def setup_inputs(seed: int = 0) -> dict:
    key = jax.random.key(seed)
    ks = jax.random.split(key, 24)
    f32 = jnp.float32

    def nrm(k, shape, scale):
        return jax.random.normal(k, shape, f32) * scale

    return {
        "x": nrm(ks[0], (BATCH, SEQ, D_MODEL), 1.0),
        "norm_mix_g": 1.0 + nrm(ks[1], (DEPTH, D_MODEL), 0.02),
        "w_in": nrm(ks[2], (DEPTH, D_MODEL, D_IN), D_MODEL ** -0.5),
        "ret_gn_g": 1.0 + nrm(ks[3], (DEPTH, RET_W), 0.02),
        "attn_sinks": nrm(ks[4], (DEPTH, SWA_HEADS), 0.5),
        "conv_dw_w": nrm(ks[5], (DEPTH, CONV_WIDTH, CONV_CH), CONV_WIDTH ** -0.5),
        "conv_dw_b": nrm(ks[6], (DEPTH, CONV_CH), 0.02),
        "conv_ln_g": 1.0 + nrm(ks[7], (DEPTH, CONV_CH), 0.02),
        "conv_ln_b": nrm(ks[8], (DEPTH, CONV_CH), 0.02),
        "conv_pw_w": nrm(ks[9], (DEPTH, CONV_GROUPS, CONV_GROUP_DIM, CONV_GROUP_DIM), CONV_GROUP_DIM ** -0.5),
        "w_out": nrm(ks[10], (DEPTH, D_MIX, D_MODEL), D_MIX ** -0.5),
        "norm_ffn_g": 1.0 + nrm(ks[11], (DEPTH, D_MODEL), 0.02),
        "ffn_w_gate": nrm(ks[12], (N_DENSE, D_MODEL, D_FF), D_MODEL ** -0.5),
        "ffn_w_up": nrm(ks[13], (N_DENSE, D_MODEL, D_FF), D_MODEL ** -0.5),
        "ffn_w_down": nrm(ks[14], (N_DENSE, D_FF, D_MODEL), D_FF ** -0.5),
        "moe_router": nrm(ks[15], (N_MOE, D_MODEL, N_EXPERTS), D_MODEL ** -0.5),
        "moe_w_gate": nrm(ks[16], (N_MOE, N_EXPERTS, D_MODEL, D_FF_EXPERT), D_MODEL ** -0.5),
        "moe_w_up": nrm(ks[17], (N_MOE, N_EXPERTS, D_MODEL, D_FF_EXPERT), D_MODEL ** -0.5),
        "moe_w_down": nrm(ks[18], (N_MOE, N_EXPERTS, D_FF_EXPERT, D_MODEL), D_FF_EXPERT ** -0.5),
        "final_norm_g": 1.0 + nrm(ks[19], (D_MODEL,), 0.02),
    }

def reference(x, norm_mix_g, w_in, ret_gn_g, attn_sinks, conv_dw_w, conv_dw_b, conv_ln_g, conv_ln_b,
              conv_pw_w, w_out, norm_ffn_g, ffn_w_gate, ffn_w_up, ffn_w_down, moe_router, moe_w_gate,
              moe_w_up, moe_w_down, final_norm_g):
    for l in range(DEPTH):
        h = rmsnorm(x, norm_mix_g[l])
        x = x + mixer(h, w_in[l], ret_gn_g[l], attn_sinks[l], conv_dw_w[l], conv_dw_b[l],
                      conv_ln_g[l], conv_ln_b[l], conv_pw_w[l], w_out[l])
        h = rmsnorm(x, norm_ffn_g[l])
        if l % 2 == 0:
            j = l // 2
            x = x + swiglu(h, ffn_w_gate[j], ffn_w_up[j], ffn_w_down[j])
        else:
            j = l // 2
            x = x + moe(h, moe_router[j], moe_w_gate[j], moe_w_up[j], moe_w_down[j])
    return rmsnorm(x, final_norm_g)


_drawn_inputs = setup_inputs


def setup_inputs(seed=0):
    import zlib

    import numpy as np

    out = dict(_drawn_inputs(seed))
    spreads = {}
    factors = {'ret_gn_g': 13.156,
     'attn_sinks': 8.801,
     'conv_ln_b': 3.444,
     'final_norm_g': 22.808,
     'conv_dw_b': 2.795,
     'conv_ln_g': 4.72,
     'norm_ffn_g': 3.585}
    for name, (base, spread) in spreads.items():
        noise = np.random.default_rng([zlib.crc32(name.encode()), seed]).standard_normal(out[name].shape)
        drawn = base * np.exp(spread * noise) if base else spread * noise
        out[name] = __import__('jax').numpy.asarray(drawn.astype(out[name].dtype))
    for name, factor in factors.items():
        out[name] = (out[name] * factor).astype(out[name].dtype)
    return out
```

```python
from contextlib import ExitStack

import numpy as np

import concourse.bass as bass
from concourse import mybir

F32 = mybir.dt.float32
F32R = mybir.dt.float32r
BF16 = mybir.dt.bfloat16
I32 = mybir.dt.int32
ALU = mybir.AluOpType
ACT = mybir.ActivationFunctionType
AX = mybir.AxisListType.X

P = 128
SEQ, DM = 256, 1024
DEPTH = 2
NT = SEQ // P
KD = DM // P
HD = 64
RH, RW = 4, 256
SH, SG = 8, 4
CC, CW = 256, 31
NC_CH = CC // P
FF = 2816
FE = 3584
NE = 8
EPS = 1e-6
NEG = -1e30
UNIT = 2048
RAW, SPLIT = 6, 3
TURN = 6
assert TURN % RAW == 0 and TURN % SPLIT == 0
WIN_UNITS, WOUT_UNITS = 9, 4
MIX_UNITS = WIN_UNITS + WOUT_UNITS
FC = FF // 256
EC = FE // 512
FFN_BASE = MIX_UNITS
MIX_BASE = [0, MIX_UNITS + 3 * FC]
MOE_BASE = MIX_BASE[1] + MIX_UNITS
ITEM = 6 * EC
assert ITEM % TURN == 0
WIN_ORDER = [8, 7, 4, 5, 6, 0, 1, 2, 3]

CONST = {}
_at = 0
for _n, _w in (("ident", P), ("mean", P), ("ones", P), ("before", P), ("slot0", P), ("slot1", P),
               ("ret_cos", NT * 32), ("ret_sin", NT * 32), ("swa_cos", NT * 8), ("swa_sin", NT * 8),
               ("decay", RH * 384), ("band", 2 * P), ("rev8", NE), ("idx8", NE)):
    CONST[_n] = (_at, _w)
    _at += _w
NCONST = _at


def shape_constants():
    c = np.zeros((P, NCONST), np.float32)

    def put(name, value):
        a, w = CONST[name]
        c[:, a:a + w] = np.asarray(value, np.float32).reshape(-1, w)

    p = np.arange(P)
    put("ident", np.eye(P))
    put("mean", np.full((P, P), 1.0 / CC))
    put("ones", np.ones((P, P)))
    put("before", p[:, None] < p[None, :])
    put("slot0", np.tile(p, (P, 1)))
    put("slot1", np.tile(p + P, (P, 1)))
    for name, theta, half in (("ret", 10000.0, 32), ("swa", 500000.0, 8)):
        inv = (1.0 / (np.float32(theta) ** (np.arange(half, dtype=np.float32) / np.float32(half)))).astype(np.float32)
        ang = np.arange(SEQ, dtype=np.float32)[:, None] * inv[None, :]
        for f, g in (("cos", np.cos), ("sin", np.sin)):
            put(f"{name}_{f}", g(ang).astype(np.float32).reshape(NT, P, half).transpose(1, 0, 2))
    lg = np.log(1.0 - 2.0 ** (-5.0 - np.arange(RH)))
    rel = np.arange(SEQ)[None, :] - p[:, None]
    near = np.where(rel[None] >= 0, np.exp(np.maximum(rel, 0)[None] * lg[:, None, None]), 0.0) * HD ** -0.5
    put("decay", np.concatenate([near, near[:, :, :P]], 2).transpose(1, 0, 2))
    i, j = p[:, None], p[None, :]
    put("band", np.concatenate([np.where(j > i, 0.0, NEG), np.where(j <= i, 0.0, NEG)], 1))
    put("rev8", np.tile(NE - np.arange(NE), (P, 1)))
    put("idx8", np.tile(np.arange(NE), (P, 1)))
    return c


def trunk(nc, t_in, out):
    ctx = ExitStack()
    with ctx:
        def sb(name, shape, dt=F32):
            return ctx.enter_context(nc.sbuf_tensor(name, shape, dt))

        def sem(name):
            return ctx.enter_context(nc.semaphore(name))

        raw = sb("raw", [P, RAW, UNIT])
        w_hi = sb("w_hi", [P, SPLIT, UNIT], F32R)
        w_lo = sb("w_lo", [P, SPLIT, UNIT], F32R)
        const = sb("const", [P, NCONST])
        zeros = sb("zeros", [P, 512], BF16)
        x = sb("x", [P, NT, DM])
        h = sb("h", [P, NT, DM])
        gain = sb("gain", [P, DM])
        t_hi = sb("t_hi", [P, KD, SEQ], F32R)
        t_lo = sb("t_lo", [P, KD, SEQ], F32R)
        act_hi = sb("act_hi", [P, 512], F32R)
        act_lo = sb("act_lo", [P, 512], F32R)
        hid = sb("hid", [P, 512])
        gact = sb("gact", [P, 512])
        work = sb("work", [P, NT * 1792])
        z = work[:, :].rearrange("p (t n) -> p t n", t=NT)
        chan_rows = sb("chan_rows", [36, CC])
        chan = sb("chan", [P, NC_CH, 36])
        sinks = sb("sinks", [P, SH])
        glu = sb("glu", [P, NC_CH, CW - 1 + SEQ])
        conv = sb("conv", [P, NC_CH, SEQ])
        conv_sq = sb("conv_sq", [P, NC_CH, SEQ])
        conv_rstd = sb("conv_rstd", [P, SEQ])
        pw = sb("pw", [P, NC_CH, P])
        scores = h[:, :, :].rearrange("p t n -> p (t n)")
        probs_t = sb("probs_t", [P, SG, 384])
        sq_t = sb("sq_t", [P, SG, SEQ])
        sk_t = sb("sk_t", [P, SEQ])
        rq_t = sb("rq_t", [P, 2, SEQ])
        rk_t = sb("rk_t", [P, 2, SEQ])
        ret_s = sb("ret_s", [P, RH, 384])
        ret_o = sb("ret_o", [P, NT * RH, HD])
        rope_a = sb("rope_a", [P, 512])
        rope_b = sb("rope_b", [P, 512])
        small = sb("small", [P, 256])
        table = sb("table", [P, 4], I32)
        h_t = work[:, 0:KD * SEQ].rearrange("p (k n) -> p k n", k=KD)
        y_exp = work[:, 0:DM]
        router = work[:, 2560:2560 + KD * NE].rearrange("p (k e) -> p k e", k=KD)
        pick = ret_s[:, 0, 0:256].rearrange("p (t n) -> p t n", t=NT)
        pick_g = ret_s[:, 1, 0:256].rearrange("p (t n) -> p t n", t=NT)
        pick_gt = ret_s[:, 2, 0:256]
        mine = ret_s[:, 3, 0:4]
        bank = [ctx.enter_context(nc.psum_tensor(f"bank{i}", [P, 512], F32)) for i in range(8)]

        def const_ap(name):
            a, w = CONST[name]
            return const[:, a:a + w]

        ident, before, ones, mean = (const_ap(n) for n in ("ident", "before", "ones", "mean"))

        raw_loaded = [sem(f"raw_loaded{i}") for i in range(RAW)]
        hi_done, lo_done, multiplied = sem("hi_done"), sem("lo_done"), sem("multiplied")
        vec_step, act_step, pool_step = sem("vec_step"), sem("act_step"), sem("pool_step")
        const_loaded, x_loaded, router_loaded = sem("const_loaded"), sem("x_loaded"), sem("router_loaded")
        gain_loaded = sem("gain_loaded")
        zeros_set = sem("zeros_set")
        x_updated = sem("x_updated")
        sq_summed, ms_done, rms_done = sem("sq_summed"), sem("ms_done"), sem("rms_done")
        h_normed = sem("h_normed")
        h_turned, t_hi_done, t_lo_done = sem("h_turned"), sem("t_hi_done"), sem("t_lo_done")
        stored = sem("stored")
        names = """chan_loaded chan_turned chan_done sinks_loaded pw_loaded pw_zeroed pads_zeroed
            gate_done glu_done z_copied conv_done conv_mean conv_centred conv_squared conv_var conv_var_eps
            conv_std conv_scaled conv_act conv_mixed swa_roped ret_roped sq_turned sqt_copied score_made
            score_max probs_made sink_exp probs_scaled probs_turned probs_copied attended rq_turned
            rqt_copied ret_scored ret_decayed ret_attended ret_gate ret_var ret_std ret_normed ret_turned
            y_hi_done y_lo_done""".split()
        S = [{n: sem(f"{n}_{l}") for n in names} for l in range(DEPTH)]
        gate_acted, hid_made, hid_hi, hid_lo = sem("gate_acted"), sem("hid_made"), sem("hid_hi"), sem("hid_lo")
        hid_turned = sem("hid_turned")
        logits_made, top_two, second_exp, chosen, ranked, routed, table_made = (
            sem(n) for n in "logits_made top_two second_exp chosen ranked routed table_made".split())
        picks_made, x_gathered, x_hi, x_lo, g_turned, g_copied, y_copied, scattered, x_final = (
            sem(n) for n in "picks_made x_gathered x_hi x_lo g_turned g_copied y_copied scattered x_final".split())
        y_copied_vec = sem("y_copied_vec")

        def u_count(c, turn):
            return 6 * turn + (c + 1)

        def load_unit(sp, c, turn, source, split_dims=None):
            if not (isinstance(turn, int) and c + 6 * turn < RAW):
                sp.wait_ge(lo_done, u_count(c - RAW, turn))
            dst = raw[:, c % RAW, :].rearrange("p (k n) -> p k n", k=source.shape[1])
            sp.dma_start(dst, source).then_inc(raw_loaded[c % RAW], 16)

        def split_hi(act, c, turn):
            act.wait_ge(raw_loaded[c % RAW], 16 * (turn + (c // RAW + 1)))
            if not (isinstance(turn, int) and c + 6 * turn < SPLIT):
                act.wait_ge(multiplied, u_count(c - SPLIT, turn))
            act.activation(w_hi[:, c % SPLIT, :], raw[:, c % RAW, :], ACT.Copy).then_inc(hi_done, 1)

        def split_lo(dve, c, turn):
            dve.wait_ge(hi_done, u_count(c, turn))
            dve.tensor_tensor(w_lo[:, c % SPLIT, :], raw[:, c % RAW, :], w_hi[:, c % SPLIT, :].bitcast(F32),
                              ALU.subtract).then_inc(lo_done, 1)

        def unit(c, k):
            return [w[:, c % SPLIT, :].rearrange("p (k n) -> p k n", k=k) for w in (w_hi, w_lo)]

        def score_view(p, i):
            return scores[:, p * 256:(p + 1) * 256] if i else scores[:, 1024 + p * P:1024 + (p + 1) * P]

        def tokens2(b):
            return b[:, :].rearrange("p (t n) -> p t n", t=2)

        HI_LO = ((0, 0), (0, 1), (1, 0))

        win_v = [t_in["w_in"][l].rearrange("(k p) n -> p k n", p=P) for l in range(DEPTH)]
        wout_v = [t_in["w_out"][l].rearrange("(k p) n -> p k n", p=P) for l in range(DEPTH)]
        fg_v, fu_v = (t_in[n][0].rearrange("(k p) n -> p k n", p=P) for n in ("ffn_w_gate", "ffn_w_up"))
        fd_v = t_in["ffn_w_down"][0].rearrange("(k p) n -> p k n", p=P)
        eg_v, eu_v, ed_v = (t_in[n][0].rearrange("e (k p) n -> p e k n", p=P)
                            for n in ("moe_w_gate", "moe_w_up", "moe_w_down"))
        x_v = t_in["x"][0].rearrange("(t p) n -> p t n", p=P)
        out_v = out[0].rearrange("(t p) n -> p t n", p=P)
        gains = [t_in["norm_mix_g"][0], t_in["norm_ffn_g"][0], t_in["norm_mix_g"][1], t_in["norm_ffn_g"][1],
                 t_in["final_norm_g"]]
        X_BEFORE = [0, 4, 8, 12]

        block = ctx.enter_context(nc.Block())

        @block.sync
        def _(sp):
            def load_gain(n):
                if n:
                    sp.wait_ge(h_normed, 2 * n)
                sp.dma_start(gain[:, :], gains[n].unsqueeze(0).broadcast_to([P, DM])).then_inc(gain_loaded, 16)

            def load_layer_vectors(l):
                s = S[l]
                if l:
                    sp.wait_ge(S[0]["chan_turned"], 1)
                    sp.wait_ge(S[0]["y_lo_done"], 8)
                sp.dma_start(chan_rows[0:CW, :], t_in["conv_dw_w"][l]).then_inc(s["chan_loaded"], 16)
                for r, n in enumerate(("conv_dw_b", "conv_ln_g", "conv_ln_b", "ret_gn_g")):
                    sp.dma_start(chan_rows[CW + r:CW + r + 1, :], t_in[n][l:l + 1, :]).then_inc(s["chan_loaded"], 16)
                sp.dma_start(sinks[:, :], t_in["attn_sinks"][l:l + 1, :].broadcast_to([P, SH])).then_inc(s["sinks_loaded"], 16)
                sp.wait_ge(s["pw_zeroed"], 1)
                for g in range(4):
                    a = 64 * (g % 2)
                    sp.dma_start(pw[a:a + 64, g // 2, a:a + 64], t_in["conv_pw_w"][l, g]).then_inc(s["pw_loaded"], 16)

            def load_mixer(l):
                c = MIX_BASE[l]
                for q, b in enumerate(WIN_ORDER):
                    load_unit(sp, c + q, 0, win_v[l][:, :, b * 256:(b + 1) * 256])
                for q in range(WOUT_UNITS):
                    load_unit(sp, c + WIN_UNITS + q, 0, wout_v[l][:, :, q * 256:(q + 1) * 256])

            sp.dma_start(x[:, :, :], x_v).then_inc(x_loaded, 16)
            sp.dma_start(const[:, :], t_in["constants"]).then_inc(const_loaded, 16)
            load_gain(0)
            load_layer_vectors(0)
            load_mixer(0)
            load_gain(1)
            c = FFN_BASE
            load_unit(sp, c, 0, fg_v[:, :, 0:256])
            load_unit(sp, c + 1, 0, fu_v[:, :, 0:256])
            with sp.Fori(0, (FC - 1) // 2) as it:
                for j in range(2):
                    a = c + 2 + 3 * j
                    cols = bass.ds(it * 512 + (256 + 256 * j), 256)
                    load_unit(sp, a, it, fg_v[:, :, cols])
                    load_unit(sp, a + 1, it, fd_v[:, bass.ds(it * 4 + 2 * j, 2), :])
                    load_unit(sp, a + 2, it, fu_v[:, :, cols])
            load_unit(sp, c + 3 * FC - 1, 0, fd_v[:, 2 * (FC - 1):2 * FC, :])
            load_gain(2)
            load_layer_vectors(1)
            load_mixer(1)
            load_gain(3)
            sp.wait_ge(S[1]["y_lo_done"], 8)
            sp.dma_start(router, t_in["moe_router"][0].rearrange("(k p) e -> p k e", p=P)).then_inc(router_loaded, 16)

            def load_item(e, turn):
                c = MOE_BASE

                def pair(c, turn, view, chunk, rows):
                    for k in range(2):
                        if rows:
                            source = view[:, e, bass.ds(chunk * 4 + 2 * k, 2), :]
                        else:
                            source = view[:, e, 4 * k:4 * k + 4, bass.ds(chunk * 512, 512)]
                        load_unit(sp, c + k, turn, squeeze(source))

                def squeeze(a):
                    return a if len(a.shape) == 3 else a.rearrange("p o k n -> p (o k) n")

                pair(c, turn, eg_v, 0, False)
                pair(c + 2, turn, eu_v, 0, False)
                with sp.Fori(0, EC - 1) as i:
                    pair(c + 4, turn + i, eg_v, i + 1, False)
                    pair(c + 6, turn + i, ed_v, i, True)
                    pair(c + 8, turn + i, eu_v, i + 1, False)
                pair(c + 4, turn + (EC - 1), ed_v, EC - 1, True)

            with sp.Fori(0, NE) as e:
                load_item(e, e * EC)
            sp.wait_ge(table_made, 1)
            n_over = sp.value_load(table[0:1, 0:1], min_val=0, max_val=3)
            with sp.If(n_over > 0):
                with sp.Fori(0, n_over) as j:
                    load_item(sp.value_load(table[0:1, bass.ds(j + 1, 1)], min_val=0, max_val=NE - 1),
                              (j + NE) * EC)
            load_gain(4)
            for t in range(NT):
                sp.wait_ge(h_normed, 8 + t + 1)
                sp.dma_start(out_v[:, t, :], h[:, t, :]).then_inc(stored, 16)
            sp.wait_ge(stored, 16 * NT)

        @block.gpsimd
        def _(pool):
            n_step = [0]

            def link(ins):
                n_step[0] += 1
                ins.then_inc(pool_step, 1)
                pool.wait_ge(pool_step, n_step[0])

            def rope(heads, first, half, tab, done):
                view = z[:, :, first:first + heads * HD].rearrange("p t (h d) -> p t h d", d=HD)
                cos, sin = (const_ap(f"{tab}_{f}").rearrange("p (t d) -> p t d", t=NT) for f in ("cos", "sin"))
                a, b = (r[:, 0:heads * half].rearrange("p (h d) -> p h d", d=half) for r in (rope_a, rope_b))
                for t in range(NT):
                    x1, x2 = view[:, t, :, 0:half], view[:, t, :, half:2 * half]
                    c = cos[:, t, :].unsqueeze(1).broadcast_to([P, heads, half])
                    d = sin[:, t, :].unsqueeze(1).broadcast_to([P, heads, half])
                    link(pool.tensor_tensor(a, x1, d, ALU.mult))
                    link(pool.tensor_tensor(b, x2, d, ALU.mult))
                    link(pool.tensor_tensor(x1, x1, c, ALU.mult))
                    link(pool.tensor_tensor(x2, x2, c, ALU.mult))
                    link(pool.tensor_tensor(x1, x1, b, ALU.subtract))
                    pool.tensor_tensor(x2, x2, a, ALU.add).then_inc(done, 1)
                    pool.wait_ge(done, t + 1)

            pool.memset(zeros[:, :], 0.0).then_inc(zeros_set, 1)
            pool.memset(glu[:, :, 0:CW - 1], 0.0).then_inc(S[0]["pads_zeroed"], 1)
            pool.wait_ge(const_loaded, 16)
            for l in range(DEPTH):
                s = S[l]
                if l:
                    pool.wait_ge(S[0]["conv_mixed"], 1)
                pool.memset(pw[:, :, :], 0.0).then_inc(s["pw_zeroed"], 1)
                pool.wait_ge(s["z_copied"], 3)
                rope(SH + 2, 1024, 8, "swa", s["swa_roped"])
                pool.wait_ge(s["z_copied"], 7)
                rope(2 * RH, 0, 32, "ret", s["ret_roped"])

            pool.wait_ge(routed, 1)
            rank = small[:, 64:80].rearrange("p (t e) -> p t e", t=NT)
            gates = small[:, 80:96].rearrange("p (t e) -> p t e", t=NT)

            def make_picks(e, n, slots):
                if not (isinstance(n, int) and n == 0):
                    pool.wait_ge(g_turned, n)
                    pool.wait_ge(x_gathered, 2 * n)
                    pool.wait_ge(picks_made, 7 * n)
                pool.tensor_copy(mine[:, 0:2], rank[:, :, bass.ds(e, 1)].rearrange("p t o -> p (t o)")
                                 ).then_inc(picks_made, 1)
                pool.tensor_copy(mine[:, 2:4], gates[:, :, bass.ds(e, 1)].rearrange("p t o -> p (t o)")
                                 ).then_inc(picks_made, 1)
                pool.wait_ge(picks_made, 7 * n + 2)
                pool.tensor_tensor(rope_a[:, 0:2], mine[:, 0:2], mine[:, 2:4], ALU.mult).then_inc(picks_made, 1)
                for t in range(NT):
                    pool.tensor_scalar(pick[:, t, :], slots, mine[:, t:t + 1], None,
                                       ALU.is_equal).then_inc(picks_made, 1)
                    pool.tensor_scalar(pick_g[:, t, :], slots, mine[:, t:t + 1], mine[:, 2 + t:3 + t],
                                       ALU.is_equal, ALU.mult).then_inc(picks_made, 1)

            make_picks(0, 0, const_ap("slot0"))
            with pool.Fori(1, NE) as e:
                make_picks(e, e, const_ap("slot0"))
            pool.wait_ge(table_made, 1)
            n_over = pool.value_load(table[0:1, 0:1], min_val=0, max_val=3)
            with pool.If(n_over > 0):
                with pool.Fori(0, n_over) as j:
                    e = pool.value_load(table[0:1, bass.ds(j + 1, 1)], min_val=0, max_val=NE - 1)
                    make_picks(e, j + NE, const_ap("slot1"))

        @block.scalar
        def _(act):
            def norm(n):
                if n in (1, 2, 3):
                    act.wait_ge(x_updated, 4 * n)
                elif n == 4:
                    act.wait_ge(x_final, 1)
                for t in range(NT):
                    act.activation(h[:, t, :], x[:, t, :], ACT.Square,
                                   accum_out=small[:, t:t + 1]).then_inc(sq_summed, 1)
                act.wait_ge(ms_done, n + 1)
                act.activation(small[:, 4:6], small[:, 2:4], ACT.Sqrt).then_inc(rms_done, 1)

            def turn_h(n):
                dst = h_t if n == 3 else t_hi
                for b in range(4):
                    act.wait_ge(h_turned, 4 * n + b + 1)
                    act.activation(dst[:, 2 * b:2 * b + 2, :], tokens2(bank[4 + b]), ACT.Copy).then_inc(t_hi_done, 1)

            def round_y(l, k, src, scale=None):
                for i in range(2):
                    act.activation(t_hi[:, k + i, :], src[:, i * 256:(i + 1) * 256], ACT.Copy,
                                   scale=scale[i] if scale else 1.0).then_inc(S[l]["y_hi_done"], 1)

            def mixer(l):
                s = S[l]
                c = MIX_BASE[l]
                act.wait_ge(s["chan_turned"], 1)
                act.activation(chan[:, :, 0:35], bank[3][:, 0:72].rearrange("p (c n) -> p c n", c=2)[:, :, 0:35],
                               ACT.Copy).then_inc(s["chan_done"], 1)
                for q in range(WIN_UNITS):
                    split_hi(act, c + q + 2, 0)
                    act.wait_ge(multiplied, c + q + 1)
                    if q == 0:
                        act.activation(gact[:, :], bank[0][:, :], ACT.Sigmoid).then_inc(s["gate_done"], 1)
                    elif q > 1:
                        b = WIN_ORDER[q]
                        dst, src = z[:, :, b * 256:(b + 1) * 256], tokens2(bank[q % 2])
                        if b in (4, 5):
                            dst = z[:, :, 1024:1536].rearrange("p t (h g d) -> p t h g d", g=2, d=HD)[:, :, :, b - 4, :]
                            src = src.rearrange("p t (h d) -> p t h d", d=HD)
                        act.activation(dst, src, ACT.Copy).then_inc(s["z_copied"], 1)
                split_hi(act, c + WIN_UNITS + 2, 0)

                def exps(g):
                    act.wait_ge(s["score_max"], g + 1)
                    for i in range(2):
                        for p in range(SG):
                            n = g * 8 + i * 4 + p
                            v = score_view(p, i)
                            act.activation(v, v, ACT.Exp, bias=small[:, 32 + n:33 + n],
                                           accum_out=small[:, 48 + n:49 + n]).then_inc(s["probs_made"], 1)
                    act.activation(small[:, 96 + 8 * g:104 + 8 * g], small[:, 112 + 8 * g:120 + 8 * g],
                                   ACT.Exp).then_inc(s["sink_exp"], 1)

                def copy_probs(g):
                    for b in range(3):
                        act.wait_ge(s["probs_turned"], 3 * g + b + 1)
                        act.activation(probs_t[:, :, b * P:(b + 1) * P],
                                       bank[([4, 5, 6], [7, 0, 1])[g][b]][:, :].rearrange("p (h n) -> p h n", h=SG),
                                       ACT.Copy).then_inc(s["probs_copied"], 1)

                for b in range(3):
                    act.wait_ge(s["sq_turned"], b + 1)
                    if b < 2:
                        act.activation(sq_t[:, 2 * b:2 * b + 2, :], tokens2(bank[4 + b]), ACT.Copy).then_inc(s["sqt_copied"], 1)
                    else:
                        act.activation(sk_t[:, :], bank[6][:, 0:256], ACT.Copy).then_inc(s["sqt_copied"], 1)
                exps(0)
                copy_probs(0)
                act.wait_ge(s["attended"], 1)
                round_y(l, 2, bank[4])
                for b in range(2):
                    act.wait_ge(s["rq_turned"], b + 1)
                    act.activation((rq_t, rk_t)[b][:, :, :], tokens2(bank[5 + b]), ACT.Copy).then_inc(s["rqt_copied"], 1)
                exps(1)
                act.wait_ge(s["conv_centred"], 1)
                act.activation(conv_sq[:, :, :], conv[:, :, :], ACT.Square).then_inc(s["conv_squared"], 1)
                copy_probs(1)
                act.wait_ge(s["attended"], 2)
                round_y(l, 4, bank[7])
                act.wait_ge(s["conv_var_eps"], 1)
                act.activation(conv_rstd[:, :], conv_rstd[:, :], ACT.Sqrt).then_inc(s["conv_std"], 1)
                act.activation(tokens2(gact), z[:, :, 768:1024], ACT.Silu).then_inc(s["ret_gate"], 1)
                act.wait_ge(s["conv_scaled"], 1)
                for i in range(NC_CH):
                    act.activation(conv_sq[:, i, :], conv[:, i, :], ACT.Silu, bias=chan[:, i, CW + 2:CW + 3],
                                   scale=chan[:, i, CW + 1:CW + 2]).then_inc(s["conv_act"], 1)
                act.wait_ge(s["conv_mixed"], 1)
                round_y(l, 6, bank[3])
                act.wait_ge(s["ret_var"], 1)
                act.activation(small[:, 136:144], small[:, 136:144], ACT.Sqrt).then_inc(s["ret_std"], 1)
                act.wait_ge(s["ret_turned"], 1)
                round_y(l, 0, bank[5], [chan[:, i, CW + 3:CW + 4] for i in range(2)])
                for q in range(1, WOUT_UNITS):
                    split_hi(act, c + WIN_UNITS + q + 2, 0)

            for c in range(SPLIT - 1):
                split_hi(act, c, 0)
            act.wait_ge(x_loaded, 16)
            norm(0)
            turn_h(0)
            mixer(0)
            norm(1)
            turn_h(1)

            def act_gate(c, turn, m):
                act.wait_ge(multiplied, u_count(c, turn))
                if not (isinstance(m, int) and m == 0):
                    act.wait_ge(hid_made, m)
                act.activation(gact[:, :], bank[0][:, :], ACT.Silu).then_inc(gate_acted, 1)

            def round_ffn(m):
                act.wait_ge(hid_made, m + 1)
                act.activation(act_hi[:, :], hid[:, :], ACT.Copy).then_inc(hid_hi, 1)

            c = FFN_BASE
            split_hi(act, c + 2, 0)
            act_gate(c, 0, 0)
            split_hi(act, c + 3, 0)
            round_ffn(0)
            with act.Fori(0, (FC - 1) // 2) as it:
                for j in range(2):
                    a, m = c + 2 + 3 * j, it * 2 + (1 + j)
                    split_hi(act, a + 2, it)
                    act_gate(a, it, m)
                    split_hi(act, a + 3, it)
                    split_hi(act, a + 4, it)
                    round_ffn(m)
            split_hi(act, c + 3 * FC + 1, 0)
            norm(2)
            turn_h(2)
            mixer(1)
            norm(3)
            turn_h(3)
            act.wait_ge(top_two, 1)
            act.activation(small[:, 20:22], small[:, 18:20], ACT.Exp).then_inc(second_exp, 1)

            def round_x(n):
                for b in range(2):
                    act.wait_ge(x_gathered, 2 * n + (b + 1))
                    act.activation(t_hi[:, 4 * b:4 * b + 4, 0:P], bank[6 + b][:, :].rearrange("p (k n) -> p k n", k=4),
                                   ACT.Copy).then_inc(x_hi, 1)

            def round_hid(m):
                act.wait_ge(hid_turned, m + 1)
                act.activation(act_hi[:, :], bank[2][:, :], ACT.Copy).then_inc(hid_hi, 1)

            def expert(n, turn, ahead):
                c = MOE_BASE
                m = n * EC
                split_hi(act, c + 2, turn)
                split_hi(act, c + 3, turn)
                act_gate(c + 1, turn, m + FC)
                act.wait_ge(g_turned, n + 1)
                act.activation(pick_gt, bank[3][:, 0:256], ACT.Copy).then_inc(g_copied, 1)
                split_hi(act, c + 4, turn)
                split_hi(act, c + 5, turn)
                with act.Fori(0, EC - 1) as i:
                    a, at = c + 4, turn + i
                    split_hi(act, a + 2, at)
                    round_hid(m + i)
                    split_hi(act, a + 3, at)
                    act_gate(a + 1, at, m + i + (FC + 1))
                    for k in range(4, 8):
                        split_hi(act, a + k, at)
                last = turn + (EC - 1)
                if ahead:
                    round_x(n + 1)
                round_hid(m + (EC - 1))
                if ahead:
                    split_hi(act, c + 6, last)
                    split_hi(act, c + 7, last)
                act.wait_ge(multiplied, u_count(c + 5, last))
                act.activation(y_exp[:, 0:512], bank[4][:, :], ACT.Copy).then_inc(y_copied, 1)

            round_x(0)
            with act.Fori(0, NE - 1) as e:
                expert(e, e * EC, True)
            expert(NE - 1, (NE - 1) * EC, False)
            act.wait_ge(table_made, 1)
            n_over = act.value_load(table[0:1, 0:1], min_val=0, max_val=3)
            with act.If(n_over > 0):
                with act.Fori(0, n_over) as j:
                    for k in range(2):
                        split_hi(act, MOE_BASE + k, (j + NE) * EC)
                    round_x(j + NE)
                    expert(j + NE, (j + NE) * EC, False)
            norm(4)

        @block.vector
        def _(dve):
            n_step = [0]

            def link(ins):
                n_step[0] += 1
                ins.then_inc(vec_step, 1)
                dve.wait_ge(vec_step, n_step[0])

            def norm(n):
                dve.wait_ge(sq_summed, 2 * n + 2)
                dve.tensor_scalar(small[:, 2:4], small[:, 0:2], 1.0 / DM, EPS, ALU.mult, ALU.add).then_inc(ms_done, 1)
                dve.wait_ge(rms_done, n + 1)
                link(dve.reciprocal(small[:, 6:8], small[:, 4:6]))
                dve.wait_ge(gain_loaded, 16 * (n + 1))
                for t in range(NT):
                    dve.scalar_tensor_tensor(out=h[:, t, :], in0=x[:, t, :], scalar=small[:, 6 + t:7 + t], in1=gain[:, :],
                                             op0=ALU.mult, op1=ALU.mult).then_inc(h_normed, 1)

            def turn_h(n):
                for b in range(4):
                    dve.wait_ge(t_hi_done, 4 * n + b + 1)
                    dve.tensor_tensor(t_lo[:, 2 * b:2 * b + 2, :], tokens2(bank[4 + b]),
                                      t_hi[:, 2 * b:2 * b + 2, :].bitcast(F32), ALU.subtract).then_inc(t_lo_done, 1)

            def rest_y(l, k, src, n, scale=None):
                for i in range(2):
                    dve.wait_ge(S[l]["y_hi_done"], n + 2)
                    o, a, b = t_lo[:, k + i, :], src[:, i * 256:(i + 1) * 256], t_hi[:, k + i, :].bitcast(F32)
                    if scale:
                        ins = dve.scalar_tensor_tensor(out=o, in0=a, scalar=scale[i], in1=b, op0=ALU.mult, op1=ALU.subtract)
                    else:
                        ins = dve.tensor_tensor(o, a, b, ALU.subtract)
                    ins.then_inc(S[l]["y_lo_done"], 1)

            def mixer(l):
                s = S[l]
                c = MIX_BASE[l]
                taps = [(k, i) for k in range(CW) for i in range(NC_CH)]

                def tap(k, i):
                    v, w = glu[:, i, k:k + SEQ], chan[:, i, k:k + 1]
                    if k == 0:
                        ins = dve.tensor_scalar(conv[:, i, :], v, w, chan[:, i, CW:CW + 1], ALU.mult, ALU.add)
                    else:
                        dve.wait_ge(s["conv_done"], (k - 1) * NC_CH + i + 1)
                        ins = dve.scalar_tensor_tensor(out=conv[:, i, :], in0=v, scalar=w, in1=conv[:, i, :],
                                                       op0=ALU.mult, op1=ALU.add)
                    ins.then_inc(s["conv_done"], 1)

                for q in range(WIN_UNITS):
                    split_lo(dve, c + q + 2, 0)
                    if q == 1:
                        dve.wait_ge(s["gate_done"], 1)
                        dve.wait_ge(multiplied, c + 2)
                        dve.wait_ge(S[0]["pads_zeroed"], 1)
                        dve.tensor_tensor(glu[:, :, CW - 1:], tokens2(bank[1]), tokens2(gact), ALU.mult).then_inc(s["glu_done"], 1)
                        dve.wait_ge(s["glu_done"], 1)
                        dve.wait_ge(s["chan_done"], 1)
                    if q >= 1:
                        for _ in range(8):
                            if taps:
                                tap(*taps.pop(0))
                while taps:
                    tap(*taps.pop(0))
                split_lo(dve, c + WIN_UNITS + 2, 0)

                band = const_ap("band")

                def read_scores(g):
                    b = ([4, 5, 6], [7, 0, 1])[g]
                    dve.wait_ge(s["score_made"], 3 * g + 3)
                    if g:
                        dve.wait_ge(s["probs_turned"], 3)
                    for k in range(2):
                        dve.scalar_tensor_tensor(
                            out=scores[:, k * 512:(k + 1) * 512].rearrange("p (h n) -> p h n", h=2),
                            in0=tokens2(bank[b[k]]), scalar=HD ** -0.5,
                            in1=band.unsqueeze(1).broadcast_to([P, 2, 256]), op0=ALU.mult, op1=ALU.add).then_inc(vec_step, 1)
                        n_step[0] += 1
                    link(dve.scalar_tensor_tensor(
                        out=scores[:, 1024:1536].rearrange("p (h n) -> p h n", h=SG),
                        in0=bank[b[2]][:, :].rearrange("p (h n) -> p h n", h=SG), scalar=HD ** -0.5,
                        in1=band[:, P:2 * P].unsqueeze(1).broadcast_to([P, SG, P]), op0=ALU.mult, op1=ALU.add))
                    top = small[:, 176 + 8 * g:184 + 8 * g]
                    dve.tensor_reduce(top[:, 0:4], scores[:, 1024:1536].rearrange("p (h n) -> p h n", h=SG), AX,
                                      ALU.max).then_inc(vec_step, 1)
                    n_step[0] += 1
                    link(dve.tensor_reduce(top[:, 4:8], scores[:, 0:1024].rearrange("p (h n) -> p h n", h=SG), AX, ALU.max))
                    own = sinks[:, g * SG:(g + 1) * SG].unsqueeze(1).broadcast_to([P, 2, SG])
                    dve.wait_ge(s["sinks_loaded"], 16)
                    link(dve.tensor_tensor(top.rearrange("p (i h) -> p i h", i=2), top.rearrange("p (i h) -> p i h", i=2),
                                           own, ALU.max))
                    neg = small[:, 32 + 8 * g:40 + 8 * g]
                    link(dve.tensor_scalar(neg, top, -1.0, None, ALU.mult))
                    dve.tensor_tensor(small[:, 112 + 8 * g:120 + 8 * g].rearrange("p (i h) -> p i h", i=2), own,
                                      neg.rearrange("p (i h) -> p i h", i=2), ALU.add).then_inc(s["score_max"], 1)

                def scale_probs(g):
                    dve.wait_ge(s["probs_made"], 8 * g + 8)
                    dve.wait_ge(s["sink_exp"], g + 1)
                    r = small[:, 160 + 8 * g:168 + 8 * g]
                    link(dve.tensor_tensor(r, small[:, 48 + 8 * g:56 + 8 * g], small[:, 96 + 8 * g:104 + 8 * g], ALU.add))
                    link(dve.reciprocal(r, r))
                    for i in range(2):
                        v = (scores[:, 0:1024] if i else scores[:, 1024:1536]).rearrange("p (h n) -> p h n", h=SG)
                        dve.tensor_tensor(v, v, r[:, 4 * i:4 * i + 4].unsqueeze(2).broadcast_to([P, SG, v.shape[2]]),
                                          ALU.mult).then_inc(s["probs_scaled"], 1)

                read_scores(0)
                scale_probs(0)
                dve.wait_ge(s["conv_mean"], 1)
                dve.wait_ge(s["conv_done"], CW * NC_CH)
                dve.tensor_tensor(conv[:, :, :], conv[:, :, :], bank[2][:, 0:256].unsqueeze(1).broadcast_to([P, 2, 256]),
                                  ALU.subtract).then_inc(s["conv_centred"], 1)
                read_scores(1)
                rest_y(l, 2, bank[4], 0)
                scale_probs(1)
                rest_y(l, 4, bank[7], 2)
                dve.wait_ge(s["conv_var"], 1)
                dve.tensor_scalar(conv_rstd[:, :], bank[2][:, 256:512], EPS, None, ALU.add).then_inc(s["conv_var_eps"], 1)
                dve.wait_ge(s["conv_std"], 1)
                link(dve.reciprocal(conv_rstd[:, :], conv_rstd[:, :]))
                dve.wait_ge(s["conv_centred"], 1)
                dve.tensor_tensor(conv[:, :, :], conv[:, :, :], conv_rstd[:, :].unsqueeze(1).broadcast_to([P, 2, 256]),
                                  ALU.mult).then_inc(s["conv_scaled"], 1)
                decay = const_ap("decay").rearrange("p (h n) -> p h n", h=RH)
                for i, b in enumerate((5, 6, 0, 1)):
                    dve.wait_ge(s["ret_scored"], i + 1)
                    dve.tensor_tensor(ret_s[:, i, :], bank[b][:, 0:384], decay[:, i, :], ALU.mult).then_inc(s["ret_decayed"], 1)
                rest_y(l, 6, bank[3], 4)
                dve.wait_ge(s["ret_attended"], 1)
                o = bank[6][:, :].rearrange("p (g d) -> p g d", d=HD)
                mu, var, std, rstd = (small[:, a:a + 8] for a in (128, 144, 136, 152))

                def wide(v):
                    return v.unsqueeze(2).broadcast_to([P, NT * RH, HD])

                link(dve.tensor_reduce(mu, o, AX, ALU.add))
                link(dve.tensor_scalar(mu, mu, 1.0 / HD, None, ALU.mult))
                link(dve.tensor_tensor(ret_o[:, :, :], o, wide(mu), ALU.subtract))
                square = rope_a[:, :].rearrange("p (g d) -> p g d", d=HD)
                link(dve.tensor_tensor(square, ret_o[:, :, :], ret_o[:, :, :], ALU.mult))
                link(dve.tensor_reduce(var, square, AX, ALU.add))
                dve.tensor_scalar(std, var, 1.0 / HD, EPS, ALU.mult, ALU.add).then_inc(s["ret_var"], 1)
                dve.wait_ge(s["ret_std"], 1)
                link(dve.reciprocal(rstd, std))
                link(dve.tensor_tensor(ret_o[:, :, :], ret_o[:, :, :], wide(rstd), ALU.mult))
                dve.wait_ge(s["ret_gate"], 1)
                dve.tensor_tensor(ret_o[:, :, :], ret_o[:, :, :], gact[:, :].rearrange("p (g d) -> p g d", d=HD),
                                  ALU.mult).then_inc(s["ret_normed"], 1)
                rest_y(l, 0, bank[5], 6, [chan[:, i, CW + 3:CW + 4] for i in range(2)])
                for q in range(WOUT_UNITS):
                    if q:
                        split_lo(dve, c + WIN_UNITS + q + 2, 0)
                    dve.wait_ge(multiplied, c + WIN_UNITS + q + 1)
                    v = x[:, :, q * 256:(q + 1) * 256]
                    dve.tensor_tensor(v, v, tokens2(bank[q % 2]), ALU.add).then_inc(x_updated, 1)

            for c in range(SPLIT - 1):
                split_lo(dve, c, 0)
            norm(0)
            turn_h(0)
            mixer(0)
            norm(1)
            turn_h(1)

            def make_hid(c, turn, m, up):
                dve.wait_ge(multiplied, u_count(c, turn))
                dve.wait_ge(gate_acted, m + 1)
                if not (isinstance(m, int) and m == 0):
                    dve.wait_ge(hid_hi, m)
                    dve.wait_ge(hid_lo, m)
                dve.tensor_tensor(hid[:, :], gact[:, :], up[:, :], ALU.mult).then_inc(hid_made, 1)

            def rest_hid(m, src):
                dve.wait_ge(hid_hi, m + 1)
                dve.tensor_tensor(act_lo[:, :], src[:, :], act_hi[:, :].bitcast(F32), ALU.subtract).then_inc(hid_lo, 1)

            c = FFN_BASE
            split_lo(dve, c + 2, 0)
            split_lo(dve, c + 3, 0)
            make_hid(c + 1, 0, 0, bank[2])
            rest_hid(0, hid)
            with dve.Fori(0, (FC - 1) // 2) as it:
                for j in range(2):
                    a, m = c + 2 + 3 * j, it * 2 + (1 + j)
                    split_lo(dve, a + 2, it)
                    split_lo(dve, a + 3, it)
                    split_lo(dve, a + 4, it)
                    make_hid(a + 2, it, m, bank[2])
                    rest_hid(m, hid)
            split_lo(dve, c + 3 * FC + 1, 0)
            dve.wait_ge(multiplied, c + 3 * FC)
            dve.wait_ge(x_updated, 4)
            for t in range(NT):
                for i in range(2):
                    v = x[:, t, i * 512:(i + 1) * 512]
                    dve.tensor_tensor(v, v, bank[4 + 2 * t + i][:, :], ALU.add).then_inc(x_updated, 1)
            norm(2)
            turn_h(2)
            mixer(1)
            norm(3)

            def cols(a, w=2 * NE):
                return small[:, a:a + w]

            def by_token(v):
                return v.rearrange("p (t e) -> p t e", t=NT)

            def wide8(v):
                return v.unsqueeze(2).broadcast_to([P, NT, NE])

            idx = const_ap("rev8").unsqueeze(1).broadcast_to([P, NT, NE])
            logits, first, second, cand = (by_token(cols(a)) for a in (32, 96, 112, 160))
            top1, top2, pos, gap, e2, den, w1, w2 = (small[:, a:a + 2] for a in (10, 12, 14, 18, 20, 22, 24, 26))
            dve.wait_ge(logits_made, 1)
            link(dve.tensor_copy(logits, bank[3][:, 0:16].rearrange("p (t e) -> p t e", t=NT)))

            def one_hot(top, hot):
                link(dve.tensor_reduce(top, logits, AX, ALU.max))
                link(dve.tensor_tensor(cand, logits, wide8(top), ALU.is_equal))
                link(dve.tensor_tensor(cand, cand, idx, ALU.mult))
                link(dve.tensor_reduce(pos, cand, AX, ALU.max))
                link(dve.tensor_tensor(hot, cand, wide8(pos), ALU.is_equal))

            one_hot(top1, first)
            link(dve.scalar_tensor_tensor(out=logits, in0=first, scalar=-3e38, in1=logits, op0=ALU.mult, op1=ALU.add))
            one_hot(top2, second)
            dve.tensor_tensor(gap, top2, top1, ALU.subtract).then_inc(top_two, 1)
            sel = by_token(cols(192))
            dve.tensor_tensor(sel, first, second, ALU.add).then_inc(chosen, 1)
            dve.wait_ge(second_exp, 1)
            link(dve.tensor_scalar(den, e2, 1.0, None, ALU.add))
            link(dve.reciprocal(w1, den))
            link(dve.tensor_tensor(w2, e2, w1, ALU.mult))
            gates, rank = by_token(cols(80)), by_token(cols(64))
            link(dve.tensor_tensor(gates, first, wide8(w1), ALU.mult))
            link(dve.tensor_tensor(second, second, wide8(w2), ALU.mult))
            link(dve.tensor_tensor(gates, gates, second, ALU.add))
            dve.wait_ge(ranked, 1)
            counts = small[:, 208:232]
            link(dve.tensor_copy(counts, bank[3][:, 16:40]))
            link(dve.scalar_tensor_tensor(out=rank, in0=by_token(counts[:, 0:16]), scalar=1.0, in1=sel, op0=ALU.add,
                                          op1=ALU.mult))
            dve.tensor_scalar(rank, rank, -1.0, None, ALU.add).then_inc(routed, 1)
            over, upto, hot = small[:, 232:240], small[:, 240:248], small[:, 248:256]
            listed = small[:, 96:100]
            link(dve.tensor_scalar(over, counts[:, 16:24], float(P), None, ALU.is_gt))
            link(dve.memset(hot, 0.0))
            link(dve.tensor_tensor_scan(upto, over, hot, 0.0, ALU.add, ALU.add))
            link(dve.tensor_copy(listed[:, 0:1], upto[:, 7:8]))
            for j in range(3):
                link(dve.scalar_tensor_tensor(out=hot, in0=upto, scalar=float(j + 1), in1=over, op0=ALU.is_equal,
                                              op1=ALU.mult))
                link(dve.tensor_tensor(hot, hot, const_ap("idx8"), ALU.mult))
                link(dve.tensor_reduce(listed[:, j + 1:j + 2], hot, AX, ALU.add))
            dve.tensor_copy(table[:, :], listed).then_inc(table_made, 1)

            def rest_x(n):
                for b in range(2):
                    dve.wait_ge(x_hi, 2 * n + (b + 1))
                    dve.tensor_tensor(t_lo[:, 4 * b:4 * b + 4, 0:P], bank[6 + b][:, :].rearrange("p (k n) -> p k n", k=4),
                                      t_hi[:, 4 * b:4 * b + 4, 0:P].bitcast(F32), ALU.subtract).then_inc(x_lo, 1)

            def expert(n, turn, ahead):
                c = MOE_BASE
                m = n * EC + FC
                for k in range(2, 6):
                    split_lo(dve, c + k, turn)
                make_hid(c + 3, turn, m, bank[1])
                with dve.Fori(0, EC - 1) as i:
                    a, at = c + 4, turn + i
                    split_lo(dve, a + 2, at)
                    rest_hid(m + i, bank[2])
                    for k in range(3, 8):
                        split_lo(dve, a + k, at)
                    make_hid(a + 5, at, m + i + 1, bank[1])
                last = turn + (EC - 1)
                if ahead:
                    rest_x(n + 1)
                rest_hid(m + (EC - 1), bank[2])
                if ahead:
                    split_lo(dve, c + 6, last)
                    split_lo(dve, c + 7, last)
                dve.wait_ge(multiplied, u_count(c + 5, last))
                dve.tensor_copy(y_exp[:, 512:1024], bank[5][:, :]).then_inc(y_copied_vec, 1)
                dve.wait_ge(x_updated, 4 * n + 12)
                for q in range(4):
                    dve.wait_ge(scattered, 4 * n + (q + 1))
                    v = x[:, q // 2, (q % 2) * 512:(q % 2 + 1) * 512]
                    dve.tensor_tensor(v, v, bank[6 + q % 2][:, :], ALU.add).then_inc(x_updated, 1)

            rest_x(0)
            with dve.Fori(0, NE - 1) as e:
                expert(e, e * EC, True)
            expert(NE - 1, (NE - 1) * EC, False)
            dve.wait_ge(x_updated, 12 + 4 * NE)
            dve.wait_ge(table_made, 1)
            n_over = dve.value_load(table[0:1, 0:1], min_val=0, max_val=3)
            with dve.If(n_over > 0):
                with dve.Fori(0, n_over) as j:
                    for k in range(2):
                        split_lo(dve, MOE_BASE + k, (j + NE) * EC)
                    rest_x(j + NE)
                    expert(j + NE, (j + NE) * EC, False)
                    dve.wait_ge(x_updated, 4 * j + (16 + 4 * NE))
                    link_free = dve.memset(small[:, 9:10], 0.0)
            dve.memset(small[:, 8:9], 0.0).then_inc(x_final, 1)
            norm(4)

        @block.tensor
        def _(pe):
            def turn_rows(n):
                pe.wait_ge(h_normed, 2 * n + 2)
                if n == 0:
                    pe.wait_ge(const_loaded, 16)
                for b in range(4):
                    for k in range(2):
                        for t in range(NT):
                            f = (2 * b + k) * P
                            ins = pe.transpose(bank[4 + b][:, k * 256 + t * P:k * 256 + (t + 1) * P],
                                               h[:, t, f:f + P], ident)
                    ins.then_inc(h_turned, 1)

            def turn_channels(l):
                s = S[l]
                pe.wait_ge(const_loaded, 16)
                pe.wait_ge(s["chan_loaded"], 16 * 5)
                for i in range(NC_CH):
                    ins = pe.transpose(bank[3][:, i * 36:i * 36 + 35], chan_rows[0:35, i * P:(i + 1) * P], ident[0:35, 0:35])
                ins.then_inc(s["chan_turned"], 1)

            def rows_by_weights(dst, c, turn):
                w = unit(c, KD)
                for t in range(NT):
                    for k in range(KD):
                        for a, b in HI_LO:
                            ins = pe.matmul(dst[:, t * 256:(t + 1) * 256], (t_hi, t_lo)[a][:, k, t * P:(t + 1) * P],
                                            w[b][:, k, :], start=(k == 0 and (a, b) == (0, 0)),
                                            stop=(k == KD - 1 and (a, b) == (1, 0)))
                ins.then_inc(multiplied, 1)

            def weights_by_rows(dst, c, turn):
                w = unit(c, KD)
                for i in range(2):
                    for k in range(KD):
                        for a, b in HI_LO:
                            ins = pe.matmul(dst[:, i * 256:(i + 1) * 256], w[b][:, k, i * P:(i + 1) * P],
                                            (t_hi, t_lo)[a][:, k, :], start=(k == 0 and (a, b) == (0, 0)),
                                            stop=(k == KD - 1 and (a, b) == (1, 0)))
                ins.then_inc(multiplied, 1)

            def mixer(l):
                s = S[l]
                c = MIX_BASE[l]
                for q in range(WIN_UNITS):
                    pe.wait_ge(lo_done, c + q + 1)
                    if q == 0:
                        pe.wait_ge(t_lo_done, 4 * 2 * l + 4)
                    if q in (0, 1) and l:
                        pass
                    if q == 2:
                        pe.wait_ge(s["gate_done"], 1)
                    elif q == 3:
                        pe.wait_ge(s["glu_done"], 1)
                    elif q > 3:
                        pe.wait_ge(s["z_copied"], q - 3)
                    (weights_by_rows if q < 2 else rows_by_weights)(bank[q % 2], c + q, 0)

                pe.wait_ge(s["swa_roped"], 2)
                for b in range(2):
                    for k in range(2):
                        p = 2 * b + k
                        for t in range(NT):
                            two = z[:, t, 1024 + p * P:1024 + (p + 1) * P]
                            ins = pe.transpose(bank[4 + b][:, k * 256 + t * P:k * 256 + (t + 1) * P], two, ident)
                    ins.then_inc(s["sq_turned"], 1)
                for t in range(NT):
                    ins = pe.transpose(bank[6][:, t * P:(t + 1) * P], z[:, t, 1536:1664], ident)
                ins.then_inc(s["sq_turned"], 1)
                BANKS = ([4, 5, 6], [7, 0, 1])
                for g in range(2):
                    a = 64 * g
                    pe.wait_ge(s["sqt_copied"], 3)
                    if g:
                        pe.wait_ge(s["z_copied"], 7)
                    for p in range(SG):
                        ins = pe.matmul(bank[BANKS[g][p // 2]][:, (p % 2) * 256:(p % 2 + 1) * 256],
                                        sq_t[a:a + 64, p, P:2 * P], sk_t[a:a + 64, :], start=True, stop=True)
                        if p % 2:
                            ins.then_inc(s["score_made"], 1)
                    for p in range(SG):
                        ins = pe.matmul(bank[BANKS[g][2]][:, p * P:(p + 1) * P], sq_t[a:a + 64, p, 0:P],
                                        sk_t[a:a + 64, 0:P], start=True, stop=True)
                    ins.then_inc(s["score_made"], 1)
                pe.wait_ge(s["conv_done"], CW * NC_CH)
                for i in range(NC_CH):
                    ins = pe.matmul(bank[2][:, 0:256], mean, conv[:, i, :], start=(i == 0), stop=(i == 1))
                ins.then_inc(s["conv_mean"], 1)

                def attend(g):
                    pe.wait_ge(s["probs_scaled"], 2 * g + 2)
                    for b in range(3):
                        for p in range(SG):
                            v = score_view(p, 0) if b == 0 else score_view(p, 1)[:, (b - 1) * P:b * P]
                            ins = pe.transpose(bank[BANKS[g][b]][:, p * P:(p + 1) * P], v, ident)
                        ins.then_inc(s["probs_turned"], 1)
                    pe.wait_ge(s["probs_copied"], 3 * g + 3)
                    v = z[:, :, 1664 + g * HD:1664 + (g + 1) * HD]
                    for p in range(SG):
                        o = bank[BANKS[g][0]][64 * (p % 2):64 * (p % 2) + 64, (p // 2) * 256:(p // 2 + 1) * 256]
                        pe.matmul(o, v[:, 0, :], probs_t[:, p, 0:256], start=True, stop=False)
                        ins = pe.matmul(o[:, P:], v[:, 1, :], probs_t[:, p, 256:384], start=False, stop=True)
                    ins.then_inc(s["attended"], 1)

                attend(0)
                pe.wait_ge(s["ret_roped"], 2)
                for b in range(2):
                    for k in range(2):
                        for t in range(NT):
                            f = b * 256 + k * P
                            ins = pe.transpose(bank[5 + b][:, k * 256 + t * P:k * 256 + (t + 1) * P], z[:, t, f:f + P], ident)
                    ins.then_inc(s["rq_turned"], 1)
                attend(1)
                pe.wait_ge(s["conv_squared"], 1)
                for i in range(NC_CH):
                    ins = pe.matmul(bank[2][:, 256:512], mean, conv_sq[:, i, :], start=(i == 0), stop=(i == 1))
                ins.then_inc(s["conv_var"], 1)
                pe.wait_ge(s["rqt_copied"], 2)
                for i, b in enumerate((5, 6, 0, 1)):
                    q, k = (v[64 * (i % 2):64 * (i % 2) + 64, i // 2, :] for v in (rq_t, rk_t))
                    pe.matmul(bank[b][:, 0:256], k[:, 0:P], q, start=True, stop=True)
                    pe.matmul(bank[b][:, 256:384], k[:, P:], q[:, P:], start=True, stop=True).then_inc(s["ret_scored"], 1)
                pe.wait_ge(s["conv_act"], 2)
                pe.wait_ge(s["pw_loaded"], 16 * 4)
                for i in range(NC_CH):
                    ins = pe.matmul(bank[3][:, i * 256:(i + 1) * 256], pw[:, i, :], conv_sq[:, i, :], start=True, stop=True)
                ins.then_inc(s["conv_mixed"], 1)
                pe.wait_ge(s["ret_decayed"], RH)
                for t in range(NT):
                    for i in range(RH):
                        o = bank[6][:, (t * RH + i) * HD:(t * RH + i + 1) * HD]
                        v = z[:, :, 512 + i * HD:512 + (i + 1) * HD]
                        ins = pe.matmul(o, ret_s[:, i, t * P:(t + 1) * P], v[:, 0, :], start=True, stop=(t == 0))
                        if t:
                            ins = pe.matmul(o, ret_s[:, i, 256:384], v[:, 1, :], start=False, stop=True)
                ins.then_inc(s["ret_attended"], 1)
                pe.wait_ge(s["ret_normed"], 1)
                flat = ret_o[:, :, :].rearrange("p g d -> p (g d)")
                for k in range(2):
                    for t in range(NT):
                        ins = pe.transpose(bank[5][:, k * 256 + t * P:k * 256 + (t + 1) * P],
                                           flat[:, t * 256 + k * P:t * 256 + (k + 1) * P], ident)
                ins.then_inc(s["ret_turned"], 1)
                pe.wait_ge(s["y_lo_done"], 8)
                for q in range(WOUT_UNITS):
                    pe.wait_ge(lo_done, c + WIN_UNITS + q + 1)
                    if q >= 2:
                        pe.wait_ge(x_updated, 8 * l + q - 1)
                    rows_by_weights(bank[q % 2], c + WIN_UNITS + q, 0)

            turn_channels(0)
            turn_rows(0)
            mixer(0)
            turn_rows(1)

            c = FFN_BASE
            pe.wait_ge(zeros_set, 1)

            def clear(b):
                pe.matmul(bank[b][:, :], zeros[:, 0:P], zeros[:, :], start=True, stop=False, skip_group_check=True)

            def ffn_down(c, turn, m, last=False):
                pe.wait_ge(lo_done, u_count(c, turn))
                pe.wait_ge(hid_lo, m + 1)
                w = unit(c, 2)
                for f in range(2):
                    for t in range(NT):
                        for i in range(2):
                            for a, b in HI_LO:
                                ins = pe.matmul(bank[4 + 2 * t + i][:, :], (act_hi, act_lo)[a][:, f * 256 + t * P:f * 256 + (t + 1) * P],
                                                w[b][:, f, i * 512:(i + 1) * 512], start=False,
                                                stop=(last and f == 1 and (a, b) == (1, 0)), skip_group_check=True)
                ins.then_inc(multiplied, 1)

            pe.wait_ge(t_lo_done, 8)
            for b in range(4, 8):
                clear(b)
            pe.wait_ge(lo_done, c + 1)
            pe.wait_ge(x_updated, 4)
            weights_by_rows(bank[0], c, 0)
            pe.wait_ge(lo_done, c + 2)
            weights_by_rows(bank[2], c + 1, 0)
            with pe.Fori(0, (FC - 1) // 2) as it:
                for j in range(2):
                    a, m = c + 2 + 3 * j, it * 2 + (1 + j)
                    pe.wait_ge(lo_done, u_count(a, it))
                    pe.wait_ge(gate_acted, m)
                    weights_by_rows(bank[0], a, it)
                    ffn_down(a + 1, it, m - 1)
                    pe.wait_ge(lo_done, u_count(a + 2, it))
                    pe.wait_ge(hid_made, m)
                    weights_by_rows(bank[2], a + 2, it)
            ffn_down(c + 3 * FC - 1, 0, FC - 1, True)
            turn_channels(1)
            turn_rows(2)
            mixer(1)
            turn_rows(3)

            pe.wait_ge(t_hi_done, 16)
            pe.wait_ge(router_loaded, 16)
            for t in range(NT):
                for k in range(KD):
                    ins = pe.matmul(bank[3][:, t * NE:(t + 1) * NE], h_t[:, k, t * P:(t + 1) * P], router[:, k, :],
                                    start=(k == 0), stop=(k == KD - 1))
            ins.then_inc(logits_made, 1)
            pe.wait_ge(chosen, 1)
            sel = small[:, 192:208]
            pe.matmul(bank[3][:, 16:24], before, sel[:, 0:8], start=True, stop=True)
            pe.matmul(bank[3][:, 24:32], before, sel[:, 8:16], start=True, stop=False)
            pe.matmul(bank[3][:, 24:32], ones, sel[:, 0:8], start=False, stop=True)
            pe.matmul(bank[3][:, 32:40], ones, sel[:, 0:8], start=True, stop=False)
            pe.matmul(bank[3][:, 32:40], ones, sel[:, 8:16], start=False, stop=True).then_inc(ranked, 1)

            def gather(n, before_it):
                pe.wait_ge(picks_made, 7 * n + 7)
                if before_it is not None:
                    pe.wait_ge(x_updated, before_it)
                for b in range(2):
                    for k in range(4):
                        f = (4 * b + k) * P
                        for t in range(NT):
                            ins = pe.matmul(bank[6 + b][:, k * P:(k + 1) * P], h[:, t, f:f + P], pick[:, t, :],
                                            start=(t == 0), stop=(t == 1))
                    ins.then_inc(x_gathered, 1)

            def rows_by_expert(dst, c, turn, half):
                pe.wait_ge(lo_done, u_count(c, turn))
                w = unit(c, 4)
                for k in range(4):
                    for a, b in HI_LO:
                        ins = pe.matmul(dst[:, :], (t_hi, t_lo)[a][:, 4 * half + k, 0:P], w[b][:, k, :],
                                        start=(half == 0 and k == 0 and (a, b) == (0, 0)),
                                        stop=(half == 1 and k == 3 and (a, b) == (1, 0)), skip_group_check=True)
                ins.then_inc(multiplied, 1)

            def turn_hid(m):
                pe.wait_ge(hid_made, m + 1)
                pe.wait_ge(hid_lo, m)
                for k in range(4):
                    ins = pe.transpose(bank[2][:, k * P:(k + 1) * P], hid[:, k * P:(k + 1) * P], ident)
                ins.then_inc(hid_turned, 1)

            def expert_down(c, turn, m, half, last):
                pe.wait_ge(lo_done, u_count(c, turn))
                pe.wait_ge(hid_lo, m + 1)
                w = unit(c, 2)
                for f in range(2):
                    for i in range(2):
                        for a, b in HI_LO:
                            ins = pe.matmul(bank[4 + i][:, :], (act_hi, act_lo)[a][:, (2 * half + f) * P:(2 * half + f + 1) * P],
                                            w[b][:, f, i * 512:(i + 1) * 512], start=False,
                                            stop=(last and half == 1 and f == 1 and (a, b) == (1, 0)), skip_group_check=True)
                ins.then_inc(multiplied, 1)

            def expert(n, turn, ahead):
                c = MOE_BASE
                m = n * EC + FC
                pe.wait_ge(x_lo, 2 * n + 2)
                clear(4)
                clear(5)
                pe.wait_ge(gate_acted, m)
                for i in range(2):
                    rows_by_expert(bank[0], c + i, turn, i)
                for t in range(NT):
                    ins = pe.transpose(bank[3][:, t * P:(t + 1) * P], pick_g[:, t, :], ident)
                ins.then_inc(g_turned, 1)
                pe.wait_ge(hid_made, m)
                for i in range(2):
                    rows_by_expert(bank[1], c + 2 + i, turn, i)
                with pe.Fori(0, EC - 1) as i:
                    a, at = c + 4, turn + i
                    pe.wait_ge(gate_acted, m + i + 1)
                    rows_by_expert(bank[0], a, at, 0)
                    turn_hid(m + i)
                    rows_by_expert(bank[0], a + 1, at, 1)
                    for k in range(2):
                        expert_down(a + 2 + k, at, m + i, k, False)
                    for k in range(2):
                        rows_by_expert(bank[1], a + 4 + k, at, k)
                if ahead:
                    gather(n + 1, 4 * n + 12)
                turn_hid(m + (EC - 1))
                for k in range(2):
                    expert_down(c + 4 + k, turn + (EC - 1), m + (EC - 1), k, True)
                pe.wait_ge(g_copied, n + 1)
                pe.wait_ge(y_copied, n + 1)
                pe.wait_ge(y_copied_vec, n + 1)
                if ahead:
                    pe.wait_ge(x_lo, 2 * n + 4)
                for q in range(4):
                    t, i = q // 2, q % 2
                    if q >= 2:
                        pe.wait_ge(x_updated, 4 * n + (12 + q - 1))
                    pe.matmul(bank[6 + i][:, :], pick_gt[:, t * P:(t + 1) * P], y_exp[:, i * 512:(i + 1) * 512],
                              start=True, stop=True).then_inc(scattered, 1)

            gather(0, None)
            with pe.Fori(0, NE - 1) as e:
                expert(e, e * EC, True)
            expert(NE - 1, (NE - 1) * EC, False)
            pe.wait_ge(table_made, 1)
            n_over = pe.value_load(table[0:1, 0:1], min_val=0, max_val=3)
            with pe.If(n_over > 0):
                with pe.Fori(0, n_over) as j:
                    gather(j + NE, 4 * j + (12 + 4 * NE))
                    expert(j + NE, (j + NE) * EC, False)


INPUTS = ["x", "norm_mix_g", "w_in", "ret_gn_g", "attn_sinks", "conv_dw_w", "conv_dw_b", "conv_ln_g", "conv_ln_b",
          "conv_pw_w", "w_out", "norm_ffn_g", "ffn_w_gate", "ffn_w_up", "ffn_w_down", "moe_router", "moe_w_gate",
          "moe_w_up", "moe_w_down", "final_norm_g"]


def kernel(**inputs):
    import concourse.bacc as bacc
    from concourse.bass_utils import run_bass_kernel_spmd

    nc = bacc.Bacc("TRN2", target_bir_lowering=False, num_devices=1)
    arrays = {f"in_{n}": np.ascontiguousarray(inputs[n]) for n in INPUTS}
    arrays["in_constants"] = shape_constants()
    t_in = {n[3:]: nc.dram_tensor(n, a.shape, mybir.dt.from_np(a.dtype), kind="ExternalInput").ap()
            for n, a in arrays.items()}
    out = nc.dram_tensor("out", (1, SEQ, DM), F32, kind="ExternalOutput").ap()
    trunk(nc, t_in, out)
    return run_bass_kernel_spmd(nc, [arrays], core_ids=[0]).results[0]["out"]
```

```python
from contextlib import ExitStack

import numpy as np

import concourse.bass as bass
from concourse import mybir

F32 = mybir.dt.float32
F32R = mybir.dt.float32r
BF16 = mybir.dt.bfloat16
I32 = mybir.dt.int32
ALU = mybir.AluOpType
ACT = mybir.ActivationFunctionType
AX = mybir.AxisListType.X

P = 128
SEQ, DM = 256, 1024
DEPTH = 2
NT = SEQ // P
KD = DM // P
HD = 64
RH, RW = 4, 256
SH, SG = 8, 4
CC, CW = 256, 31
NC_CH = CC // P
FF = 2816
FE = 3584
NE = 8
EPS = 1e-6
NEG = -1e30
UNIT = 2048
RAW, SPLIT = 6, 3
TURN = 6
assert TURN % RAW == 0 and TURN % SPLIT == 0
WIN_UNITS, WOUT_UNITS = 9, 4
MIX_UNITS = WIN_UNITS + WOUT_UNITS
FC = FF // 256
EC = FE // 512
FFN_BASE = MIX_UNITS
MIX_BASE = [0, MIX_UNITS + 3 * FC]
MOE_BASE = MIX_BASE[1] + MIX_UNITS
ITEM = 6 * EC
assert ITEM % TURN == 0
WIN_ORDER = [8, 7, 4, 5, 6, 0, 1, 2, 3]

RET_HEADS = (0, 2, 1, 3)

CONST = {}
_at = 0
for _n, _w in (("ident", P), ("mean", P), ("ones", P), ("before", P), ("slot0", P), ("slot1", P),
               ("ret_cos", NT * 32), ("ret_sin", NT * 32), ("swa_cos", NT * 8), ("swa_sin", NT * 8),
               ("decay", RH * 384), ("band", 2 * P), ("rev8", NE), ("idx8", NE)):
    CONST[_n] = (_at, _w)
    _at += _w
NCONST = _at


def shape_constants():
    c = np.zeros((P, NCONST), np.float32)

    def put(name, value):
        a, w = CONST[name]
        c[:, a:a + w] = np.asarray(value, np.float32).reshape(-1, w)

    p = np.arange(P)
    put("ident", np.eye(P))
    put("mean", np.full((P, P), 1.0 / CC))
    put("ones", np.ones((P, P)))
    put("before", p[:, None] < p[None, :])
    put("slot0", np.tile(p, (P, 1)))
    put("slot1", np.tile(p + P, (P, 1)))
    for name, theta, half in (("ret", 10000.0, 32), ("swa", 500000.0, 8)):
        inv = (1.0 / (np.float32(theta) ** (np.arange(half, dtype=np.float32) / np.float32(half)))).astype(np.float32)
        ang = np.arange(SEQ, dtype=np.float32)[:, None] * inv[None, :]
        for f, g in (("cos", np.cos), ("sin", np.sin)):
            put(f"{name}_{f}", g(ang).astype(np.float32).reshape(NT, P, half).transpose(1, 0, 2))
    lg = np.log(1.0 - 2.0 ** (-5.0 - np.arange(RH)))
    rel = np.arange(SEQ)[None, :] - p[:, None]
    near = np.where(rel[None] >= 0, np.exp(np.maximum(rel, 0)[None] * lg[:, None, None]), 0.0) * HD ** -0.5
    near = near[list(RET_HEADS)].transpose(1, 0, 2)
    put("decay", np.concatenate([near.reshape(P, -1), near[:, :, :P].reshape(P, -1)], 1))
    i, j = p[:, None], p[None, :]
    put("band", np.concatenate([np.where(j > i, 0.0, NEG), np.where(j <= i, 0.0, NEG)], 1) * HD ** 0.5)
    put("rev8", np.tile(NE - np.arange(NE), (P, 1)))
    put("idx8", np.tile(np.arange(NE), (P, 1)))
    return c


def trunk(nc, t_in, out):
    ctx = ExitStack()
    with ctx:
        def sb(name, shape, dt=F32):
            return ctx.enter_context(nc.sbuf_tensor(name, shape, dt))

        def sem(name):
            return ctx.enter_context(nc.semaphore(name))

        raw = sb("raw", [P, RAW, UNIT])
        w_hi = sb("w_hi", [P, SPLIT, UNIT], F32R)
        w_lo = sb("w_lo", [P, SPLIT, UNIT], F32R)
        const = sb("const", [P, NCONST])
        zeros = sb("zeros", [P, 512], BF16)
        x = sb("x", [P, NT, DM])
        h = sb("h", [P, NT, DM])
        gain_rows = sb("gain_rows", [4 * KD, P])
        gain_cols = sb("gain_cols", [P, 4 * KD])
        squares = sb("squares", [P, NT, 4])
        t_hi = sb("t_hi", [P, KD, SEQ], F32R)
        t_lo = sb("t_lo", [P, KD, SEQ], F32R)
        act_hi = sb("act_hi", [P, 512], F32R)
        act_lo = sb("act_lo", [P, 512], F32R)
        hid = sb("hid", [P, 512])
        gact = sb("gact", [P, 512])
        work = sb("work", [P, NT * 1792])
        z = work[:, :].rearrange("p (t n) -> p t n", t=NT)
        chan_rows = sb("chan_rows", [36, CC])
        chan = sb("chan", [P, NC_CH, 36])
        sinks = sb("sinks", [P, SH])
        glu = sb("glu", [P, NC_CH, CW - 1 + SEQ])
        conv = sb("conv", [P, NC_CH, SEQ])
        conv_sq = sb("conv_sq", [P, NC_CH, SEQ])
        conv_diag = sb("conv_diag", [P, SEQ])
        pw = sb("pw", [P, NC_CH, P])
        scores = [h[:, :, :].rearrange("p t n -> p (t n)")[:, 0:1536], sb("scores1", [P, 1536])[:, :]]
        ident_bf = sb("ident_bf", [P, P], BF16)
        band_bf = sb("band_bf", [P, 2 * P], BF16)
        probs_t = sb("probs_t", [P, SG, 384])
        sq_t = sb("sq_t", [P, SG, SEQ])
        sk_t = sb("sk_t", [P, SEQ])
        rq_t = sb("rq_t", [P, 2, SEQ])
        rk_t = sb("rk_t", [P, 2, SEQ])
        ret_s = sb("ret_s", [P, RH * 384])
        ret_o = sb("ret_o", [P, NT * RH, HD])
        rope_a = sb("rope_a", [P, 512])
        rope_b = sb("rope_b", [P, 512])
        small = sb("small", [P, 256])
        router = sb("router", [P, KD, NE])
        table = sb("table", [P, 4], I32)
        h_t = work[:, 0:KD * SEQ].rearrange("p (k n) -> p k n", k=KD)
        y_exp = work[:, 0:DM]
        gain_last = work[:, DM:2 * DM]
        pick = ret_s[:, 0:256].rearrange("p (t n) -> p t n", t=NT)
        pick_g = ret_s[:, 256:512].rearrange("p (t n) -> p t n", t=NT)
        pick_gt = ret_s[:, 512:768]
        mine = ret_s[:, 768:772]
        bank = [ctx.enter_context(nc.psum_tensor(f"bank{i}", [P, 512], F32)) for i in range(8)]

        def const_ap(name):
            a, w = CONST[name]
            return const[:, a:a + w]

        ident, before, ones, mean = (const_ap(n) for n in ("ident", "before", "ones", "mean"))

        raw_loaded = [sem(f"raw_loaded{i}") for i in range(RAW)]
        hi_done, lo_done, multiplied = sem("hi_done"), sem("lo_done"), sem("multiplied")
        vec_step, act_step, pool_step = sem("vec_step"), sem("act_step"), sem("pool_step")
        const_loaded, router_loaded = sem("const_loaded"), sem("router_loaded")
        x_loaded = [sem("x_loaded0"), sem("x_loaded1")]
        gain_loaded, gain_turned, gain_done = sem("gain_loaded"), sem("gain_turned"), sem("gain_done")
        last_gain_loaded, casts_done = sem("last_gain_loaded"), sem("casts_done")
        zeros_set = sem("zeros_set")
        x_updated = sem("x_updated")
        sq_summed, ms_done, rms_done = sem("sq_summed"), sem("ms_done"), sem("rms_done")
        h_normed = sem("h_normed")
        h_turned, t_hi_done, t_lo_done = sem("h_turned"), sem("t_hi_done"), sem("t_lo_done")
        stored = sem("stored")
        names = """chan_loaded chan_turned chan_done sinks_loaded pw_loaded pw_zeroed pads_zeroed
            gate_done glu_done z_copied conv_done conv_mean conv_centred conv_squared conv_var conv_var_eps
            conv_root conv_diag conv_rstd_made conv_scaled conv_act conv_mixed swa_roped ret_roped sq_turned sqt_copied score_made
            score_max probs_made sink_exp probs_scaled probs_turned probs_copied attended rq_turned
            rqt_copied ret_scored ret_decayed ret_attended ret_gate ret_var ret_std ret_normed ret_turned
            y_hi_done y_lo_done out_made far_taps""".split()
        S = [{n: sem(f"{n}_{l}") for n in names} for l in range(DEPTH)]
        gate_acted, hid_made, hid_hi, hid_lo = sem("gate_acted"), sem("hid_made"), sem("hid_hi"), sem("hid_lo")
        hid_turned = sem("hid_turned")
        logits_made, top_two, second_exp, chosen, ranked, routed, table_made = (
            sem(n) for n in "logits_made top_two second_exp chosen ranked routed table_made".split())
        picks_made, x_gathered, x_hi, x_lo, g_turned, g_copied, y_copied, scattered, x_final = (
            sem(n) for n in "picks_made x_gathered x_hi x_lo g_turned g_copied y_copied scattered x_final".split())
        y_copied_vec = sem("y_copied_vec")

        def u_count(c, turn):
            return 6 * turn + (c + 1)

        def load_unit(sp, c, turn, source, split_dims=None):
            if not (isinstance(turn, int) and c + 6 * turn < RAW):
                sp.wait_ge(lo_done, u_count(c - RAW, turn))
            dst = raw[:, c % RAW, :].rearrange("p (k n) -> p k n", k=source.shape[1])
            sp.dma_start(dst, source).then_inc(raw_loaded[c % RAW], 16)

        def split_hi(act, c, turn):
            act.wait_ge(raw_loaded[c % RAW], 16 * (turn + (c // RAW + 1)))
            if not (isinstance(turn, int) and c + 6 * turn < SPLIT):
                act.wait_ge(multiplied, u_count(c - SPLIT, turn))
            act.activation(w_hi[:, c % SPLIT, :], raw[:, c % RAW, :], ACT.Copy).then_inc(hi_done, 1)

        def split_lo(dve, c, turn):
            dve.wait_ge(hi_done, u_count(c, turn))
            dve.tensor_tensor(w_lo[:, c % SPLIT, :], raw[:, c % RAW, :], w_hi[:, c % SPLIT, :].bitcast(F32),
                              ALU.subtract).then_inc(lo_done, 1)

        def unit(c, k):
            return [w[:, c % SPLIT, :].rearrange("p (k n) -> p k n", k=k) for w in (w_hi, w_lo)]

        def score_view(g, p, i):
            return scores[g][:, p * 256:(p + 1) * 256] if i else scores[g][:, 1024 + p * P:1024 + (p + 1) * P]

        SCORE_BANKS = ([4, 5, 6], [7, 2, 3])
        PROB_BANKS = ([4, 5, 6], [7, 0, 1])
        RET_BANKS = (5, 2, 3)
        ATTENDED = (4, 6)
        OUT_BANKS = (0, 1, 4, 6)
        OUT_ORDER = (1, 2, 0, 3)

        def score_bank(g, p, i):
            a, b, c = SCORE_BANKS[g]
            return bank[(a, b)[p // 2]][:, (p % 2) * 256:(p % 2 + 1) * 256] if i else bank[c][:, p * P:(p + 1) * P]

        def tokens2(b):
            return b[:, :].rearrange("p (t n) -> p t n", t=2)

        HI_LO = ((0, 0), (0, 1), (1, 0))

        win_v = [t_in["w_in"][l].rearrange("(k p) n -> p k n", p=P) for l in range(DEPTH)]
        wout_v = [t_in["w_out"][l].rearrange("(k p) n -> p k n", p=P) for l in range(DEPTH)]
        fg_v, fu_v = (t_in[n][0].rearrange("(k p) n -> p k n", p=P) for n in ("ffn_w_gate", "ffn_w_up"))
        fd_v = t_in["ffn_w_down"][0].rearrange("(k p) n -> p k n", p=P)
        eg_v, eu_v, ed_v = (t_in[n][0].rearrange("e (k p) n -> p e k n", p=P)
                            for n in ("moe_w_gate", "moe_w_up", "moe_w_down"))
        x_v = t_in["x"][0].rearrange("(t p) n -> p t n", p=P)
        out_v = out[0].rearrange("(t p) n -> p t n", p=P)
        gains = [t_in[n][l] for l in range(DEPTH) for n in ("norm_mix_g", "norm_ffn_g")]
        PARTS = [1, 2, 2, 2, 1]
        SUMMED = [NT * sum(PARTS[:n + 1]) for n in range(5)]

        block = ctx.enter_context(nc.Block())

        @block.sync
        def _(sp):
            def load_layer_vectors(l):
                s = S[l]
                if l:
                    sp.wait_ge(S[0]["chan_turned"], 1)
                    sp.wait_ge(S[0]["y_lo_done"], 8)
                sp.dma_start(chan_rows[0:CW, :], t_in["conv_dw_w"][l]).then_inc(s["chan_loaded"], 16)
                for r, n in enumerate(("conv_dw_b", "conv_ln_g", "conv_ln_b", "ret_gn_g")):
                    sp.dma_start(chan_rows[CW + r:CW + r + 1, :], t_in[n][l:l + 1, :]).then_inc(s["chan_loaded"], 16)
                sp.dma_start(sinks[:, :], t_in["attn_sinks"][l:l + 1, :].broadcast_to([P, SH])).then_inc(s["sinks_loaded"], 16)
                sp.wait_ge(s["pw_zeroed"], 1)
                for g in range(4):
                    a = 64 * (g % 2)
                    sp.dma_start(pw[a:a + 64, g // 2, a:a + 64], t_in["conv_pw_w"][l, g]).then_inc(s["pw_loaded"], 16)

            def load_mixer(l, first, last):
                c = MIX_BASE[l]
                for q in range(first, last):
                    if q < WIN_UNITS:
                        b = WIN_ORDER[q]
                        load_unit(sp, c + q, 0, win_v[l][:, :, b * 256:(b + 1) * 256])
                    else:
                        b = OUT_ORDER[q - WIN_UNITS]
                        load_unit(sp, c + q, 0, wout_v[l][:, 2 * b:2 * b + 2, :])

            for t in range(NT):
                sp.dma_start(x[:, t, :], x_v[:, t, :]).then_inc(x_loaded[t], 16)
            for n, g in enumerate(gains):
                sp.dma_start(gain_rows[n * KD:(n + 1) * KD, :], g.rearrange("(k p) -> k p", p=P)).then_inc(gain_loaded, 16)
            sp.dma_start(const[:, :], t_in["constants"]).then_inc(const_loaded, 16)
            load_mixer(0, 0, 2)
            load_layer_vectors(0)
            load_mixer(0, 2, MIX_UNITS)
            c = FFN_BASE
            load_unit(sp, c, 0, fg_v[:, :, 0:256])
            load_unit(sp, c + 1, 0, fu_v[:, :, 0:256])
            with sp.Fori(0, (FC - 1) // 2) as it:
                for j in range(2):
                    a = c + 2 + 3 * j
                    cols = bass.ds(it * 512 + (256 + 256 * j), 256)
                    load_unit(sp, a, it, fg_v[:, :, cols])
                    load_unit(sp, a + 1, it, fd_v[:, bass.ds(it * 4 + 2 * j, 2), :])
                    load_unit(sp, a + 2, it, fu_v[:, :, cols])
            load_unit(sp, c + 3 * FC - 1, 0, fd_v[:, 2 * (FC - 1):2 * FC, :])
            load_layer_vectors(1)
            load_mixer(1, 0, MIX_UNITS)
            sp.dma_start(router[:, :, :], t_in["moe_router"][0].rearrange("(k p) e -> p k e", p=P)).then_inc(router_loaded, 16)

            def load_item(e, turn):
                c = MOE_BASE

                def pair(c, turn, view, chunk, rows):
                    for k in range(2):
                        if rows:
                            source = view[:, e, bass.ds(chunk * 4 + 2 * k, 2), :]
                        else:
                            source = view[:, e, 4 * k:4 * k + 4, bass.ds(chunk * 512, 512)]
                        load_unit(sp, c + k, turn, squeeze(source))

                def squeeze(a):
                    return a if len(a.shape) == 3 else a.rearrange("p o k n -> p (o k) n")

                pair(c, turn, eg_v, 0, False)
                pair(c + 2, turn, eu_v, 0, False)
                with sp.Fori(0, EC - 1) as i:
                    pair(c + 4, turn + i, eg_v, i + 1, False)
                    pair(c + 6, turn + i, ed_v, i, True)
                    pair(c + 8, turn + i, eu_v, i + 1, False)
                pair(c + 4, turn + (EC - 1), ed_v, EC - 1, True)

            with sp.Fori(0, NE) as e:
                load_item(e, e * EC)
            sp.wait_ge(logits_made, 1)
            sp.dma_start(gain_last, t_in["final_norm_g"].unsqueeze(0).broadcast_to([P, DM])).then_inc(last_gain_loaded, 16)
            sp.wait_ge(table_made, 1)
            n_over = sp.value_load(table[0:1, 0:1], min_val=0, max_val=3)
            with sp.If(n_over > 0):
                with sp.Fori(0, n_over) as j:
                    load_item(sp.value_load(table[0:1, bass.ds(j + 1, 1)], min_val=0, max_val=NE - 1),
                              (j + NE) * EC)
            for t in range(NT):
                sp.wait_ge(h_normed, 8 + t + 1)
                sp.dma_start(out_v[:, t, :], h[:, t, :]).then_inc(stored, 16)
            sp.wait_ge(stored, 16 * NT)

        @block.gpsimd
        def _(pool):
            n_step = [0]

            def link(ins):
                n_step[0] += 1
                ins.then_inc(pool_step, 1)
                pool.wait_ge(pool_step, n_step[0])

            def rope(heads, first, half, tab, done):
                view = z[:, :, first:first + heads * HD].rearrange("p t (h d) -> p t h d", d=HD)
                cos, sin = (const_ap(f"{tab}_{f}").rearrange("p (t d) -> p t d", t=NT) for f in ("cos", "sin"))
                a, b = (r[:, 0:heads * half].rearrange("p (h d) -> p h d", d=half) for r in (rope_a, rope_b))
                for t in range(NT):
                    x1, x2 = view[:, t, :, 0:half], view[:, t, :, half:2 * half]
                    c = cos[:, t, :].unsqueeze(1).broadcast_to([P, heads, half])
                    d = sin[:, t, :].unsqueeze(1).broadcast_to([P, heads, half])
                    link(pool.tensor_tensor(a, x1, d, ALU.mult))
                    link(pool.tensor_tensor(b, x2, d, ALU.mult))
                    link(pool.tensor_tensor(x1, x1, c, ALU.mult))
                    link(pool.tensor_tensor(x2, x2, c, ALU.mult))
                    link(pool.tensor_tensor(x1, x1, b, ALU.subtract))
                    pool.tensor_tensor(x2, x2, a, ALU.add).then_inc(done, 1)
                    pool.wait_ge(done, t + 1)

            pool.memset(zeros[:, :], 0.0).then_inc(zeros_set, 1)
            link(pool.memset(small[:, 9:10], -0.5))

            def inverse_root(a, width, counted, value, done):
                pool.wait_ge(counted, value)
                v = small[:, a:a + width]
                pool.tensor_tensor(v, v, small[:, 9:10].broadcast_to([P, width]), ALU.pow).then_inc(done, 1)

            pool.memset(glu[:, :, 0:CW - 1], 0.0).then_inc(S[0]["pads_zeroed"], 1)
            inverse_root(2, NT, ms_done, 1, rms_done)
            pool.wait_ge(const_loaded, 16)
            pool.tensor_copy(ident_bf[:, :], ident).then_inc(casts_done, 1)
            pool.tensor_copy(band_bf[:, :], const_ap("band")).then_inc(casts_done, 1)
            for l in range(DEPTH):
                s = S[l]
                pool.memset(pw[:, :, :], 0.0).then_inc(s["pw_zeroed"], 1)
                if l:
                    inverse_root(2, NT, ms_done, 3, rms_done)
                pool.wait_ge(s["z_copied"], 3)
                rope(SH + 2, 1024, 8, "swa", s["swa_roped"])
                pool.wait_ge(s["z_copied"], 5)
                rope(2 * RH, 0, 32, "ret", s["ret_roped"])
                inverse_root(136, NT * RH, s["ret_var"], 1, s["ret_std"])
                inverse_root(4, NT, s["conv_var_eps"], 1, s["conv_root"])
                inverse_root(2, NT, ms_done, (2, 4)[l], rms_done)

            pool.wait_ge(routed, 1)
            rank = small[:, 64:80].rearrange("p (t e) -> p t e", t=NT)
            gates = small[:, 80:96].rearrange("p (t e) -> p t e", t=NT)

            def make_picks(e, n, slots):
                if not (isinstance(n, int) and n == 0):
                    pool.wait_ge(g_turned, n)
                    pool.wait_ge(x_gathered, 2 * n)
                    pool.wait_ge(picks_made, 7 * n)
                pool.tensor_copy(mine[:, 0:2], rank[:, :, bass.ds(e, 1)].rearrange("p t o -> p (t o)")
                                 ).then_inc(picks_made, 1)
                pool.tensor_copy(mine[:, 2:4], gates[:, :, bass.ds(e, 1)].rearrange("p t o -> p (t o)")
                                 ).then_inc(picks_made, 1)
                pool.wait_ge(picks_made, 7 * n + 2)
                pool.tensor_tensor(rope_a[:, 0:2], mine[:, 0:2], mine[:, 2:4], ALU.mult).then_inc(picks_made, 1)
                for t in range(NT):
                    pool.tensor_scalar(pick[:, t, :], slots, mine[:, t:t + 1], None,
                                       ALU.is_equal).then_inc(picks_made, 1)
                for t in range(NT):
                    pool.tensor_scalar(pick_g[:, t, :], slots, mine[:, t:t + 1], mine[:, 2 + t:3 + t],
                                       ALU.is_equal, ALU.mult).then_inc(picks_made, 1)

            make_picks(0, 0, const_ap("slot0"))
            with pool.Fori(1, NE) as e:
                make_picks(e, e, const_ap("slot0"))
            pool.wait_ge(table_made, 1)
            n_over = pool.value_load(table[0:1, 0:1], min_val=0, max_val=3)
            with pool.If(n_over > 0):
                with pool.Fori(0, n_over) as j:
                    e = pool.value_load(table[0:1, bass.ds(j + 1, 1)], min_val=0, max_val=NE - 1)
                    make_picks(e, j + NE, const_ap("slot1"))
            inverse_root(2, NT, ms_done, 5, rms_done)

        @block.scalar
        def _(act):
            def sum_squares(t, part, first, width):
                act.activation(h[:, t, first:first + width], x[:, t, first:first + width], ACT.Square,
                               accum_out=squares[:, t, part:part + 1]).then_inc(sq_summed, 1)

            def turn_h(n):
                dst = h_t if n == 3 else t_hi
                for b in range(4):
                    act.wait_ge(h_turned, 4 * n + b + 1)
                    for k in range(2 * b, 2 * b + 2):
                        act.activation(dst[:, k, :], bank[4 + b][:, (k % 2) * 256:(k % 2 + 1) * 256], ACT.Copy,
                                       scale=gain_cols[:, n * KD + k:n * KD + k + 1]).then_inc(t_hi_done, 1)

            def round_y(l, k, src, scale=None):
                for i in range(2):
                    act.activation(t_hi[:, k + i, :], src[:, i * 256:(i + 1) * 256], ACT.Copy,
                                   scale=scale[i] if scale else 1.0).then_inc(S[l]["y_hi_done"], 1)

            def mixer(l):
                s = S[l]
                c = MIX_BASE[l]

                def copy_turned():
                    for b in range(3):
                        act.wait_ge(s["sq_turned"], b + 1)
                        if b < 2:
                            act.activation(sq_t[:, 2 * b:2 * b + 2, :], tokens2(bank[4 + b]),
                                           ACT.Copy).then_inc(s["sqt_copied"], 1)
                        else:
                            act.activation(sk_t[:, :], bank[6][:, 0:256], ACT.Copy).then_inc(s["sqt_copied"], 1)

                def exps(g):
                    act.wait_ge(s["score_max"], g + 1)
                    for i in range(2):
                        for p in range(SG):
                            n = g * 8 + i * 4 + p
                            act.activation(score_view(g, p, i), score_bank(g, p, i), ACT.Exp, scale=HD ** -0.5,
                                           bias=small[:, 32 + n:33 + n],
                                           accum_out=small[:, 48 + n:49 + n]).then_inc(s["probs_made"], 1)
                    act.activation(small[:, 96 + 8 * g:104 + 8 * g], small[:, 112 + 8 * g:120 + 8 * g],
                                   ACT.Exp).then_inc(s["sink_exp"], 1)

                def copy_probs(g):
                    for b in range(3):
                        act.wait_ge(s["probs_turned"], 3 * g + b + 1)
                        act.activation(probs_t[:, :, b * P:(b + 1) * P],
                                       bank[PROB_BANKS[g][b]][:, :].rearrange("p (h n) -> p h n", h=SG),
                                       ACT.Copy).then_inc(s["probs_copied"], 1)

                act.wait_ge(s["chan_turned"], 1)
                act.activation(chan[:, :, 0:35], bank[3][:, 0:72].rearrange("p (c n) -> p c n", c=2)[:, :, 0:35],
                               ACT.Copy).then_inc(s["chan_done"], 1)
                for q in range(WIN_UNITS):
                    split_hi(act, c + q + 2, 0)
                    if q == 6:
                        copy_turned()
                    elif q > 6:
                        exps(q - 7)
                    act.wait_ge(multiplied, c + q + 1)
                    if q == 0:
                        act.activation(gact[:, :], bank[0][:, :], ACT.Sigmoid).then_inc(s["gate_done"], 1)
                    elif q > 1:
                        b = WIN_ORDER[q]
                        dst, src = z[:, :, b * 256:(b + 1) * 256], tokens2(bank[q % 2])
                        if b in (4, 5):
                            dst = z[:, :, 1024:1536].rearrange("p t (h g d) -> p t h g d", g=2, d=HD)[:, :, :, b - 4, :]
                            src = src.rearrange("p t (h d) -> p t h d", d=HD)
                        act.activation(dst, src, ACT.Copy).then_inc(s["z_copied"], 1)
                split_hi(act, c + WIN_UNITS + 2, 0)
                copy_probs(0)
                for b in range(2):
                    act.wait_ge(s["rq_turned"], b + 1)
                    act.activation((rq_t, rk_t)[b][:, :, :], tokens2(bank[2 + b]), ACT.Copy).then_inc(s["rqt_copied"], 1)
                for g in range(2):
                    act.wait_ge(s["attended"], g + 1)
                    if g == 0:
                        copy_probs(1)
                    round_y(l, 2 + 2 * g, bank[ATTENDED[g]])
                act.activation(tokens2(gact), z[:, :, 768:1024], ACT.Silu).then_inc(s["ret_gate"], 1)
                split_hi(act, c + WIN_UNITS + 3, 0)
                act.wait_ge(s["ret_turned"], 1)
                round_y(l, 0, bank[5], [chan[:, i, CW + 3:CW + 4] for i in range(2)])
                act.wait_ge(s["conv_centred"], 1)
                act.activation(conv_sq[:, :, :], conv[:, :, :], ACT.Square).then_inc(s["conv_squared"], 1)
                split_hi(act, c + WIN_UNITS + 4, 0)
                act.wait_ge(s["conv_scaled"], 1)
                for i in range(NC_CH):
                    act.activation(conv_sq[:, i, :], conv[:, i, :], ACT.Silu, bias=chan[:, i, CW + 2:CW + 3],
                                   scale=chan[:, i, CW + 1:CW + 2]).then_inc(s["conv_act"], 1)
                act.wait_ge(s["conv_mixed"], 1)
                round_y(l, 6, bank[3])
                split_hi(act, c + WIN_UNITS + 5, 0)
                for t in range(NT):
                    for i in range(2):
                        act.wait_ge(x_updated, 8 * l + 2 * t + i + 1)
                        sum_squares(t, i, i * 512, 512)

            for t in range(NT):
                act.wait_ge(x_loaded[t], 16)
                sum_squares(t, 0, 0, DM)
            act.wait_ge(gain_turned, 1)
            act.activation(gain_cols[:, :], bank[2][:, 0:4 * KD], ACT.Copy).then_inc(gain_done, 1)
            act.wait_ge(gain_done, 1)
            split_hi(act, 0, 0)
            turn_h(0)
            split_hi(act, 1, 0)
            mixer(0)
            turn_h(1)

            def act_gate(c, turn, m):
                act.wait_ge(multiplied, u_count(c, turn))
                if not (isinstance(m, int) and m == 0):
                    act.wait_ge(hid_made, m)
                act.activation(gact[:, :], bank[0][:, :], ACT.Silu).then_inc(gate_acted, 1)

            def round_ffn(m):
                act.wait_ge(hid_made, m + 1)
                act.activation(act_hi[:, :], hid[:, :], ACT.Copy).then_inc(hid_hi, 1)

            c = FFN_BASE
            split_hi(act, c + 2, 0)
            act_gate(c, 0, 0)
            split_hi(act, c + 3, 0)
            round_ffn(0)
            with act.Fori(0, (FC - 1) // 2) as it:
                for j in range(2):
                    a, m = c + 2 + 3 * j, it * 2 + (1 + j)
                    split_hi(act, a + 2, it)
                    act_gate(a, it, m)
                    split_hi(act, a + 3, it)
                    split_hi(act, a + 4, it)
                    round_ffn(m)
            split_hi(act, c + 3 * FC + 1, 0)
            for t in range(NT):
                for i in range(2):
                    act.wait_ge(x_updated, 4 + 2 * t + i + 1)
                    sum_squares(t, i, i * 512, 512)
            turn_h(2)
            mixer(1)
            turn_h(3)
            act.wait_ge(top_two, 1)
            act.activation(small[:, 20:22], small[:, 18:20], ACT.Exp).then_inc(second_exp, 1)

            def round_x(n, b):
                act.wait_ge(x_gathered, 2 * n + (b + 1))
                for k in range(4):
                    g = 3 * KD + 4 * b + k
                    act.activation(t_hi[:, 4 * b + k, 0:P], bank[6 + b][:, k * P:(k + 1) * P], ACT.Copy,
                                   scale=gain_cols[:, g:g + 1]).then_inc(x_hi, 1)

            def round_hid(m):
                act.wait_ge(hid_turned, m + 1)
                act.activation(act_hi[:, :], bank[2][:, :], ACT.Copy).then_inc(hid_hi, 1)

            def first_gate(n, turn):
                split_hi(act, MOE_BASE + 2, turn)
                split_hi(act, MOE_BASE + 3, turn)
                act_gate(MOE_BASE + 1, turn, n * EC + FC)

            def expert(n, turn, ahead):
                c = MOE_BASE
                m = n * EC
                act.wait_ge(g_turned, n + 1)
                act.activation(pick_gt, bank[3][:, 0:256], ACT.Copy).then_inc(g_copied, 1)
                split_hi(act, c + 4, turn)
                split_hi(act, c + 5, turn)
                with act.Fori(0, EC - 1) as i:
                    a, at = c + 4, turn + i
                    split_hi(act, a + 2, at)
                    round_hid(m + i)
                    split_hi(act, a + 3, at)
                    act_gate(a + 1, at, m + i + (FC + 1))
                    for k in range(4, 8):
                        split_hi(act, a + k, at)
                last = turn + (EC - 1)
                if ahead:
                    round_x(n + 1, 0)
                round_hid(m + (EC - 1))
                if ahead:
                    round_x(n + 1, 1)
                    split_hi(act, c + 6, last)
                    split_hi(act, c + 7, last)
                act.wait_ge(multiplied, u_count(c + 5, last))
                act.activation(y_exp[:, 0:512], bank[4][:, :], ACT.Copy).then_inc(y_copied, 1)
                if ahead:
                    first_gate(n + 1, turn + EC)

            round_x(0, 0)
            round_x(0, 1)
            first_gate(0, 0)
            with act.Fori(0, NE - 1) as e:
                expert(e, e * EC, True)
            expert(NE - 1, (NE - 1) * EC, False)
            act.wait_ge(table_made, 1)
            n_over = act.value_load(table[0:1, 0:1], min_val=0, max_val=3)
            with act.If(n_over > 0):
                with act.Fori(0, n_over) as j:
                    for k in range(2):
                        split_hi(act, MOE_BASE + k, (j + NE) * EC)
                    round_x(j + NE, 0)
                    round_x(j + NE, 1)
                    first_gate(j + NE, (j + NE) * EC)
                    expert(j + NE, (j + NE) * EC, False)
            act.wait_ge(x_final, 1)
            for t in range(NT):
                sum_squares(t, 0, 0, DM)

        @block.vector
        def _(dve):
            n_step = [0]

            def link(ins):
                n_step[0] += 1
                ins.then_inc(vec_step, 1)
                dve.wait_ge(vec_step, n_step[0])

            def norm(n):
                dve.wait_ge(sq_summed, SUMMED[n])
                total = squares[:, :, 0:1]
                if PARTS[n] > 1:
                    total = small[:, 0:2].unsqueeze(2)
                    link(dve.tensor_reduce(total, squares[:, :, 0:PARTS[n]], AX, ALU.add))
                dve.tensor_scalar(small[:, 2:4].unsqueeze(2), total, 1.0 / DM, EPS, ALU.mult, ALU.add).then_inc(ms_done, 1)
                dve.wait_ge(rms_done, n + 1)
                for t in range(NT):
                    if n < 4:
                        ins = dve.tensor_scalar(h[:, t, :], x[:, t, :], small[:, 2 + t:3 + t], None, ALU.mult)
                    else:
                        dve.wait_ge(last_gain_loaded, 16)
                        ins = dve.scalar_tensor_tensor(out=h[:, t, :], in0=x[:, t, :], scalar=small[:, 2 + t:3 + t],
                                                       in1=gain_last, op0=ALU.mult, op1=ALU.mult)
                    ins.then_inc(h_normed, 1)

            def turn_h(n):
                for b in range(4):
                    dve.wait_ge(t_hi_done, KD * n + 2 * b + 2)
                    for k in range(2 * b, 2 * b + 2):
                        dve.scalar_tensor_tensor(out=t_lo[:, k, :], in0=bank[4 + b][:, (k % 2) * 256:(k % 2 + 1) * 256],
                                                 scalar=gain_cols[:, n * KD + k:n * KD + k + 1],
                                                 in1=t_hi[:, k, :].bitcast(F32), op0=ALU.mult,
                                                 op1=ALU.subtract).then_inc(t_lo_done, 1)

            def rest_y(l, k, src, n, scale=None):
                for i in range(2):
                    dve.wait_ge(S[l]["y_hi_done"], n + 2)
                    o, a, b = t_lo[:, k + i, :], src[:, i * 256:(i + 1) * 256], t_hi[:, k + i, :].bitcast(F32)
                    if scale:
                        ins = dve.scalar_tensor_tensor(out=o, in0=a, scalar=scale[i], in1=b, op0=ALU.mult, op1=ALU.subtract)
                    else:
                        ins = dve.tensor_tensor(o, a, b, ALU.subtract)
                    ins.then_inc(S[l]["y_lo_done"], 1)

            def mixer(l):
                s = S[l]
                c = MIX_BASE[l]
                taps = [(k, i) for k in range(CW) for i in range(NC_CH)]

                def tap(k, i):
                    v, w = glu[:, i, k:k + SEQ], chan[:, i, k:k + 1]
                    if k == 0:
                        ins = dve.tensor_scalar(conv[:, i, :], v, w, chan[:, i, CW:CW + 1], ALU.mult, ALU.add)
                    else:
                        dve.wait_ge(s["conv_done"], (k - 1) * NC_CH + i + 1)
                        ins = dve.scalar_tensor_tensor(out=conv[:, i, :], in0=v, scalar=w, in1=conv[:, i, :],
                                                       op0=ALU.mult, op1=ALU.add)
                    ins.then_inc(s["conv_done"], 1)

                def some_taps(n):
                    for _ in range(min(n, len(taps))):
                        tap(*taps.pop(0))

                def score_max(g):
                    a, b, last = (bank[k] for k in SCORE_BANKS[g])
                    dve.wait_ge(s["score_made"], 3 * g + 3)
                    top = small[:, 176 + 8 * g:184 + 8 * g]
                    for k, v in enumerate((a, b)):
                        link(dve.tensor_reduce(top[:, 4 + 2 * k:6 + 2 * k], tokens2(v), AX, ALU.max))
                    link(dve.tensor_reduce(top[:, 0:4], last[:, :].rearrange("p (h n) -> p h n", h=SG), AX, ALU.max))
                    own = sinks[:, g * SG:(g + 1) * SG].unsqueeze(1).broadcast_to([P, 2, SG])
                    dve.wait_ge(s["sinks_loaded"], 16)
                    top = top.rearrange("p (i h) -> p i h", i=2)
                    link(dve.scalar_tensor_tensor(out=top, in0=top, scalar=HD ** -0.5, in1=own, op0=ALU.mult, op1=ALU.max))
                    neg = small[:, 32 + 8 * g:40 + 8 * g].rearrange("p (i h) -> p i h", i=2)
                    link(dve.tensor_scalar(neg, top, -1.0, None, ALU.mult))
                    dve.tensor_tensor(small[:, 112 + 8 * g:120 + 8 * g].rearrange("p (i h) -> p i h", i=2), own,
                                      neg, ALU.add).then_inc(s["score_max"], 1)

                def scale_probs(g):
                    dve.wait_ge(s["probs_made"], 8 * g + 8)
                    dve.wait_ge(s["sink_exp"], g + 1)
                    r = small[:, 160 + 8 * g:168 + 8 * g]
                    link(dve.tensor_tensor(r, small[:, 48 + 8 * g:56 + 8 * g], small[:, 96 + 8 * g:104 + 8 * g], ALU.add))
                    link(dve.reciprocal(r, r))
                    for i in range(2):
                        v = (scores[g][:, 0:1024] if i else scores[g][:, 1024:1536]).rearrange("p (h n) -> p h n", h=SG)
                        dve.tensor_tensor(v, v, r[:, 4 * i:4 * i + 4].unsqueeze(2).broadcast_to([P, SG, v.shape[2]]),
                                          ALU.mult).then_inc(s["probs_scaled"], 1)

                for q in range(WIN_UNITS):
                    split_lo(dve, c + q + 2, 0)
                    if q == 1:
                        dve.wait_ge(s["gate_done"], 1)
                        dve.wait_ge(multiplied, c + 2)
                        dve.wait_ge(S[0]["pads_zeroed"], 1)
                        dve.tensor_tensor(glu[:, :, CW - 1:], tokens2(bank[1]), tokens2(gact), ALU.mult).then_inc(s["glu_done"], 1)
                        dve.wait_ge(s["glu_done"], 1)
                        dve.wait_ge(s["chan_done"], 1)
                    if q == 7:
                        score_max(0)
                        score_max(1)
                    some_taps((0, 4, 7, 7, 7, 7, 7, 2, 4)[q])
                    if q >= 7:
                        scale_probs(q - 7)
                split_lo(dve, c + WIN_UNITS + 2, 0)
                some_taps(6)
                rest_y(l, 2, bank[ATTENDED[0]], 0)
                for i, b in enumerate(RET_BANKS):
                    dve.wait_ge(s["ret_scored"], (1, 2, 4)[i])
                    dve.tensor_tensor(ret_s[:, i * 512:(i + 1) * 512], bank[b][:, :],
                                      const_ap("decay")[:, i * 512:(i + 1) * 512], ALU.mult).then_inc(s["ret_decayed"], 1)
                rest_y(l, 4, bank[ATTENDED[1]], 2)
                dve.wait_ge(s["ret_attended"], 1)
                o = bank[2][:, :].rearrange("p (g d) -> p g d", d=HD)
                mu, var, rstd = (small[:, a:a + 8] for a in (128, 144, 136))

                def wide(v):
                    return v.unsqueeze(2).broadcast_to([P, NT * RH, HD])

                link(dve.tensor_reduce(mu, o, AX, ALU.add))
                link(dve.tensor_scalar(mu, mu, 1.0 / HD, None, ALU.mult))
                link(dve.tensor_tensor(ret_o[:, :, :], o, wide(mu), ALU.subtract))
                square = rope_a[:, :].rearrange("p (g d) -> p g d", d=HD)
                link(dve.tensor_tensor(square, ret_o[:, :, :], ret_o[:, :, :], ALU.mult))
                link(dve.tensor_reduce(var, square, AX, ALU.add))
                dve.tensor_scalar(rstd, var, 1.0 / HD, EPS, ALU.mult, ALU.add).then_inc(s["ret_var"], 1)
                some_taps(62)
                dve.wait_ge(s["ret_std"], 1)
                link(dve.tensor_tensor(ret_o[:, :, :], ret_o[:, :, :], wide(rstd), ALU.mult))
                dve.wait_ge(s["ret_gate"], 1)
                dve.tensor_tensor(ret_o[:, :, :], ret_o[:, :, :], gact[:, :].rearrange("p (g d) -> p g d", d=HD),
                                  ALU.mult).then_inc(s["ret_normed"], 1)
                split_lo(dve, c + WIN_UNITS + 3, 0)
                rest_y(l, 0, bank[5], 4, [chan[:, i, CW + 3:CW + 4] for i in range(2)])
                dve.wait_ge(s["conv_mean"], 1)
                dve.wait_ge(s["conv_done"], CW * NC_CH)
                dve.tensor_tensor(conv[:, :, :], conv[:, :, :], bank[7][:, 0:256].unsqueeze(1).broadcast_to([P, 2, 256]),
                                  ALU.subtract).then_inc(s["conv_centred"], 1)
                dve.wait_ge(s["conv_var"], 1)
                dve.tensor_scalar(small[:, 4:6], bank[7][:, 256:258], EPS, None, ALU.add).then_inc(s["conv_var_eps"], 1)
                dve.wait_ge(s["conv_root"], 1)
                for t in range(NT):
                    dve.tensor_scalar(conv_diag[:, t * P:(t + 1) * P], ident, small[:, 4 + t:5 + t], None,
                                      ALU.mult).then_inc(s["conv_diag"], 1)
                split_lo(dve, c + WIN_UNITS + 4, 0)
                dve.wait_ge(s["conv_rstd_made"], 1)
                dve.tensor_tensor(conv[:, :, :], conv[:, :, :], bank[7][:, 256:512].unsqueeze(1).broadcast_to([P, 2, 256]),
                                  ALU.mult).then_inc(s["conv_scaled"], 1)
                rest_y(l, 6, bank[3], 6)
                split_lo(dve, c + WIN_UNITS + 5, 0)
                for n, b in enumerate(OUT_BANKS):
                    if n < 3:
                        dve.wait_ge(s["out_made"], n + 1)
                    else:
                        dve.wait_ge(multiplied, c + MIX_UNITS)
                    v = x[:, n // 2, (n % 2) * 512:(n % 2 + 1) * 512]
                    dve.tensor_tensor(v, v, bank[b][:, :], ALU.add).then_inc(x_updated, 1)

            norm(0)
            split_lo(dve, 0, 0)
            dve.wait_ge(gain_done, 1)
            turn_h(0)
            split_lo(dve, 1, 0)
            mixer(0)
            norm(1)
            turn_h(1)

            def make_hid(c, turn, m, up):
                dve.wait_ge(multiplied, u_count(c, turn))
                dve.wait_ge(gate_acted, m + 1)
                if not (isinstance(m, int) and m == 0):
                    dve.wait_ge(hid_hi, m)
                    dve.wait_ge(hid_lo, m)
                dve.tensor_tensor(hid[:, :], gact[:, :], up[:, :], ALU.mult).then_inc(hid_made, 1)

            def rest_hid(m, src):
                dve.wait_ge(hid_hi, m + 1)
                dve.tensor_tensor(act_lo[:, :], src[:, :], act_hi[:, :].bitcast(F32), ALU.subtract).then_inc(hid_lo, 1)

            c = FFN_BASE
            split_lo(dve, c + 2, 0)
            split_lo(dve, c + 3, 0)
            make_hid(c + 1, 0, 0, bank[2])
            rest_hid(0, hid)
            with dve.Fori(0, (FC - 1) // 2) as it:
                for j in range(2):
                    a, m = c + 2 + 3 * j, it * 2 + (1 + j)
                    split_lo(dve, a + 2, it)
                    split_lo(dve, a + 3, it)
                    split_lo(dve, a + 4, it)
                    make_hid(a + 2, it, m, bank[2])
                    rest_hid(m, hid)
            split_lo(dve, c + 3 * FC + 1, 0)
            dve.wait_ge(multiplied, c + 3 * FC)
            dve.wait_ge(x_updated, 4)
            for t in range(NT):
                for i in range(2):
                    v = x[:, t, i * 512:(i + 1) * 512]
                    dve.tensor_tensor(v, v, bank[4 + 2 * t + i][:, :], ALU.add).then_inc(x_updated, 1)
            norm(2)
            turn_h(2)
            mixer(1)
            norm(3)

            def cols(a, w=2 * NE):
                return small[:, a:a + w]

            def by_token(v):
                return v.rearrange("p (t e) -> p t e", t=NT)

            def wide8(v):
                return v.unsqueeze(2).broadcast_to([P, NT, NE])

            idx = const_ap("rev8").unsqueeze(1).broadcast_to([P, NT, NE])
            logits, first, second, cand = (by_token(cols(a)) for a in (32, 96, 112, 160))
            top1, top2, pos, gap, e2, den, w1, w2 = (small[:, a:a + 2] for a in (10, 12, 14, 18, 20, 22, 24, 26))
            dve.wait_ge(logits_made, 1)
            for t in range(NT):
                link(dve.tensor_copy(logits[:, t, :], bank[3 - t][:, 0:NE]))

            def one_hot(top, hot):
                link(dve.tensor_reduce(top, logits, AX, ALU.max))
                link(dve.tensor_tensor(cand, logits, wide8(top), ALU.is_equal))
                link(dve.tensor_tensor(cand, cand, idx, ALU.mult))
                link(dve.tensor_reduce(pos, cand, AX, ALU.max))
                link(dve.tensor_tensor(hot, cand, wide8(pos), ALU.is_equal))

            one_hot(top1, first)
            link(dve.scalar_tensor_tensor(out=logits, in0=first, scalar=-3e38, in1=logits, op0=ALU.mult, op1=ALU.add))
            one_hot(top2, second)
            dve.tensor_tensor(gap, top2, top1, ALU.subtract).then_inc(top_two, 1)
            sel = by_token(cols(192))
            dve.tensor_tensor(sel, first, second, ALU.add).then_inc(chosen, 1)
            dve.wait_ge(second_exp, 1)
            link(dve.tensor_scalar(den, e2, 1.0, None, ALU.add))
            link(dve.reciprocal(w1, den))
            link(dve.tensor_tensor(w2, e2, w1, ALU.mult))
            gates, rank = by_token(cols(80)), by_token(cols(64))
            link(dve.tensor_tensor(gates, first, wide8(w1), ALU.mult))
            link(dve.tensor_tensor(second, second, wide8(w2), ALU.mult))
            link(dve.tensor_tensor(gates, gates, second, ALU.add))
            dve.wait_ge(ranked, 1)
            counts = small[:, 208:232]
            link(dve.tensor_copy(counts, bank[3][:, 16:40]))
            link(dve.scalar_tensor_tensor(out=rank, in0=by_token(counts[:, 0:16]), scalar=1.0, in1=sel, op0=ALU.add,
                                          op1=ALU.mult))
            dve.tensor_scalar(rank, rank, -1.0, None, ALU.add).then_inc(routed, 1)
            over, upto, hot = small[:, 232:240], small[:, 240:248], small[:, 248:256]
            listed = small[:, 96:100]
            link(dve.tensor_scalar(over, counts[:, 16:24], float(P), None, ALU.is_gt))
            link(dve.memset(hot, 0.0))
            link(dve.tensor_tensor_scan(upto, over, hot, 0.0, ALU.add, ALU.add))
            link(dve.tensor_copy(listed[:, 0:1], upto[:, 7:8]))
            for j in range(3):
                link(dve.scalar_tensor_tensor(out=hot, in0=upto, scalar=float(j + 1), in1=over, op0=ALU.is_equal,
                                              op1=ALU.mult))
                link(dve.tensor_tensor(hot, hot, const_ap("idx8"), ALU.mult))
                link(dve.tensor_reduce(listed[:, j + 1:j + 2], hot, AX, ALU.add))
            dve.tensor_copy(table[:, :], listed).then_inc(table_made, 1)

            def rest_x(n, b):
                dve.wait_ge(x_hi, 8 * n + (4 * b + 4))
                for k in range(4):
                    g = 3 * KD + 4 * b + k
                    dve.scalar_tensor_tensor(out=t_lo[:, 4 * b + k, 0:P], in0=bank[6 + b][:, k * P:(k + 1) * P],
                                             scalar=gain_cols[:, g:g + 1], in1=t_hi[:, 4 * b + k, 0:P].bitcast(F32),
                                             op0=ALU.mult, op1=ALU.subtract).then_inc(x_lo, 1)

            def expert(n, turn, ahead):
                c = MOE_BASE
                m = n * EC + FC
                split_lo(dve, c + 4, turn)
                split_lo(dve, c + 5, turn)
                make_hid(c + 3, turn, m, bank[1])
                with dve.Fori(0, EC - 1) as i:
                    a, at = c + 4, turn + i
                    split_lo(dve, a + 2, at)
                    rest_hid(m + i, bank[2])
                    for k in range(3, 8):
                        split_lo(dve, a + k, at)
                    make_hid(a + 5, at, m + i + 1, bank[1])
                last = turn + (EC - 1)
                if ahead:
                    rest_x(n + 1, 0)
                rest_hid(m + (EC - 1), bank[2])
                if ahead:
                    rest_x(n + 1, 1)
                    split_lo(dve, c + 6, last)
                    split_lo(dve, c + 7, last)
                dve.wait_ge(multiplied, u_count(c + 5, last))
                dve.tensor_copy(y_exp[:, 512:1024], bank[5][:, :]).then_inc(y_copied_vec, 1)
                if ahead:
                    split_lo(dve, c + 8, last)
                    split_lo(dve, c + 9, last)
                dve.wait_ge(x_updated, 4 * n + 12)
                for q in range(4):
                    dve.wait_ge(scattered, 4 * n + (q + 1))
                    v = x[:, q // 2, (q % 2) * 512:(q % 2 + 1) * 512]
                    dve.tensor_tensor(v, v, bank[6 + q % 2][:, :], ALU.add).then_inc(x_updated, 1)

            rest_x(0, 0)
            rest_x(0, 1)
            split_lo(dve, MOE_BASE + 2, 0)
            split_lo(dve, MOE_BASE + 3, 0)
            with dve.Fori(0, NE - 1) as e:
                expert(e, e * EC, True)
            expert(NE - 1, (NE - 1) * EC, False)
            dve.wait_ge(x_updated, 12 + 4 * NE)
            dve.wait_ge(table_made, 1)
            n_over = dve.value_load(table[0:1, 0:1], min_val=0, max_val=3)
            with dve.If(n_over > 0):
                with dve.Fori(0, n_over) as j:
                    for k in range(2):
                        split_lo(dve, MOE_BASE + k, (j + NE) * EC)
                    rest_x(j + NE, 0)
                    rest_x(j + NE, 1)
                    split_lo(dve, MOE_BASE + 2, (j + NE) * EC)
                    split_lo(dve, MOE_BASE + 3, (j + NE) * EC)
                    expert(j + NE, (j + NE) * EC, False)
                    dve.wait_ge(x_updated, 4 * j + (16 + 4 * NE))
            dve.memset(small[:, 8:9], 0.0).then_inc(x_final, 1)
            norm(4)

        @block.tensor
        def _(pe):
            def turn_rows(n):
                pe.wait_ge(h_normed, 2 * n + 2)
                for b in range(4):
                    for k in range(2):
                        for t in range(NT):
                            f = (2 * b + k) * P
                            ins = pe.transpose(bank[4 + b][:, k * 256 + t * P:k * 256 + (t + 1) * P],
                                               h[:, t, f:f + P], ident)
                    ins.then_inc(h_turned, 1)

            def turn_channels(l):
                s = S[l]
                pe.wait_ge(s["chan_loaded"], 16 * 5)
                for i in range(NC_CH):
                    ins = pe.transpose(bank[3][:, i * 36:i * 36 + 35], chan_rows[0:35, i * P:(i + 1) * P], ident[0:35, 0:35])
                ins.then_inc(s["chan_turned"], 1)

            def rows_by_weights(dst, c, turn):
                w = unit(c, KD)
                for t in range(NT):
                    for k in range(KD):
                        for a, b in HI_LO:
                            ins = pe.matmul(dst[:, t * 256:(t + 1) * 256], (t_hi, t_lo)[a][:, k, t * P:(t + 1) * P],
                                            w[b][:, k, :], start=(k == 0 and (a, b) == (0, 0)),
                                            stop=(k == KD - 1 and (a, b) == (1, 0)))
                ins.then_inc(multiplied, 1)

            def weights_by_rows(dst, c, turn, arrived=None):
                w = unit(c, KD)
                for i in range(2):
                    for k in range(KD):
                        if i == 0 and arrived is not None:
                            pe.wait_ge(t_lo_done, arrived + k + 1)
                        for a, b in HI_LO:
                            ins = pe.matmul(dst[:, i * 256:(i + 1) * 256], w[b][:, k, i * P:(i + 1) * P],
                                            (t_hi, t_lo)[a][:, k, :], start=(k == 0 and (a, b) == (0, 0)),
                                            stop=(k == KD - 1 and (a, b) == (1, 0)))
                ins.then_inc(multiplied, 1)

            def mixer(l):
                s = S[l]
                c = MIX_BASE[l]
                def turn_attention():
                    pe.wait_ge(s["swa_roped"], 2)
                    for b in range(2):
                        for k in range(2):
                            p = 2 * b + k
                            for t in range(NT):
                                ins = pe.transpose(bank[4 + b][:, k * 256 + t * P:k * 256 + (t + 1) * P],
                                                   z[:, t, 1024 + p * P:1024 + (p + 1) * P], ident)
                        ins.then_inc(s["sq_turned"], 1)
                    for t in range(NT):
                        ins = pe.transpose(bank[6][:, t * P:(t + 1) * P], z[:, t, 1536:1664], ident)
                    ins.then_inc(s["sq_turned"], 1)

                def score(g):
                    a = 64 * g
                    if g == 0:
                        pe.wait_ge(s["sqt_copied"], 3)
                        pe.wait_ge(casts_done, 2)
                    for i in (1, 0):
                        for p in range(SG):
                            dst = score_bank(g, p, i)
                            first = 0 if i else P
                            pe.matmul(dst, sq_t[a:a + 64, p, i * P:(i + 1) * P], sk_t[a:a + 64, 0:2 * P - first],
                                      start=True, stop=False)
                            ins = pe.matmul(dst, ident_bf[:, :], band_bf[:, first:], start=False, stop=True)
                            if p == 3 or (i == 1 and p % 2):
                                ins.then_inc(s["score_made"], 1)

                def turn_probs(g):
                    pe.wait_ge(s["probs_scaled"], 2 * g + 2)
                    for b in range(3):
                        for p in range(SG):
                            v = score_view(g, p, 0) if b == 0 else score_view(g, p, 1)[:, (b - 1) * P:b * P]
                            ins = pe.transpose(bank[PROB_BANKS[g][b]][:, p * P:(p + 1) * P], v, ident)
                        ins.then_inc(s["probs_turned"], 1)

                def attend(g):
                    pe.wait_ge(s["probs_copied"], 3 * g + 3)
                    v = z[:, :, 1664 + g * HD:1664 + (g + 1) * HD]
                    for p in range(SG):
                        o = bank[ATTENDED[g]][64 * (p % 2):64 * (p % 2) + 64, (p // 2) * 256:(p // 2 + 1) * 256]
                        pe.matmul(o, v[:, 0, :], probs_t[:, p, 0:256], start=True, stop=False)
                        ins = pe.matmul(o[:, P:], v[:, 1, :], probs_t[:, p, 256:384], start=False, stop=True)
                    ins.then_inc(s["attended"], 1)

                def turn_retention():
                    pe.wait_ge(s["ret_roped"], 2)
                    pe.wait_ge(s["probs_made"], 16)
                    for b in range(2):
                        for k in range(2):
                            for t in range(NT):
                                f = b * 256 + k * P
                                ins = pe.transpose(bank[2 + b][:, k * 256 + t * P:k * 256 + (t + 1) * P], z[:, t, f:f + P],
                                                   ident)
                        ins.then_inc(s["rq_turned"], 1)

                def project(q):
                    pe.wait_ge(lo_done, c + WIN_UNITS + q + 1)
                    pe.wait_ge(s["y_lo_done"], max(4, 2 * q + 2))
                    w = unit(c + WIN_UNITS + q, 2)
                    for n, b in enumerate(OUT_BANKS):
                        t, i = n // 2, n % 2
                        for f in range(2):
                            k = 2 * OUT_ORDER[q] + f
                            for u, v in HI_LO:
                                ins = pe.matmul(bank[b][:, :], (t_hi, t_lo)[u][:, k, t * P:(t + 1) * P],
                                                w[v][:, f, i * 512:(i + 1) * 512], start=(q == 0 and f == 0 and (u, v) == (0, 0)),
                                                stop=(q == 3 and f == 1 and (u, v) == (1, 0)), skip_group_check=True)
                        if n == 3:
                            ins.then_inc(multiplied, 1)
                        elif q == 3:
                            ins.then_inc(s["out_made"], 1)

                for q in range(WIN_UNITS):
                    pe.wait_ge(lo_done, c + q + 1)
                    if q == 2:
                        pe.wait_ge(s["gate_done"], 1)
                    elif q == 3:
                        pe.wait_ge(s["glu_done"], 1)
                    elif q > 3:
                        pe.wait_ge(s["z_copied"], q - 3)
                    if q == 0:
                        weights_by_rows(bank[0], c, 0, 2 * KD * l)
                    elif q == 1:
                        weights_by_rows(bank[1], c + 1, 0)
                    else:
                        rows_by_weights(bank[q % 2], c + q, 0)
                    if q == 5:
                        turn_attention()
                    elif q == 6:
                        score(0)
                        score(1)
                turn_probs(0)
                turn_retention()
                pe.wait_ge(s["z_copied"], 7)
                turn_probs(1)
                attend(0)
                pe.wait_ge(s["rqt_copied"], 2)
                for b in range(4):
                    if b == 3:
                        pe.wait_ge(s["ret_scored"], 3)
                    for n in (0, 1):
                        p = RET_HEADS[2 * (b % 2) + n]
                        q, k = (v[64 * (p % 2):64 * (p % 2) + 64, p // 2, :] for v in (rq_t, rk_t))
                        if b < 2:
                            o, k = bank[RET_BANKS[b]][:, n * 256:(n + 1) * 256], k[:, 0:P]
                        else:
                            n += 2 * (b % 2)
                            o, k, q = bank[RET_BANKS[2]][:, n * P:(n + 1) * P], k[:, P:], q[:, P:]
                        ins = pe.matmul(o, k, q, start=True, stop=True)
                    ins.then_inc(s["ret_scored"], 1)
                attend(1)
                pe.wait_ge(s["ret_decayed"], 3)
                for t in range(NT):
                    for i in range(RH):
                        o = bank[2][:, (t * RH + i) * HD:(t * RH + i + 1) * HD]
                        v = z[:, :, 512 + i * HD:512 + (i + 1) * HD]
                        n = RET_HEADS.index(i)
                        ins = pe.matmul(o, ret_s[:, n * 256 + t * P:n * 256 + (t + 1) * P], v[:, 0, :], start=True,
                                        stop=(t == 0))
                        if t:
                            ins = pe.matmul(o, ret_s[:, 1024 + n * P:1024 + (n + 1) * P], v[:, 1, :], start=False, stop=True)
                ins.then_inc(s["ret_attended"], 1)
                project(0)
                pe.wait_ge(s["conv_done"], CW * NC_CH)
                for i in range(NC_CH):
                    ins = pe.matmul(bank[7][:, 0:256], mean, conv[:, i, :], start=(i == 0), stop=(i == 1))
                ins.then_inc(s["conv_mean"], 1)
                pe.wait_ge(s["ret_normed"], 1)
                flat = ret_o[:, :, :].rearrange("p g d -> p (g d)")
                for k in range(2):
                    for t in range(NT):
                        ins = pe.transpose(bank[5][:, k * 256 + t * P:k * 256 + (t + 1) * P],
                                           flat[:, t * 256 + k * P:t * 256 + (k + 1) * P], ident)
                ins.then_inc(s["ret_turned"], 1)
                project(1)
                pe.wait_ge(s["conv_squared"], 1)
                for t in range(NT):
                    for i in range(NC_CH):
                        ins = pe.matmul(bank[7][:, 256 + t:257 + t], conv_sq[:, i, t * P:(t + 1) * P], mean[:, 0:1],
                                        start=(i == 0), stop=(i == 1))
                ins.then_inc(s["conv_var"], 1)
                project(2)
                pe.wait_ge(s["conv_diag"], NT)
                pe.matmul(bank[7][:, 256:512], ones, conv_diag[:, :], start=True, stop=True).then_inc(s["conv_rstd_made"], 1)
                pe.wait_ge(s["conv_act"], 2)
                pe.wait_ge(s["pw_loaded"], 16 * 4)
                for i in range(NC_CH):
                    ins = pe.matmul(bank[3][:, i * 256:(i + 1) * 256], pw[:, i, :], conv_sq[:, i, :], start=True, stop=True)
                ins.then_inc(s["conv_mixed"], 1)
                project(3)

            pe.wait_ge(const_loaded, 16)
            pe.wait_ge(gain_loaded, 16 * 4)
            pe.transpose(bank[2][:, 0:4 * KD], gain_rows[:, :], ident[0:4 * KD, 0:4 * KD]).then_inc(gain_turned, 1)
            turn_rows(0)
            turn_channels(0)
            mixer(0)
            turn_rows(1)

            c = FFN_BASE
            pe.wait_ge(zeros_set, 1)

            def clear(b):
                pe.matmul(bank[b][:, :], zeros[:, 0:P], zeros[:, :], start=True, stop=False, skip_group_check=True)

            def ffn_down(c, turn, m, last=False):
                pe.wait_ge(lo_done, u_count(c, turn))
                pe.wait_ge(hid_lo, m + 1)
                w = unit(c, 2)
                for f in range(2):
                    for t in range(NT):
                        for i in range(2):
                            for a, b in HI_LO:
                                ins = pe.matmul(bank[4 + 2 * t + i][:, :], (act_hi, act_lo)[a][:, f * 256 + t * P:f * 256 + (t + 1) * P],
                                                w[b][:, f, i * 512:(i + 1) * 512], start=False,
                                                stop=(last and f == 1 and (a, b) == (1, 0)), skip_group_check=True)
                ins.then_inc(multiplied, 1)

            pe.wait_ge(lo_done, c + 1)
            weights_by_rows(bank[0], c, 0, KD)
            for b in range(4, 8):
                clear(b)
            pe.wait_ge(lo_done, c + 2)
            weights_by_rows(bank[2], c + 1, 0)
            with pe.Fori(0, (FC - 1) // 2) as it:
                for j in range(2):
                    a, m = c + 2 + 3 * j, it * 2 + (1 + j)
                    pe.wait_ge(lo_done, u_count(a, it))
                    pe.wait_ge(gate_acted, m)
                    weights_by_rows(bank[0], a, it)
                    ffn_down(a + 1, it, m - 1)
                    pe.wait_ge(lo_done, u_count(a + 2, it))
                    pe.wait_ge(hid_made, m)
                    weights_by_rows(bank[2], a + 2, it)
            ffn_down(c + 3 * FC - 1, 0, FC - 1, True)
            turn_rows(2)
            turn_channels(1)
            mixer(1)
            turn_rows(3)

            pe.wait_ge(router_loaded, 16)
            for k in range(KD):
                pe.wait_ge(t_hi_done, 3 * KD + k + 1)
                for t in range(NT):
                    ins = pe.matmul(bank[3 - t][:, 0:NE], h_t[:, k, t * P:(t + 1) * P], router[:, k, :],
                                    start=(k == 0), stop=(k == KD - 1))
            ins.then_inc(logits_made, 1)
            pe.wait_ge(chosen, 1)
            sel = small[:, 192:208]
            pe.matmul(bank[3][:, 16:24], before, sel[:, 0:8], start=True, stop=True)
            pe.matmul(bank[3][:, 24:32], before, sel[:, 8:16], start=True, stop=False)
            pe.matmul(bank[3][:, 24:32], ones, sel[:, 0:8], start=False, stop=True)
            pe.matmul(bank[3][:, 32:40], ones, sel[:, 0:8], start=True, stop=False)
            pe.matmul(bank[3][:, 32:40], ones, sel[:, 8:16], start=False, stop=True).then_inc(ranked, 1)

            def gather(n, b, before_it):
                pe.wait_ge(picks_made, 7 * n + 5)
                if before_it is not None:
                    pe.wait_ge(x_updated, before_it)
                for k in range(4):
                    f = (4 * b + k) * P
                    for t in range(NT):
                        ins = pe.matmul(bank[6 + b][:, k * P:(k + 1) * P], h[:, t, f:f + P], pick[:, t, :],
                                        start=(t == 0), stop=(t == 1))
                ins.then_inc(x_gathered, 1)

            def rows_by_expert(dst, c, turn, half):
                pe.wait_ge(lo_done, u_count(c, turn))
                w = unit(c, 4)
                for k in range(4):
                    for a, b in HI_LO:
                        ins = pe.matmul(dst[:, :], (t_hi, t_lo)[a][:, 4 * half + k, 0:P], w[b][:, k, :],
                                        start=(half == 0 and k == 0 and (a, b) == (0, 0)),
                                        stop=(half == 1 and k == 3 and (a, b) == (1, 0)), skip_group_check=True)
                ins.then_inc(multiplied, 1)

            def turn_hid(m):
                pe.wait_ge(hid_made, m + 1)
                pe.wait_ge(hid_lo, m)
                for k in range(4):
                    ins = pe.transpose(bank[2][:, k * P:(k + 1) * P], hid[:, k * P:(k + 1) * P], ident)
                ins.then_inc(hid_turned, 1)

            def expert_down(c, turn, m, half, last):
                pe.wait_ge(lo_done, u_count(c, turn))
                pe.wait_ge(hid_lo, m + 1)
                w = unit(c, 2)
                for f in range(2):
                    for i in range(2):
                        for a, b in HI_LO:
                            ins = pe.matmul(bank[4 + i][:, :], (act_hi, act_lo)[a][:, (2 * half + f) * P:(2 * half + f + 1) * P],
                                            w[b][:, f, i * 512:(i + 1) * 512], start=False,
                                            stop=(last and half == 1 and f == 1 and (a, b) == (1, 0)), skip_group_check=True)
                ins.then_inc(multiplied, 1)

            def first_gate(n, turn):
                pe.wait_ge(x_lo, 8 * n + 8)
                pe.wait_ge(gate_acted, n * EC + FC)
                for i in range(2):
                    rows_by_expert(bank[0], MOE_BASE + i, turn, i)

            def expert(n, turn, ahead):
                c = MOE_BASE
                m = n * EC + FC
                clear(4)
                clear(5)
                pe.wait_ge(picks_made, 7 * n + 7)
                for t in range(NT):
                    ins = pe.transpose(bank[3][:, t * P:(t + 1) * P], pick_g[:, t, :], ident)
                ins.then_inc(g_turned, 1)
                pe.wait_ge(hid_made, m)
                for i in range(2):
                    rows_by_expert(bank[1], c + 2 + i, turn, i)
                with pe.Fori(0, EC - 1) as i:
                    a, at = c + 4, turn + i
                    pe.wait_ge(gate_acted, m + i + 1)
                    rows_by_expert(bank[0], a, at, 0)
                    turn_hid(m + i)
                    rows_by_expert(bank[0], a + 1, at, 1)
                    for k in range(2):
                        expert_down(a + 2 + k, at, m + i, k, False)
                    for k in range(2):
                        rows_by_expert(bank[1], a + 4 + k, at, k)
                if ahead:
                    gather(n + 1, 0, 4 * n + 12)
                turn_hid(m + (EC - 1))
                if ahead:
                    gather(n + 1, 1, None)
                for k in range(2):
                    expert_down(c + 4 + k, turn + (EC - 1), m + (EC - 1), k, True)
                if ahead:
                    first_gate(n + 1, turn + EC)
                pe.wait_ge(g_copied, n + 1)
                pe.wait_ge(y_copied, n + 1)
                pe.wait_ge(y_copied_vec, n + 1)
                for q in range(4):
                    t, i = q // 2, q % 2
                    if q >= 2:
                        pe.wait_ge(x_updated, 4 * n + (12 + q - 1))
                    pe.matmul(bank[6 + i][:, :], pick_gt[:, t * P:(t + 1) * P], y_exp[:, i * 512:(i + 1) * 512],
                              start=True, stop=True).then_inc(scattered, 1)

            gather(0, 0, None)
            gather(0, 1, None)
            first_gate(0, 0)
            with pe.Fori(0, NE - 1) as e:
                expert(e, e * EC, True)
            expert(NE - 1, (NE - 1) * EC, False)
            pe.wait_ge(table_made, 1)
            n_over = pe.value_load(table[0:1, 0:1], min_val=0, max_val=3)
            with pe.If(n_over > 0):
                with pe.Fori(0, n_over) as j:
                    gather(j + NE, 0, 4 * j + (12 + 4 * NE))
                    gather(j + NE, 1, None)
                    first_gate(j + NE, (j + NE) * EC)
                    expert(j + NE, (j + NE) * EC, False)


INPUTS = ["x", "norm_mix_g", "w_in", "ret_gn_g", "attn_sinks", "conv_dw_w", "conv_dw_b", "conv_ln_g", "conv_ln_b",
          "conv_pw_w", "w_out", "norm_ffn_g", "ffn_w_gate", "ffn_w_up", "ffn_w_down", "moe_router", "moe_w_gate",
          "moe_w_up", "moe_w_down", "final_norm_g"]


def kernel(**inputs):
    import concourse.bacc as bacc
    from concourse.bass_utils import run_bass_kernel_spmd

    nc = bacc.Bacc("TRN2", target_bir_lowering=False, num_devices=1)
    arrays = {f"in_{n}": np.ascontiguousarray(inputs[n]) for n in INPUTS}
    arrays["in_constants"] = shape_constants()
    t_in = {n[3:]: nc.dram_tensor(n, a.shape, mybir.dt.from_np(a.dtype), kind="ExternalInput").ap()
            for n, a in arrays.items()}
    out = nc.dram_tensor("out", (1, SEQ, DM), F32, kind="ExternalOutput").ap()
    trunk(nc, t_in, out)
    return run_bass_kernel_spmd(nc, [arrays], core_ids=[0]).results[0]["out"]
```

```python
from contextlib import ExitStack

import numpy as np

import concourse.bass as bass
from concourse import mybir

F32 = mybir.dt.float32
F32R = mybir.dt.float32r
BF16 = mybir.dt.bfloat16
I32 = mybir.dt.int32
ALU = mybir.AluOpType
ACT = mybir.ActivationFunctionType
AX = mybir.AxisListType.X

P = 128
SEQ, DM = 256, 1024
DEPTH = 2
NT = SEQ // P
KD = DM // P
HD = 64
RH, RW = 4, 256
SH, SG = 8, 4
CC, CW = 256, 31
NC_CH = CC // P
FF = 2816
FE = 3584
NE = 8
EPS = 1e-6
NEG = -1e30
UNIT = 2048
RAW, SPLIT = 6, 3
TURN = 6
assert TURN % RAW == 0 and TURN % SPLIT == 0
WIN_UNITS, WOUT_UNITS = 9, 4
MIX_UNITS = WIN_UNITS + WOUT_UNITS
FC = FF // 256
EC = FE // 512
FFN_BASE = MIX_UNITS
MIX_BASE = [0, MIX_UNITS + 3 * FC]
MOE_BASE = MIX_BASE[1] + MIX_UNITS
ITEM = 6 * EC
assert ITEM % TURN == 0
WIN_ORDER = [8, 7, 4, 5, 6, 0, 1, 2, 3]

NEAR_TAPS = CW - 3
RET_HEADS = (0, 2, 1, 3)

CONST = {}
_at = 0
for _n, _w in (("ident", P), ("mean", P), ("ones", P), ("before", P), ("slot0", P), ("slot1", P),
               ("ret_cos", NT * 32), ("ret_sin", NT * 32), ("swa_cos", NT * 8), ("swa_sin", NT * 8),
               ("decay", RH * 384), ("band", 2 * P), ("rev8", NE), ("idx8", NE)):
    CONST[_n] = (_at, _w)
    _at += _w
NCONST = _at


def shape_constants():
    c = np.zeros((P, NCONST), np.float32)

    def put(name, value):
        a, w = CONST[name]
        c[:, a:a + w] = np.asarray(value, np.float32).reshape(-1, w)

    p = np.arange(P)
    put("ident", np.eye(P))
    put("mean", np.full((P, P), 1.0 / CC))
    put("ones", np.ones((P, P)))
    put("before", p[:, None] < p[None, :])
    put("slot0", np.tile(p + 1, (P, 1)))
    put("slot1", np.tile(p + P + 1, (P, 1)))
    for name, theta, half in (("ret", 10000.0, 32), ("swa", 500000.0, 8)):
        inv = (1.0 / (np.float32(theta) ** (np.arange(half, dtype=np.float32) / np.float32(half)))).astype(np.float32)
        ang = np.arange(SEQ, dtype=np.float32)[:, None] * inv[None, :]
        for f, g in (("cos", np.cos), ("sin", np.sin)):
            put(f"{name}_{f}", g(ang).astype(np.float32).reshape(NT, P, half).transpose(1, 0, 2))
    lg = np.log(1.0 - 2.0 ** (-5.0 - np.arange(RH)))
    rel = np.arange(SEQ)[None, :] - p[:, None]
    near = np.where(rel[None] >= 0, np.exp(np.maximum(rel, 0)[None] * lg[:, None, None]), 0.0) * HD ** -0.5
    near = near[list(RET_HEADS)].transpose(1, 0, 2)
    put("decay", np.concatenate([near.reshape(P, -1), near[:, :, :P].reshape(P, -1)], 1))
    i, j = p[:, None], p[None, :]
    put("band", np.concatenate([np.where(j > i, 0.0, NEG), np.where(j <= i, 0.0, NEG)], 1) * HD ** 0.5)
    put("rev8", np.tile(NE - np.arange(NE), (P, 1)))
    put("idx8", np.tile(np.arange(NE), (P, 1)))
    return c


def trunk(nc, t_in, out):
    ctx = ExitStack()
    with ctx:
        def sb(name, shape, dt=F32):
            return ctx.enter_context(nc.sbuf_tensor(name, shape, dt))

        def sem(name):
            return ctx.enter_context(nc.semaphore(name))

        raw = sb("raw", [P, RAW, UNIT])
        w_hi = sb("w_hi", [P, SPLIT, UNIT], F32R)
        w_lo = sb("w_lo", [P, SPLIT, UNIT], F32R)
        const = sb("const", [P, NCONST])
        zeros = sb("zeros", [P, 512], BF16)
        x = sb("x", [P, NT, DM])
        h = sb("h", [P, NT, DM])
        gain_rows = sb("gain_rows", [4 * KD, P])
        gain_cols = sb("gain_cols", [P, 4 * KD])
        squares = sb("squares", [P, NT, 4])
        t_hi = sb("t_hi", [P, KD, SEQ], F32R)
        t_lo = sb("t_lo", [P, KD, SEQ], F32R)
        act_hi = sb("act_hi", [P, 512], F32R)
        act_lo = sb("act_lo", [P, 512], F32R)
        hid = sb("hid", [P, 512])
        gact = sb("gact", [P, 512])
        work = sb("work", [P, NT * 1792])
        z = work[:, :].rearrange("p (t n) -> p t n", t=NT)
        chan_rows = sb("chan_rows", [36, CC])
        chan = sb("chan", [P, NC_CH, 36])
        sinks = sb("sinks", [P, SH])
        glu = sb("glu", [P, NC_CH, CW - 1 + SEQ])
        conv = sb("conv", [P, NC_CH, SEQ])
        conv_sq = sb("conv_sq", [P, NC_CH, SEQ])
        conv_diag = sb("conv_diag", [P, SEQ])
        pw = sb("pw", [P, NC_CH, P])
        scores = [h[:, :, :].rearrange("p t n -> p (t n)")[:, 0:1536], sb("scores1", [P, 1536])[:, :]]
        ident_bf = sb("ident_bf", [P, P], BF16)
        band_bf = sb("band_bf", [P, 2 * P], BF16)
        probs_t = sb("probs_t", [P, SG, 384])
        sq_t = sb("sq_t", [P, SG, SEQ])
        sk_t = sb("sk_t", [P, SEQ])
        rq_t = sb("rq_t", [P, 2, SEQ])
        rk_t = sb("rk_t", [P, 2, SEQ])
        ret_s = sb("ret_s", [P, RH * 384])
        ret_o = sb("ret_o", [P, NT * RH, HD])
        rope_a = sb("rope_a", [P, 512])
        rope_b = sb("rope_b", [P, 512])
        tap_product = rope_a[:, :].rearrange("p (c n) -> p c n", c=NC_CH)
        small = sb("small", [P, 256])
        router = sb("router", [P, KD, NE])
        table = sb("table", [P, 4], I32)
        h_t = work[:, 0:KD * SEQ].rearrange("p (k n) -> p k n", k=KD)
        y_exp = work[:, 0:DM]
        gain_last = work[:, DM:2 * DM]
        pick = ret_s[:, 0:256].rearrange("p (t n) -> p t n", t=NT)
        pick_g = ret_s[:, 256:512].rearrange("p (t n) -> p t n", t=NT)
        pick_gt = ret_s[:, 512:768]
        mine = ret_s[:, 768:772]
        bank = [ctx.enter_context(nc.psum_tensor(f"bank{i}", [P, 512], F32)) for i in range(8)]

        def const_ap(name):
            a, w = CONST[name]
            return const[:, a:a + w]

        ident, before, ones, mean = (const_ap(n) for n in ("ident", "before", "ones", "mean"))

        raw_loaded = [sem(f"raw_loaded{i}") for i in range(RAW)]
        hi_done, lo_done, multiplied = sem("hi_done"), sem("lo_done"), sem("multiplied")
        vec_step, pool_step = sem("vec_step"), sem("pool_step")
        ident_loaded, const_loaded, router_loaded = sem("ident_loaded"), sem("const_loaded"), sem("router_loaded")
        x_loaded = [sem("x_loaded0"), sem("x_loaded1")]
        gain_loaded, gain_turned, gain_done = sem("gain_loaded"), sem("gain_turned"), sem("gain_done")
        last_gain_loaded, casts_done = sem("last_gain_loaded"), sem("casts_done")
        zeros_set = sem("zeros_set")
        x_updated = sem("x_updated")
        sq_summed, ms_done, rms_done = sem("sq_summed"), sem("ms_done"), sem("rms_done")
        h_normed = sem("h_normed")
        h_turned, t_hi_done, t_lo_done = sem("h_turned"), sem("t_hi_done"), sem("t_lo_done")
        stored = sem("stored")
        names = """chan_loaded chan_turned chan_done sinks_loaded pw_loaded pw_zeroed pads_zeroed
            gate_done glu_done z_copied conv_done conv_mean conv_centred conv_squared conv_var conv_var_eps
            conv_root conv_diag conv_rstd_made conv_scaled conv_act conv_mixed swa_roped ret_roped
            sq_turned sqt_copied score_made score_max probs_made sink_exp probs_scaled probs_turned probs_copied attended rq_turned
            rqt_copied ret_scored ret_decayed ret_attended ret_gate ret_var ret_std ret_normed ret_turned
            y_hi_done y_lo_done out_made far_taps""".split()
        S = [{n: sem(f"{n}_{l}") for n in names} for l in range(DEPTH)]
        gate_acted, hid_made, hid_hi, hid_lo = sem("gate_acted"), sem("hid_made"), sem("hid_hi"), sem("hid_lo")
        hid_turned, ffn_made = sem("hid_turned"), sem("ffn_made")
        logits_summed, logits_copied, logits_made, top_two, second_exp, chosen = (
            sem(n) for n in "logits_summed logits_copied logits_made top_two second_exp chosen".split())
        ranked, routed, gates_made, counted, table_made = (
            sem(n) for n in "ranked routed gates_made counted table_made".split())
        picks_made, x_gathered, x_hi, x_lo, g_turned, g_copied = (
            sem(n) for n in "picks_made x_gathered x_hi x_lo g_turned g_copied".split())
        y_copied_act, y_copied_vec, scattered = sem("y_copied_act"), sem("y_copied_vec"), sem("scattered")

        def u_count(c, turn):
            return 6 * turn + (c + 1)

        def load_unit(sp, c, turn, source):
            if not (isinstance(turn, int) and c + 6 * turn < RAW):
                sp.wait_ge(lo_done, u_count(c - RAW, turn))
            dst = raw[:, c % RAW, :].rearrange("p (k n) -> p k n", k=source.shape[1])
            sp.dma_start(dst, source).then_inc(raw_loaded[c % RAW], 16)

        def split_hi(act, c, turn):
            act.wait_ge(raw_loaded[c % RAW], 16 * (turn + (c // RAW + 1)))
            if not (isinstance(turn, int) and c + 6 * turn < SPLIT):
                act.wait_ge(multiplied, u_count(c - SPLIT, turn))
            act.activation(w_hi[:, c % SPLIT, :], raw[:, c % RAW, :], ACT.Copy).then_inc(hi_done, 1)

        def split_lo(dve, c, turn):
            dve.wait_ge(hi_done, u_count(c, turn))
            dve.tensor_tensor(w_lo[:, c % SPLIT, :], raw[:, c % RAW, :], w_hi[:, c % SPLIT, :].bitcast(F32),
                              ALU.subtract).then_inc(lo_done, 1)

        def unit(c, k):
            return [w[:, c % SPLIT, :].rearrange("p (k n) -> p k n", k=k) for w in (w_hi, w_lo)]

        def score_view(g, p, i):
            return scores[g][:, p * 256:(p + 1) * 256] if i else scores[g][:, 1024 + p * P:1024 + (p + 1) * P]

        SCORE_BANKS = ([4, 5, 6], [7, 2, 3])
        PROB_BANKS = ([4, 5, 6], [7, 0, 1])
        RET_BANKS = (5, 2, 3)
        ATTENDED = (4, 6)
        OUT_BANKS = (0, 1, 4, 6)
        OUT_ORDER = (1, 2, 0, 3)

        def score_bank(g, p, i):
            a, b, c = SCORE_BANKS[g]
            return bank[(a, b)[p // 2]][:, (p % 2) * 256:(p % 2 + 1) * 256] if i else bank[c][:, p * P:(p + 1) * P]

        def tokens2(b):
            return b[:, :].rearrange("p (t n) -> p t n", t=2)

        HI_LO = ((0, 0), (0, 1), (1, 0))

        win_v = [t_in["w_in"][l].rearrange("(k p) n -> p k n", p=P) for l in range(DEPTH)]
        wout_v = [t_in["w_out"][l].rearrange("(k p) n -> p k n", p=P) for l in range(DEPTH)]
        fg_v, fu_v = (t_in[n][0].rearrange("(k p) n -> p k n", p=P) for n in ("ffn_w_gate", "ffn_w_up"))
        fd_v = t_in["ffn_w_down"][0].rearrange("(k p) n -> p k n", p=P)
        eg_v, eu_v, ed_v = (t_in[n][0].rearrange("e (k p) n -> p e k n", p=P)
                            for n in ("moe_w_gate", "moe_w_up", "moe_w_down"))
        x_v = t_in["x"][0].rearrange("(t p) n -> p t n", p=P)
        out_v = out[0].rearrange("(t p) n -> p t n", p=P)
        gains = [t_in[n][l] for l in range(DEPTH) for n in ("norm_mix_g", "norm_ffn_g")]
        PARTS = [1, 2, 2, 2, 2]
        SUMMED = [NT * sum(PARTS[:n + 1]) for n in range(5)]

        block = ctx.enter_context(nc.Block())

        @block.sync
        def _(sp):
            def load_layer_vectors(l):
                s = S[l]
                if l:
                    sp.wait_ge(S[0]["chan_turned"], 1)
                    sp.wait_ge(S[0]["y_lo_done"], 8)
                sp.dma_start(chan_rows[0:CW, :], t_in["conv_dw_w"][l]).then_inc(s["chan_loaded"], 16)
                for r, n in enumerate(("conv_dw_b", "conv_ln_g", "conv_ln_b", "ret_gn_g")):
                    sp.dma_start(chan_rows[CW + r:CW + r + 1, :], t_in[n][l:l + 1, :]).then_inc(s["chan_loaded"], 16)
                sp.dma_start(sinks[:, :], t_in["attn_sinks"][l:l + 1, :].broadcast_to([P, SH])).then_inc(s["sinks_loaded"], 16)
                sp.wait_ge(s["pw_zeroed"], 1)
                for g in range(4):
                    a = 64 * (g % 2)
                    sp.dma_start(pw[a:a + 64, g // 2, a:a + 64], t_in["conv_pw_w"][l, g]).then_inc(s["pw_loaded"], 16)

            def load_mixer(l, first, last):
                c = MIX_BASE[l]
                for q in range(first, last):
                    if q < WIN_UNITS:
                        b = WIN_ORDER[q]
                        load_unit(sp, c + q, 0, win_v[l][:, :, b * 256:(b + 1) * 256])
                    else:
                        b = OUT_ORDER[q - WIN_UNITS]
                        load_unit(sp, c + q, 0, wout_v[l][:, 2 * b:2 * b + 2, :])

            for t in range(NT):
                sp.dma_start(x[:, t, :], x_v[:, t, :]).then_inc(x_loaded[t], 16)
            sp.dma_start(ident, t_in["constants"][:, 0:P]).then_inc(ident_loaded, 16)
            for n, g in enumerate(gains):
                sp.dma_start(gain_rows[n * KD:(n + 1) * KD, :], g.rearrange("(k p) -> k p", p=P)).then_inc(gain_loaded, 16)
            load_mixer(0, 0, 2)
            load_layer_vectors(0)
            load_mixer(0, 2, 4)
            sp.dma_start(const[:, P:], t_in["constants"][:, P:]).then_inc(const_loaded, 16)
            load_mixer(0, 4, MIX_UNITS)
            c = FFN_BASE
            load_unit(sp, c, 0, fg_v[:, :, 0:256])
            load_unit(sp, c + 1, 0, fu_v[:, :, 0:256])
            with sp.Fori(0, (FC - 1) // 2) as it:
                for j in range(2):
                    a = c + 2 + 3 * j
                    cols = bass.ds(it * 512 + (256 + 256 * j), 256)
                    load_unit(sp, a, it, fg_v[:, :, cols])
                    load_unit(sp, a + 1, it, fd_v[:, bass.ds(it * 4 + 2 * j, 2), :])
                    load_unit(sp, a + 2, it, fu_v[:, :, cols])
            load_unit(sp, c + 3 * FC - 1, 0, fd_v[:, 2 * (FC - 1):2 * FC, :])
            load_layer_vectors(1)
            load_mixer(1, 0, MIX_UNITS)
            sp.dma_start(router[:, :, :], t_in["moe_router"][0].rearrange("(k p) e -> p k e", p=P)).then_inc(router_loaded, 16)

            def load_item(e, turn):
                c = MOE_BASE

                def pair(c, turn, view, chunk, rows):
                    for k in range(2):
                        if rows:
                            source = view[:, e, bass.ds(chunk * 4 + 2 * k, 2), :]
                        else:
                            source = view[:, e, 4 * k:4 * k + 4, bass.ds(chunk * 512, 512)]
                        load_unit(sp, c + k, turn, squeeze(source))

                def squeeze(a):
                    return a if len(a.shape) == 3 else a.rearrange("p o k n -> p (o k) n")

                pair(c, turn, eg_v, 0, False)
                pair(c + 2, turn, eu_v, 0, False)
                with sp.Fori(0, EC - 1) as i:
                    pair(c + 4, turn + i, eg_v, i + 1, False)
                    pair(c + 6, turn + i, ed_v, i, True)
                    pair(c + 8, turn + i, eu_v, i + 1, False)
                pair(c + 4, turn + (EC - 1), ed_v, EC - 1, True)

            with sp.Fori(0, NE) as e:
                load_item(e, e * EC)
            sp.wait_ge(logits_made, 1)
            sp.dma_start(gain_last, t_in["final_norm_g"].unsqueeze(0).broadcast_to([P, DM])).then_inc(last_gain_loaded, 16)
            sp.wait_ge(table_made, 1)
            n_over = sp.value_load(table[0:1, 0:1], min_val=0, max_val=3)
            with sp.If(n_over > 0):
                with sp.Fori(0, n_over) as j:
                    load_item(sp.value_load(table[0:1, bass.ds(j + 1, 1)], min_val=0, max_val=NE - 1),
                              (j + NE) * EC)
            for q in range(4):
                sp.wait_ge(h_normed, 8 + q + 1)
                half = slice((q % 2) * 512, (q % 2 + 1) * 512)
                sp.dma_start(out_v[:, q // 2, half], h[:, q // 2, half]).then_inc(stored, 16)
            sp.wait_ge(stored, 16 * 4)

        @block.gpsimd
        def _(pool):
            n_step = [0]

            def link(ins):
                n_step[0] += 1
                ins.then_inc(pool_step, 1)
                pool.wait_ge(pool_step, n_step[0])

            def rope(heads, first, half, tab, done):
                view = z[:, :, first:first + heads * HD].rearrange("p t (h d) -> p t h d", d=HD)
                cos, sin = (const_ap(f"{tab}_{f}").rearrange("p (t d) -> p t d", t=NT) for f in ("cos", "sin"))
                a, b = (r[:, 0:heads * half].rearrange("p (h d) -> p h d", d=half) for r in (rope_a, rope_b))
                for t in range(NT):
                    x1, x2 = view[:, t, :, 0:half], view[:, t, :, half:2 * half]
                    c = cos[:, t, :].unsqueeze(1).broadcast_to([P, heads, half])
                    d = sin[:, t, :].unsqueeze(1).broadcast_to([P, heads, half])
                    link(pool.tensor_tensor(a, x1, d, ALU.mult))
                    link(pool.tensor_tensor(b, x2, d, ALU.mult))
                    link(pool.tensor_tensor(x1, x1, c, ALU.mult))
                    link(pool.tensor_tensor(x2, x2, c, ALU.mult))
                    link(pool.tensor_tensor(x1, x1, b, ALU.subtract))
                    pool.tensor_tensor(x2, x2, a, ALU.add).then_inc(done, 1)
                    pool.wait_ge(done, t + 1)

            pool.memset(zeros[:, :], 0.0).then_inc(zeros_set, 1)
            link(pool.memset(small[:, 9:10], -0.5))

            def inverse_root(a, width, counted, value, done):
                pool.wait_ge(counted, value)
                v = small[:, a:a + width]
                pool.tensor_tensor(v, v, small[:, 9:10].broadcast_to([P, width]), ALU.pow).then_inc(done, 1)

            pool.memset(pw[:, :, :], 0.0).then_inc(S[0]["pw_zeroed"], 1)
            pool.memset(glu[:, :, 0:CW - 1], 0.0).then_inc(S[0]["pads_zeroed"], 1)
            def inverse_rms(n):
                for t in range(NT):
                    inverse_root(2 + t, 1, ms_done, 2 * n + t + 1, rms_done)

            inverse_rms(0)
            pool.wait_ge(ident_loaded, 16)
            pool.wait_ge(const_loaded, 16)
            pool.tensor_copy(ident_bf[:, :], ident).then_inc(casts_done, 1)
            pool.tensor_copy(band_bf[:, :], const_ap("band")).then_inc(casts_done, 1)
            for l in range(DEPTH):
                s = S[l]
                if l:
                    pool.memset(pw[:, :, :], 0.0).then_inc(s["pw_zeroed"], 1)
                    inverse_rms(2)
                pool.wait_ge(s["glu_done"], 1)
                pool.wait_ge(s["chan_done"], 1)
                for n, k in enumerate(range(NEAR_TAPS, CW)):
                    dst = tap_product if n else conv_sq
                    for i in range(NC_CH):
                        pool.tensor_scalar(dst[:, i, :], glu[:, i, k:k + SEQ], chan[:, i, k:k + 1], None,
                                           ALU.mult).then_inc(s["far_taps"], 1)
                    pool.wait_ge(s["far_taps"], 3 * n + 1 if n else 2)
                    if n:
                        pool.tensor_tensor(conv_sq[:, :, :], conv_sq[:, :, :], tap_product, ALU.add).then_inc(s["far_taps"], 1)
                        pool.wait_ge(s["far_taps"], 3 * n + 2)
                pool.wait_ge(s["z_copied"], 3)
                rope(SH + 2, 1024, 8, "swa", s["swa_roped"])
                pool.wait_ge(s["z_copied"], 5)
                rope(2 * RH, 0, 32, "ret", s["ret_roped"])
                inverse_root(136, NT * RH, s["ret_var"], 1, s["ret_std"])
                inverse_root(4, NT, s["conv_var_eps"], 1, s["conv_root"])
                inverse_rms(2 * l + 1)

            pool.wait_ge(routed, 1)
            pool.wait_ge(gates_made, 1)
            rank = small[:, 64:80].rearrange("p (t e) -> p t e", t=NT)
            gates = small[:, 80:96].rearrange("p (t e) -> p t e", t=NT)

            def make_picks(e, n, slots):
                pool.wait_ge(g_turned, n)
                pool.wait_ge(x_gathered, 2 * n)
                pool.wait_ge(picks_made, 7 * n)
                pool.tensor_copy(mine[:, 0:2], rank[:, :, bass.ds(e, 1)].rearrange("p t o -> p (t o)")
                                 ).then_inc(picks_made, 1)
                pool.tensor_copy(mine[:, 2:4], gates[:, :, bass.ds(e, 1)].rearrange("p t o -> p (t o)")
                                 ).then_inc(picks_made, 1)
                pool.wait_ge(picks_made, 7 * n + 2)
                pool.tensor_tensor(rope_a[:, 0:2], mine[:, 0:2], mine[:, 2:4], ALU.mult).then_inc(picks_made, 1)
                for t in range(NT):
                    pool.tensor_scalar(pick[:, t, :], slots, mine[:, t:t + 1], None,
                                       ALU.is_equal).then_inc(picks_made, 1)
                for t in range(NT):
                    pool.tensor_scalar(pick_g[:, t, :], slots, mine[:, t:t + 1], mine[:, 2 + t:3 + t],
                                       ALU.is_equal, ALU.mult).then_inc(picks_made, 1)

            with pool.Fori(1, NE) as e:
                make_picks(e, e, const_ap("slot0"))
            pool.wait_ge(table_made, 1)
            n_over = pool.value_load(table[0:1, 0:1], min_val=0, max_val=3)
            with pool.If(n_over > 0):
                with pool.Fori(0, n_over) as j:
                    e = pool.value_load(table[0:1, bass.ds(j + 1, 1)], min_val=0, max_val=NE - 1)
                    make_picks(e, j + NE, const_ap("slot1"))
            inverse_rms(4)

        @block.scalar
        def _(act):
            def sum_squares(t, part, first, width, unused=None):
                act.activation(h[:, t, first:first + width] if unused is None else unused, x[:, t, first:first + width], ACT.Square,
                               accum_out=squares[:, t, part:part + 1]).then_inc(sq_summed, 1)

            def turn_h(n):
                dst = h_t if n == 3 else t_hi
                for b in range(4):
                    act.wait_ge(h_turned, 4 * n + b + 1)
                    for k in range(2 * b, 2 * b + 2):
                        act.activation(dst[:, k, :], bank[4 + b][:, (k % 2) * 256:(k % 2 + 1) * 256], ACT.Copy,
                                       scale=gain_cols[:, n * KD + k:n * KD + k + 1]).then_inc(t_hi_done, 1)

            def round_y(l, k, src, scale=None):
                for i in range(2):
                    act.activation(t_hi[:, k + i, :], src[:, i * 256:(i + 1) * 256], ACT.Copy,
                                   scale=scale[i] if scale else 1.0).then_inc(S[l]["y_hi_done"], 1)

            def mixer(l):
                s = S[l]
                c = MIX_BASE[l]

                def copy_turned():
                    for b in range(3):
                        act.wait_ge(s["sq_turned"], b + 1)
                        if b < 2:
                            act.activation(sq_t[:, 2 * b:2 * b + 2, :], tokens2(bank[4 + b]),
                                           ACT.Copy).then_inc(s["sqt_copied"], 1)
                        else:
                            act.activation(sk_t[:, :], bank[6][:, 0:256], ACT.Copy).then_inc(s["sqt_copied"], 1)

                def exps(g):
                    act.wait_ge(s["score_max"], g + 1)
                    for i in range(2):
                        for p in range(SG):
                            n = g * 8 + i * 4 + p
                            act.activation(score_view(g, p, i), score_bank(g, p, i), ACT.Exp, scale=HD ** -0.5,
                                           bias=small[:, 32 + n:33 + n],
                                           accum_out=small[:, 48 + n:49 + n]).then_inc(s["probs_made"], 1)
                    act.activation(small[:, 96 + 8 * g:104 + 8 * g], small[:, 112 + 8 * g:120 + 8 * g],
                                   ACT.Exp).then_inc(s["sink_exp"], 1)

                def copy_probs(g):
                    for b in range(3):
                        act.wait_ge(s["probs_turned"], 3 * g + b + 1)
                        act.activation(probs_t[:, :, b * P:(b + 1) * P],
                                       bank[PROB_BANKS[g][b]][:, :].rearrange("p (h n) -> p h n", h=SG),
                                       ACT.Copy).then_inc(s["probs_copied"], 1)

                for q in range(WIN_UNITS):
                    split_hi(act, c + q + 2, 0)
                    if q == 6:
                        copy_turned()
                    elif q > 6:
                        exps(q - 7)
                    act.wait_ge(multiplied, c + q + 1)
                    if q == 0:
                        act.activation(gact[:, :], bank[0][:, :], ACT.Sigmoid).then_inc(s["gate_done"], 1)
                        act.wait_ge(s["chan_turned"], 1)
                        act.activation(chan[:, :, 0:35], bank[3][:, 0:72].rearrange("p (c n) -> p c n", c=2)[:, :, 0:35],
                                       ACT.Copy).then_inc(s["chan_done"], 1)
                    elif q > 1:
                        b = WIN_ORDER[q]
                        dst, src = z[:, :, b * 256:(b + 1) * 256], tokens2(bank[q % 2])
                        if b in (4, 5):
                            dst = z[:, :, 1024:1536].rearrange("p t (h g d) -> p t h g d", g=2, d=HD)[:, :, :, b - 4, :]
                            src = src.rearrange("p t (h d) -> p t h d", d=HD)
                        act.activation(dst, src, ACT.Copy).then_inc(s["z_copied"], 1)
                split_hi(act, c + WIN_UNITS + 2, 0)
                copy_probs(0)
                for b in range(2):
                    act.wait_ge(s["rq_turned"], b + 1)
                    act.activation((rq_t, rk_t)[b][:, :, :], tokens2(bank[2 + b]), ACT.Copy).then_inc(s["rqt_copied"], 1)
                for g in range(2):
                    act.wait_ge(s["attended"], g + 1)
                    if g == 0:
                        copy_probs(1)
                    round_y(l, 2 + 2 * g, bank[ATTENDED[g]])
                act.activation(tokens2(gact), z[:, :, 768:1024], ACT.Silu).then_inc(s["ret_gate"], 1)
                split_hi(act, c + WIN_UNITS + 3, 0)
                act.wait_ge(s["conv_centred"], 1)
                act.activation(conv_sq[:, :, :], conv[:, :, :], ACT.Square).then_inc(s["conv_squared"], 1)
                act.wait_ge(s["ret_turned"], 1)
                round_y(l, 0, bank[5], [chan[:, i, CW + 3:CW + 4] for i in range(2)])
                act.wait_ge(s["conv_scaled"], 1)
                for i in range(NC_CH):
                    act.activation(conv_sq[:, i, :], conv[:, i, :], ACT.Silu, bias=chan[:, i, CW + 2:CW + 3],
                                   scale=chan[:, i, CW + 1:CW + 2]).then_inc(s["conv_act"], 1)
                split_hi(act, c + WIN_UNITS + 4, 0)
                act.wait_ge(s["conv_mixed"], 1)
                round_y(l, 6, bank[3])
                for t in range(NT):
                    for i in range(2):
                        act.wait_ge(x_updated, 8 * l + 2 * t + i + 1)
                        sum_squares(t, i, i * 512, 512)
                split_hi(act, c + WIN_UNITS + 5, 0)

            for t in range(NT):
                act.wait_ge(x_loaded[t], 16)
                sum_squares(t, 0, 0, DM)
            act.wait_ge(gain_turned, 1)
            act.activation(gain_cols[:, :], bank[2][:, 0:4 * KD], ACT.Copy).then_inc(gain_done, 1)
            act.wait_ge(gain_done, 1)
            split_hi(act, 0, 0)
            turn_h(0)
            split_hi(act, 1, 0)
            mixer(0)
            turn_h(1)

            def act_gate(c, turn, m):
                act.wait_ge(multiplied, u_count(c, turn))
                if not (isinstance(m, int) and m == 0):
                    act.wait_ge(hid_made, m)
                act.activation(gact[:, :], bank[0][:, :], ACT.Silu).then_inc(gate_acted, 1)

            def round_ffn(m):
                act.wait_ge(hid_made, m + 1)
                act.activation(act_hi[:, :], hid[:, :], ACT.Copy).then_inc(hid_hi, 1)

            c = FFN_BASE
            split_hi(act, c + 2, 0)
            act_gate(c, 0, 0)
            split_hi(act, c + 3, 0)
            round_ffn(0)
            with act.Fori(0, (FC - 1) // 2) as it:
                for j in range(2):
                    a, m = c + 2 + 3 * j, it * 2 + (1 + j)
                    split_hi(act, a + 2, it)
                    act_gate(a, it, m)
                    split_hi(act, a + 3, it)
                    split_hi(act, a + 4, it)
                    round_ffn(m)
            split_hi(act, c + 3 * FC + 1, 0)
            for t in range(NT):
                for i in range(2):
                    act.wait_ge(x_updated, 4 + 2 * t + i + 1)
                    sum_squares(t, i, i * 512, 512)
            turn_h(2)
            mixer(1)
            turn_h(3)
            split_hi(act, MOE_BASE + 2, 0)
            act.wait_ge(top_two, 1)
            act.activation(small[:, 20:22], small[:, 18:20], ACT.Exp).then_inc(second_exp, 1)

            def round_x(n, b):
                act.wait_ge(x_gathered, 2 * n + (b + 1))
                for k in range(4):
                    g = 3 * KD + 4 * b + k
                    act.activation(t_hi[:, 4 * b + k, 0:P], bank[6 + b][:, k * P:(k + 1) * P], ACT.Copy,
                                   scale=gain_cols[:, g:g + 1]).then_inc(x_hi, 1)

            def round_hid(m):
                act.wait_ge(hid_turned, m + 1)
                act.activation(act_hi[:, :], bank[2][:, :], ACT.Copy).then_inc(hid_hi, 1)

            def first_gate(n, turn):
                if not (isinstance(n, int) and n == 0):
                    split_hi(act, MOE_BASE + 2, turn)
                split_hi(act, MOE_BASE + 3, turn)
                act_gate(MOE_BASE + 1, turn, n * EC + FC)

            def expert(n, turn, ahead):
                c = MOE_BASE
                m = n * EC
                act.wait_ge(g_turned, n + 1)
                act.activation(pick_gt, bank[3][:, 0:256], ACT.Copy).then_inc(g_copied, 1)
                split_hi(act, c + 4, turn)
                split_hi(act, c + 5, turn)
                with act.Fori(0, EC - 1) as i:
                    a, at = c + 4, turn + i
                    split_hi(act, a + 2, at)
                    round_hid(m + i)
                    split_hi(act, a + 3, at)
                    act_gate(a + 1, at, m + i + (FC + 1))
                    for k in range(4, 8):
                        split_hi(act, a + k, at)
                last = turn + (EC - 1)
                if ahead:
                    round_x(n + 1, 0)
                round_hid(m + (EC - 1))
                if ahead:
                    round_x(n + 1, 1)
                    split_hi(act, c + 6, last)
                    split_hi(act, c + 7, last)
                act.wait_ge(multiplied, u_count(c + 5, last))
                act.activation(y_exp[:, 0:512], bank[4][:, :], ACT.Copy).then_inc(y_copied_act, 1)
                if ahead:
                    first_gate(n + 1, turn + EC)
                else:
                    for q in range(4):
                        act.wait_ge(sq_summed, 4 * n + (SUMMED[3] - 4 * (NE - 1) + q))
                        act.wait_ge(x_updated, 4 * n + (12 + q + 1))
                        sum_squares(q // 2, q % 2, (q % 2) * 512, 512, gact[:, :])

            round_x(0, 0)
            round_x(0, 1)
            first_gate(0, 0)
            with act.Fori(0, NE - 1) as e:
                expert(e, e * EC, True)
            expert(NE - 1, (NE - 1) * EC, False)
            act.wait_ge(table_made, 1)
            n_over = act.value_load(table[0:1, 0:1], min_val=0, max_val=3)
            with act.If(n_over > 0):
                with act.Fori(0, n_over) as j:
                    for k in range(2):
                        split_hi(act, MOE_BASE + k, (j + NE) * EC)
                    round_x(j + NE, 0)
                    round_x(j + NE, 1)
                    first_gate(j + NE, (j + NE) * EC)
                    expert(j + NE, (j + NE) * EC, False)

        @block.vector
        def _(dve):
            n_step = [0]

            def link(ins):
                n_step[0] += 1
                ins.then_inc(vec_step, 1)
                dve.wait_ge(vec_step, n_step[0])

            def mean_square(n, t):
                dve.wait_ge(sq_summed, (SUMMED[n - 1] if n else 0) + PARTS[n] * (t + 1))
                total = squares[:, t, 0:1]
                if PARTS[n] > 1:
                    total = small[:, t:t + 1]
                    link(dve.tensor_reduce(total, squares[:, t, 0:PARTS[n]], AX, ALU.add))
                dve.tensor_scalar(small[:, 2 + t:3 + t], total, 1.0 / DM, EPS, ALU.mult, ALU.add).then_inc(ms_done, 1)

            def norm_rows(n, t):
                dve.wait_ge(rms_done, 2 * n + t + 1)
                if n < 4:
                    dve.tensor_scalar(h[:, t, :], x[:, t, :], small[:, 2 + t:3 + t], None, ALU.mult).then_inc(h_normed, 1)
                else:
                    dve.wait_ge(last_gain_loaded, 16)
                    for i in range(2):
                        half = slice(i * 512, (i + 1) * 512)
                        dve.scalar_tensor_tensor(out=h[:, t, half], in0=x[:, t, half], scalar=small[:, 2 + t:3 + t],
                                                 in1=gain_last[:, half], op0=ALU.mult, op1=ALU.mult).then_inc(h_normed, 1)

            def update_and_norm(n, sums, made, last_made, updates):
                for t in range(NT):
                    for i in range(2):
                        if 2 * t + i < 3:
                            dve.wait_ge(made, 2 * t + i + 1)
                        else:
                            dve.wait_ge(multiplied, last_made)
                        v = x[:, t, i * 512:(i + 1) * 512]
                        dve.tensor_tensor(v, v, bank[sums[2 * t + i]][:, :], ALU.add).then_inc(x_updated, 1)
                    if t:
                        dve.wait_ge(x_updated, updates)
                        norm_rows(n, 0)
                    mean_square(n, t)
                norm_rows(n, 1)

            def turn_h(n):
                for b in range(4):
                    dve.wait_ge(t_hi_done, KD * n + 2 * b + 2)
                    for k in range(2 * b, 2 * b + 2):
                        dve.scalar_tensor_tensor(out=t_lo[:, k, :], in0=bank[4 + b][:, (k % 2) * 256:(k % 2 + 1) * 256],
                                                 scalar=gain_cols[:, n * KD + k:n * KD + k + 1],
                                                 in1=t_hi[:, k, :].bitcast(F32), op0=ALU.mult,
                                                 op1=ALU.subtract).then_inc(t_lo_done, 1)

            def rest_y(l, k, src, n, scale=None):
                for i in range(2):
                    dve.wait_ge(S[l]["y_hi_done"], n + 2)
                    o, a, b = t_lo[:, k + i, :], src[:, i * 256:(i + 1) * 256], t_hi[:, k + i, :].bitcast(F32)
                    if scale:
                        ins = dve.scalar_tensor_tensor(out=o, in0=a, scalar=scale[i], in1=b, op0=ALU.mult, op1=ALU.subtract)
                    else:
                        ins = dve.tensor_tensor(o, a, b, ALU.subtract)
                    ins.then_inc(S[l]["y_lo_done"], 1)

            def mixer(l):
                s = S[l]
                c = MIX_BASE[l]
                taps = [(k, i) for k in range(NEAR_TAPS) for i in range(NC_CH)]

                def tap(k, i):
                    v, w = glu[:, i, k:k + SEQ], chan[:, i, k:k + 1]
                    if k == 0:
                        ins = dve.tensor_scalar(conv[:, i, :], v, w, chan[:, i, CW:CW + 1], ALU.mult, ALU.add)
                    else:
                        dve.wait_ge(s["conv_done"], (k - 1) * NC_CH + i + 1)
                        ins = dve.scalar_tensor_tensor(out=conv[:, i, :], in0=v, scalar=w, in1=conv[:, i, :],
                                                       op0=ALU.mult, op1=ALU.add)
                    ins.then_inc(s["conv_done"], 1)

                def some_taps(n):
                    for _ in range(min(n, len(taps))):
                        tap(*taps.pop(0))

                def score_max(g):
                    a, b, last = (bank[k] for k in SCORE_BANKS[g])
                    dve.wait_ge(s["score_made"], 3 * g + 3)
                    top = small[:, 176 + 8 * g:184 + 8 * g]
                    for k, v in enumerate((a, b)):
                        link(dve.tensor_reduce(top[:, 4 + 2 * k:6 + 2 * k], tokens2(v), AX, ALU.max))
                    link(dve.tensor_reduce(top[:, 0:4], last[:, :].rearrange("p (h n) -> p h n", h=SG), AX, ALU.max))
                    own = sinks[:, g * SG:(g + 1) * SG].unsqueeze(1).broadcast_to([P, 2, SG])
                    dve.wait_ge(s["sinks_loaded"], 16)
                    top = top.rearrange("p (i h) -> p i h", i=2)
                    link(dve.scalar_tensor_tensor(out=top, in0=top, scalar=HD ** -0.5, in1=own, op0=ALU.mult, op1=ALU.max))
                    neg = small[:, 32 + 8 * g:40 + 8 * g].rearrange("p (i h) -> p i h", i=2)
                    link(dve.tensor_scalar(neg, top, -1.0, None, ALU.mult))
                    dve.tensor_tensor(small[:, 112 + 8 * g:120 + 8 * g].rearrange("p (i h) -> p i h", i=2), own,
                                      neg, ALU.add).then_inc(s["score_max"], 1)

                def scale_probs(g):
                    dve.wait_ge(s["probs_made"], 8 * g + 8)
                    dve.wait_ge(s["sink_exp"], g + 1)
                    r = small[:, 160 + 8 * g:168 + 8 * g]
                    link(dve.tensor_tensor(r, small[:, 48 + 8 * g:56 + 8 * g], small[:, 96 + 8 * g:104 + 8 * g], ALU.add))
                    link(dve.reciprocal(r, r))
                    for i in range(2):
                        v = (scores[g][:, 0:1024] if i else scores[g][:, 1024:1536]).rearrange("p (h n) -> p h n", h=SG)
                        dve.tensor_tensor(v, v, r[:, 4 * i:4 * i + 4].unsqueeze(2).broadcast_to([P, SG, v.shape[2]]),
                                          ALU.mult).then_inc(s["probs_scaled"], 1)

                for q in range(WIN_UNITS):
                    split_lo(dve, c + q + 2, 0)
                    if q == 1:
                        dve.wait_ge(s["gate_done"], 1)
                        dve.wait_ge(multiplied, c + 2)
                        dve.wait_ge(S[0]["pads_zeroed"], 1)
                        dve.tensor_tensor(glu[:, :, CW - 1:], tokens2(bank[1]), tokens2(gact), ALU.mult).then_inc(s["glu_done"], 1)
                        dve.wait_ge(s["glu_done"], 1)
                        dve.wait_ge(s["chan_done"], 1)
                    if q == 7:
                        score_max(0)
                        score_max(1)
                    some_taps((0, 8, 7, 7, 7, 7, 7, 2, 4)[q])
                    if q >= 7:
                        scale_probs(q - 7)
                split_lo(dve, c + WIN_UNITS + 2, 0)
                some_taps(6)
                rest_y(l, 2, bank[ATTENDED[0]], 0)
                dve.wait_ge(const_loaded, 16)
                for i, b in enumerate(RET_BANKS):
                    dve.wait_ge(s["ret_scored"], (1, 2, 4)[i])
                    dve.tensor_tensor(ret_s[:, i * 512:(i + 1) * 512], bank[b][:, :],
                                      const_ap("decay")[:, i * 512:(i + 1) * 512], ALU.mult).then_inc(s["ret_decayed"], 1)
                rest_y(l, 4, bank[ATTENDED[1]], 2)
                dve.wait_ge(s["ret_attended"], 1)
                o = bank[2][:, :].rearrange("p (g d) -> p g d", d=HD)
                mu, var, rstd = (small[:, a:a + 8] for a in (128, 144, 136))

                def wide(v):
                    return v.unsqueeze(2).broadcast_to([P, NT * RH, HD])

                link(dve.tensor_reduce(mu, o, AX, ALU.add))
                link(dve.tensor_scalar(mu, mu, 1.0 / HD, None, ALU.mult))
                link(dve.tensor_tensor(ret_o[:, :, :], o, wide(mu), ALU.subtract))
                square = rope_a[:, :].rearrange("p (g d) -> p g d", d=HD)
                link(dve.tensor_tensor(square, ret_o[:, :, :], ret_o[:, :, :], ALU.mult))
                link(dve.tensor_reduce(var, square, AX, ALU.add))
                dve.tensor_scalar(rstd, var, 1.0 / HD, EPS, ALU.mult, ALU.add).then_inc(s["ret_var"], 1)
                some_taps(len(taps))
                dve.wait_ge(s["conv_done"], NEAR_TAPS * NC_CH)
                dve.wait_ge(s["far_taps"], 3 * (CW - NEAR_TAPS) - 1)
                dve.tensor_tensor(conv[:, :, :], conv[:, :, :], conv_sq[:, :, :], ALU.add).then_inc(s["conv_done"], 1)
                dve.wait_ge(s["ret_std"], 1)
                link(dve.tensor_tensor(ret_o[:, :, :], ret_o[:, :, :], wide(rstd), ALU.mult))
                dve.wait_ge(s["ret_gate"], 1)
                dve.tensor_tensor(ret_o[:, :, :], ret_o[:, :, :], gact[:, :].rearrange("p (g d) -> p g d", d=HD),
                                  ALU.mult).then_inc(s["ret_normed"], 1)
                dve.wait_ge(s["conv_mean"], 1)
                dve.wait_ge(s["conv_done"], NEAR_TAPS * NC_CH + 1)
                dve.tensor_tensor(conv[:, :, :], conv[:, :, :], bank[7][:, 0:256].unsqueeze(1).broadcast_to([P, 2, 256]),
                                  ALU.subtract).then_inc(s["conv_centred"], 1)
                split_lo(dve, c + WIN_UNITS + 3, 0)
                rest_y(l, 0, bank[5], 4, [chan[:, i, CW + 3:CW + 4] for i in range(2)])
                dve.wait_ge(s["conv_var"], 1)
                dve.tensor_scalar(small[:, 4:6], bank[7][:, 256:258], EPS, None, ALU.add).then_inc(s["conv_var_eps"], 1)
                dve.wait_ge(s["conv_root"], 1)
                for t in range(NT):
                    dve.tensor_scalar(conv_diag[:, t * P:(t + 1) * P], ident, small[:, 4 + t:5 + t], None,
                                      ALU.mult).then_inc(s["conv_diag"], 1)
                dve.wait_ge(s["conv_rstd_made"], 1)
                dve.tensor_tensor(conv[:, :, :], conv[:, :, :], bank[7][:, 256:512].unsqueeze(1).broadcast_to([P, 2, 256]),
                                  ALU.mult).then_inc(s["conv_scaled"], 1)
                split_lo(dve, c + WIN_UNITS + 4, 0)
                rest_y(l, 6, bank[3], 6)
                update_and_norm(2 * l + 1, OUT_BANKS, s["out_made"], c + MIX_UNITS, 8 * l + 4)

            for t in range(NT):
                mean_square(0, t)
            for t in range(NT):
                norm_rows(0, t)
            split_lo(dve, 0, 0)
            dve.wait_ge(gain_done, 1)
            turn_h(0)
            split_lo(dve, 1, 0)
            mixer(0)
            turn_h(1)
            split_lo(dve, MIX_UNITS + 1, 0)

            def make_hid(c, turn, m, up):
                dve.wait_ge(multiplied, u_count(c, turn))
                dve.wait_ge(gate_acted, m + 1)
                if not (isinstance(m, int) and m == 0):
                    dve.wait_ge(hid_hi, m)
                    dve.wait_ge(hid_lo, m)
                dve.tensor_tensor(hid[:, :], gact[:, :], up[:, :], ALU.mult).then_inc(hid_made, 1)

            def rest_hid(m, src):
                dve.wait_ge(hid_hi, m + 1)
                dve.tensor_tensor(act_lo[:, :], src[:, :], act_hi[:, :].bitcast(F32), ALU.subtract).then_inc(hid_lo, 1)

            c = FFN_BASE
            split_lo(dve, c + 2, 0)
            split_lo(dve, c + 3, 0)
            make_hid(c + 1, 0, 0, bank[2])
            rest_hid(0, hid)
            with dve.Fori(0, (FC - 1) // 2) as it:
                for j in range(2):
                    a, m = c + 2 + 3 * j, it * 2 + (1 + j)
                    split_lo(dve, a + 2, it)
                    split_lo(dve, a + 3, it)
                    split_lo(dve, a + 4, it)
                    make_hid(a + 2, it, m, bank[2])
                    rest_hid(m, hid)
            split_lo(dve, c + 3 * FC + 1, 0)
            update_and_norm(2, (4, 5, 6, 7), ffn_made, c + 3 * FC, 8)
            turn_h(2)
            mixer(1)
            split_lo(dve, MOE_BASE + 1, 0)

            def cols(a, w=2 * NE):
                return small[:, a:a + w]

            def by_token(v):
                return v.rearrange("p (t e) -> p t e", t=NT)

            def wide8(v):
                return v.unsqueeze(2).broadcast_to([P, NT, NE])

            idx = const_ap("rev8").unsqueeze(1).broadcast_to([P, NT, NE])
            logits, first, second, cand = (by_token(cols(a)) for a in (32, 96, 112, 160))
            top1, top2, pos, gap, e2, den, w1, w2 = (small[:, a:a + 2] for a in (10, 12, 14, 18, 20, 22, 24, 26))
            dve.wait_ge(logits_summed, 1)
            dve.tensor_copy(gact[0:NE, 0:SEQ], bank[3][0:NE, 0:SEQ]).then_inc(logits_copied, 1)
            dve.wait_ge(logits_made, 1)
            link(dve.tensor_copy(cols(32), bank[2][:, 0:2 * NE]))

            def one_hot(top, hot):
                link(dve.tensor_reduce(top, logits, AX, ALU.max))
                link(dve.tensor_tensor(cand, logits, wide8(top), ALU.is_equal))
                link(dve.tensor_tensor(cand, cand, idx, ALU.mult))
                link(dve.tensor_reduce(pos, cand, AX, ALU.max))
                link(dve.tensor_tensor(hot, cand, wide8(pos), ALU.is_equal))

            one_hot(top1, first)
            link(dve.scalar_tensor_tensor(out=logits, in0=first, scalar=-3e38, in1=logits, op0=ALU.mult, op1=ALU.add))
            one_hot(top2, second)
            dve.tensor_tensor(gap, top2, top1, ALU.subtract).then_inc(top_two, 1)
            sel = by_token(cols(192))
            dve.tensor_tensor(sel, first, second, ALU.add).then_inc(chosen, 1)
            gates, rank = by_token(cols(80)), by_token(cols(64))
            dve.wait_ge(ranked, 1)
            dve.scalar_tensor_tensor(out=rank, in0=by_token(bank[3][:, 0:16]), scalar=1.0, in1=sel, op0=ALU.add,
                                     op1=ALU.mult).then_inc(routed, 1)
            dve.wait_ge(routed, 1)
            for t in range(NT):
                dve.tensor_scalar(pick[:, t, :], const_ap("slot0"), rank[:, t, 0:1], None,
                                  ALU.is_equal).then_inc(picks_made, (4, 1)[t])
            dve.wait_ge(second_exp, 1)
            link(dve.tensor_scalar(den, e2, 1.0, None, ALU.add))
            link(dve.reciprocal(w1, den))
            link(dve.tensor_tensor(w2, e2, w1, ALU.mult))
            link(dve.tensor_tensor(gates, first, wide8(w1), ALU.mult))
            link(dve.tensor_tensor(second, second, wide8(w2), ALU.mult))
            dve.tensor_tensor(gates, gates, second, ALU.add).then_inc(gates_made, 1)
            dve.wait_ge(gates_made, 1)
            for t in range(NT):
                dve.tensor_scalar(pick_g[:, t, :], const_ap("slot0"), rank[:, t, 0:1], gates[:, t, 0:1],
                                  ALU.is_equal, ALU.mult).then_inc(picks_made, 1)
            def rest_x(n, b):
                dve.wait_ge(x_hi, 8 * n + (4 * b + 4))
                for k in range(4):
                    g = 3 * KD + 4 * b + k
                    dve.scalar_tensor_tensor(out=t_lo[:, 4 * b + k, 0:P], in0=bank[6 + b][:, k * P:(k + 1) * P],
                                             scalar=gain_cols[:, g:g + 1], in1=t_hi[:, 4 * b + k, 0:P].bitcast(F32),
                                             op0=ALU.mult, op1=ALU.subtract).then_inc(x_lo, 1)

            def expert(n, turn, ahead):
                c = MOE_BASE
                m = n * EC + FC
                split_lo(dve, c + 4, turn)
                split_lo(dve, c + 5, turn)
                make_hid(c + 3, turn, m, bank[1])

                def chunk(i, hid_first):
                    a, at = c + 4, turn + i
                    split_lo(dve, a + 2, at)
                    rest_hid(m + i, bank[2])
                    for k in range(3, 7):
                        split_lo(dve, a + k, at)
                    if hid_first:
                        make_hid(a + 5, at, m + i + 1, bank[1])
                        rest_hid(m + i + 1, bank[2])
                    split_lo(dve, a + 7, at)
                    if not hid_first:
                        make_hid(a + 5, at, m + i + 1, bank[1])

                with dve.Fori(0, EC - 1 if ahead else EC - 2) as i:
                    chunk(i, False)
                if not ahead:
                    chunk(EC - 2, True)
                last = turn + (EC - 1)
                if ahead:
                    rest_x(n + 1, 0)
                    rest_hid(m + (EC - 1), bank[2])
                    rest_x(n + 1, 1)
                    split_lo(dve, c + 6, last)
                    split_lo(dve, c + 7, last)
                dve.wait_ge(multiplied, u_count(c + 5, last))
                dve.tensor_copy(y_exp[:, 512:1024], bank[5][:, :]).then_inc(y_copied_vec, 1)
                if ahead:
                    split_lo(dve, c + 8, last)
                    split_lo(dve, c + 9, last)
                dve.wait_ge(x_updated, 4 * n + 12)
                for q in range(4):
                    dve.wait_ge(scattered, 4 * n + (q + 1))
                    v = x[:, q // 2, (q % 2) * 512:(q % 2 + 1) * 512]
                    dve.tensor_tensor(v, v, bank[6 + q % 2][:, :], ALU.add).then_inc(x_updated, 1)

            split_lo(dve, MOE_BASE + 2, 0)
            rest_x(0, 0)
            rest_x(0, 1)
            over, upto, hot = small[:, 232:240], small[:, 240:248], small[:, 248:256]
            listed = small[:, 96:100]
            dve.wait_ge(counted, 1)
            link(dve.tensor_scalar(over, bank[2][:, 16:24], float(P), None, ALU.is_gt))
            link(dve.memset(hot, 0.0))
            link(dve.tensor_tensor_scan(upto, over, hot, 0.0, ALU.add, ALU.add))
            link(dve.tensor_copy(listed[:, 0:1], upto[:, 7:8]))
            for j in range(3):
                link(dve.scalar_tensor_tensor(out=hot, in0=upto, scalar=float(j + 1), in1=over, op0=ALU.is_equal,
                                              op1=ALU.mult))
                link(dve.tensor_tensor(hot, hot, const_ap("idx8"), ALU.mult))
                link(dve.tensor_reduce(listed[:, j + 1:j + 2], hot, AX, ALU.add))
            dve.tensor_copy(table[:, :], listed).then_inc(table_made, 1)
            split_lo(dve, MOE_BASE + 3, 0)
            with dve.Fori(0, NE - 1) as e:
                expert(e, e * EC, True)
            expert(NE - 1, (NE - 1) * EC, False)
            dve.wait_ge(x_updated, 12 + 4 * NE)
            dve.wait_ge(table_made, 1)
            n_over = dve.value_load(table[0:1, 0:1], min_val=0, max_val=3)
            with dve.If(n_over > 0):
                with dve.Fori(0, n_over) as j:
                    for k in range(2):
                        split_lo(dve, MOE_BASE + k, (j + NE) * EC)
                    rest_x(j + NE, 0)
                    rest_x(j + NE, 1)
                    split_lo(dve, MOE_BASE + 2, (j + NE) * EC)
                    split_lo(dve, MOE_BASE + 3, (j + NE) * EC)
                    expert(j + NE, (j + NE) * EC, False)
                    dve.wait_ge(x_updated, 4 * j + (16 + 4 * NE))
                    dve.wait_ge(sq_summed, 4 * j + (SUMMED[4] + 4))
            for t in range(NT):
                mean_square(4, t)
            for t in range(NT):
                norm_rows(4, t)

        @block.tensor
        def _(pe):
            pe.wait_ge(zeros_set, 1)

            def warm(b, n):
                for _ in range(n):
                    pe.matmul(bank[b][:, :], zeros[:, 0:P], zeros[:, :], start=True, stop=True)

            def turn_rows(n):
                for t in range(NT):
                    pe.wait_ge(h_normed, 2 * n + t + 1)
                    for b in range(4):
                        for k in range(2):
                            f = (2 * b + k) * P
                            ins = pe.transpose(bank[4 + b][:, k * 256 + t * P:k * 256 + (t + 1) * P],
                                               h[:, t, f:f + P], ident)
                        if t:
                            ins.then_inc(h_turned, 1)

            def turn_channels(l):
                s = S[l]
                pe.wait_ge(s["chan_loaded"], 16 * 5)
                for i in range(NC_CH):
                    ins = pe.transpose(bank[3][:, i * 36:i * 36 + 35], chan_rows[0:35, i * P:(i + 1) * P], ident[0:35, 0:35])
                ins.then_inc(s["chan_turned"], 1)

            def rows_by_weights(dst, c, turn):
                w = unit(c, KD)
                for t in range(NT):
                    for k in range(KD):
                        for a, b in HI_LO:
                            ins = pe.matmul(dst[:, t * 256:(t + 1) * 256], (t_hi, t_lo)[a][:, k, t * P:(t + 1) * P],
                                            w[b][:, k, :], start=(k == 0 and (a, b) == (0, 0)),
                                            stop=(k == KD - 1 and (a, b) == (1, 0)))
                ins.then_inc(multiplied, 1)

            def weights_by_rows(dst, c, turn, arrived=None):
                w = unit(c, KD)
                for i in range(2):
                    for k in range(KD):
                        if i == 0 and arrived is not None:
                            pe.wait_ge(t_lo_done, arrived + k + 1)
                        for a, b in HI_LO:
                            ins = pe.matmul(dst[:, i * 256:(i + 1) * 256], w[b][:, k, i * P:(i + 1) * P],
                                            (t_hi, t_lo)[a][:, k, :], start=(k == 0 and (a, b) == (0, 0)),
                                            stop=(k == KD - 1 and (a, b) == (1, 0)))
                ins.then_inc(multiplied, 1)

            def mixer(l):
                s = S[l]
                c = MIX_BASE[l]
                def turn_attention():
                    pe.wait_ge(s["swa_roped"], 2)
                    for b in range(2):
                        for k in range(2):
                            p = 2 * b + k
                            for t in range(NT):
                                ins = pe.transpose(bank[4 + b][:, k * 256 + t * P:k * 256 + (t + 1) * P],
                                                   z[:, t, 1024 + p * P:1024 + (p + 1) * P], ident)
                        ins.then_inc(s["sq_turned"], 1)
                    for t in range(NT):
                        ins = pe.transpose(bank[6][:, t * P:(t + 1) * P], z[:, t, 1536:1664], ident)
                    ins.then_inc(s["sq_turned"], 1)

                def score(g):
                    a = 64 * g
                    if g == 0:
                        pe.wait_ge(s["sqt_copied"], 3)
                        pe.wait_ge(casts_done, 2)
                    for i in (1, 0):
                        for p in range(SG):
                            dst = score_bank(g, p, i)
                            first = 0 if i else P
                            pe.matmul(dst, sq_t[a:a + 64, p, i * P:(i + 1) * P], sk_t[a:a + 64, 0:2 * P - first],
                                      start=True, stop=False)
                            ins = pe.matmul(dst, ident_bf[:, :], band_bf[:, first:], start=False, stop=True)
                            if p == 3 or (i == 1 and p % 2):
                                ins.then_inc(s["score_made"], 1)

                def turn_probs(g):
                    pe.wait_ge(s["probs_scaled"], 2 * g + 2)
                    for b in range(3):
                        for p in range(SG):
                            v = score_view(g, p, 0) if b == 0 else score_view(g, p, 1)[:, (b - 1) * P:b * P]
                            ins = pe.transpose(bank[PROB_BANKS[g][b]][:, p * P:(p + 1) * P], v, ident)
                        ins.then_inc(s["probs_turned"], 1)

                def attend(g):
                    pe.wait_ge(s["probs_copied"], 3 * g + 3)
                    v = z[:, :, 1664 + g * HD:1664 + (g + 1) * HD]
                    for p in range(0, SG, 2):
                        o = [bank[ATTENDED[g]][64 * a:64 * a + 64, (p // 2) * 256:(p // 2 + 1) * 256] for a in range(2)]
                        for a in range(2):
                            pe.matmul(o[a], v[:, 0, :], probs_t[:, p + a, 0:256], start=True, stop=False)
                        for a in range(2):
                            ins = pe.matmul(o[a][:, P:], v[:, 1, :], probs_t[:, p + a, 256:384], start=False, stop=True)
                    ins.then_inc(s["attended"], 1)

                def turn_retention():
                    pe.wait_ge(s["ret_roped"], 2)
                    pe.wait_ge(s["probs_made"], 16)
                    for b in range(2):
                        for k in range(2):
                            for t in range(NT):
                                f = b * 256 + k * P
                                ins = pe.transpose(bank[2 + b][:, k * 256 + t * P:k * 256 + (t + 1) * P], z[:, t, f:f + P],
                                                   ident)
                        ins.then_inc(s["rq_turned"], 1)

                def project(q, sums=(0, 1, 2, 3)):
                    pe.wait_ge(lo_done, c + WIN_UNITS + q + 1)
                    pe.wait_ge(s["y_lo_done"], max(4, 2 * q + 2))
                    w = unit(c + WIN_UNITS + q, 2)
                    for n in sums:
                        b, t, i = OUT_BANKS[n], n // 2, n % 2
                        for f in range(2):
                            k = 2 * OUT_ORDER[q] + f
                            for u, v in HI_LO:
                                ins = pe.matmul(bank[b][:, :], (t_hi, t_lo)[u][:, k, t * P:(t + 1) * P],
                                                w[v][:, f, i * 512:(i + 1) * 512], start=(q == 0 and f == 0 and (u, v) == (0, 0)),
                                                stop=(q == 3 and f == 1 and (u, v) == (1, 0)), skip_group_check=True)
                        if n == 3:
                            ins.then_inc(multiplied, 1)
                        elif q == 3:
                            ins.then_inc(s["out_made"], 1)

                for q in range(WIN_UNITS):
                    pe.wait_ge(lo_done, c + q + 1)
                    if q == 2:
                        pe.wait_ge(s["gate_done"], 1)
                    elif q == 3:
                        pe.wait_ge(s["glu_done"], 1)
                    elif q > 3:
                        pe.wait_ge(s["z_copied"], q - 3)
                    if q == 0:
                        weights_by_rows(bank[0], c, 0, 2 * KD * l)
                        turn_channels(l)
                    elif q == 1:
                        weights_by_rows(bank[1], c + 1, 0)
                    else:
                        rows_by_weights(bank[q % 2], c + q, 0)
                    if q == 5:
                        turn_attention()
                    elif q == 6:
                        score(0)
                        score(1)
                turn_probs(0)
                turn_retention()
                pe.wait_ge(s["z_copied"], 7)
                turn_probs(1)
                attend(0)
                pe.wait_ge(s["rqt_copied"], 2)
                def retain(bank_at, p, far):
                    n = RET_HEADS.index(p)
                    q, k = (v[64 * (p % 2):64 * (p % 2) + 64, p // 2, :] for v in (rq_t, rk_t))
                    if far:
                        return pe.matmul(bank[bank_at][:, n * P:(n + 1) * P], k[:, P:], q[:, P:], start=True, stop=True)
                    return pe.matmul(bank[bank_at][:, (n % 2) * 256:(n % 2 + 1) * 256], k[:, 0:P], q, start=True, stop=True)

                for p in range(RH):
                    ins = retain(RET_BANKS[p % 2], p, False)
                    if p >= 2:
                        ins.then_inc(s["ret_scored"], 1)
                for p in RET_HEADS:
                    if p == 1:
                        pe.wait_ge(s["ret_scored"], 3)
                    ins = retain(RET_BANKS[2], p, True)
                    if p >= 2:
                        ins.then_inc(s["ret_scored"], 1)
                attend(1)
                pe.wait_ge(s["ret_decayed"], 3)
                for t in range(NT):
                    for i in range(RH):
                        o = bank[2][:, (t * RH + i) * HD:(t * RH + i + 1) * HD]
                        v = z[:, :, 512 + i * HD:512 + (i + 1) * HD]
                        n = RET_HEADS.index(i)
                        ins = pe.matmul(o, ret_s[:, n * 256 + t * P:n * 256 + (t + 1) * P], v[:, 0, :], start=True,
                                        stop=(t == 0))
                        if t:
                            ins = pe.matmul(o, ret_s[:, 1024 + n * P:1024 + (n + 1) * P], v[:, 1, :], start=False, stop=True)
                ins.then_inc(s["ret_attended"], 1)
                project(0)
                pe.wait_ge(const_loaded, 16)
                pe.wait_ge(s["conv_done"], NEAR_TAPS * NC_CH + 1)
                for i in range(NC_CH):
                    ins = pe.matmul(bank[7][:, 0:256], mean, conv[:, i, :], start=(i == 0), stop=(i == 1))
                ins.then_inc(s["conv_mean"], 1)
                pe.wait_ge(s["ret_normed"], 1)
                flat = ret_o[:, :, :].rearrange("p g d -> p (g d)")
                for k in range(2):
                    for t in range(NT):
                        ins = pe.transpose(bank[5][:, k * 256 + t * P:k * 256 + (t + 1) * P],
                                           flat[:, t * 256 + k * P:t * 256 + (k + 1) * P], ident)
                ins.then_inc(s["ret_turned"], 1)
                pe.wait_ge(s["conv_squared"], 1)
                for t in range(NT):
                    for i in range(NC_CH):
                        ins = pe.matmul(bank[7][:, 256 + t:257 + t], conv_sq[:, i, t * P:(t + 1) * P], mean[:, 0:1],
                                        start=(i == 0), stop=(i == 1))
                ins.then_inc(s["conv_var"], 1)
                project(1, (0, 1))
                pe.wait_ge(s["conv_diag"], NT)
                pe.matmul(bank[7][:, 256:512], ones, conv_diag[:, :], start=True, stop=True).then_inc(s["conv_rstd_made"], 1)
                project(1, (2, 3))
                pe.wait_ge(s["conv_act"], 2)
                pe.wait_ge(s["pw_loaded"], 16 * 4)
                for i in range(NC_CH):
                    ins = pe.matmul(bank[3][:, i * 256:(i + 1) * 256], pw[:, i, :], conv_sq[:, i, :], start=True, stop=True)
                ins.then_inc(s["conv_mixed"], 1)
                project(2)
                project(3)
                warm(3, 4)

            warm(3, 14)
            pe.wait_ge(ident_loaded, 16)
            pe.wait_ge(gain_loaded, 16 * 4)
            pe.transpose(bank[2][:, 0:4 * KD], gain_rows[:, :], ident[0:4 * KD, 0:4 * KD]).then_inc(gain_turned, 1)
            turn_rows(0)
            mixer(0)
            turn_rows(1)

            c = FFN_BASE

            def clear(b):
                pe.matmul(bank[b][:, :], zeros[:, 0:P], zeros[:, :], start=True, stop=False, skip_group_check=True)

            def ffn_down(c, turn, m, last=False):
                pe.wait_ge(lo_done, u_count(c, turn))
                pe.wait_ge(hid_lo, m + 1)
                w = unit(c, 2)
                for t in range(NT):
                    for i in range(2):
                        for f in range(2):
                            for a, b in HI_LO:
                                ins = pe.matmul(bank[4 + 2 * t + i][:, :], (act_hi, act_lo)[a][:, f * 256 + t * P:f * 256 + (t + 1) * P],
                                                w[b][:, f, i * 512:(i + 1) * 512], start=False,
                                                stop=(last and f == 1 and (a, b) == (1, 0)), skip_group_check=True)
                        if last and 2 * t + i < 3:
                            ins.then_inc(ffn_made, 1)
                ins.then_inc(multiplied, 1)

            pe.wait_ge(lo_done, c + 1)
            weights_by_rows(bank[0], c, 0, KD)
            for b in range(4, 8):
                clear(b)
            pe.wait_ge(lo_done, c + 2)
            weights_by_rows(bank[2], c + 1, 0)
            with pe.Fori(0, (FC - 1) // 2) as it:
                for j in range(2):
                    a, m = c + 2 + 3 * j, it * 2 + (1 + j)
                    pe.wait_ge(lo_done, u_count(a, it))
                    pe.wait_ge(gate_acted, m)
                    weights_by_rows(bank[0], a, it)
                    ffn_down(a + 1, it, m - 1)
                    pe.wait_ge(lo_done, u_count(a + 2, it))
                    pe.wait_ge(hid_made, m)
                    weights_by_rows(bank[2], a + 2, it)
            ffn_down(c + 3 * FC - 1, 0, FC - 1, True)
            warm(3, 4)
            turn_rows(2)
            mixer(1)
            turn_rows(3)

            pe.wait_ge(router_loaded, 16)
            for k in range(KD):
                pe.wait_ge(t_hi_done, 3 * KD + k + 1)
                ins = pe.matmul(bank[3][0:NE, 0:SEQ], router[:, k, :], h_t[:, k, :], start=(k == 0), stop=(k == KD - 1))
            ins.then_inc(logits_summed, 1)
            pe.wait_ge(logits_copied, 1)
            for t in range(NT):
                ins = pe.transpose(bank[2][:, t * NE:(t + 1) * NE], gact[0:NE, t * P:(t + 1) * P], ident[0:NE, 0:NE])
            ins.then_inc(logits_made, 1)
            warm(0, 8)
            pe.wait_ge(chosen, 1)
            sel = small[:, 192:208]
            pe.matmul(bank[3][:, 0:16], before, sel, start=True, stop=True)
            pe.matmul(bank[3][:, 8:16], ones, sel[:, 0:8], start=False, stop=True, skip_group_check=True).then_inc(ranked, 1)
            pe.matmul(bank[2][:, 16:24], ones, sel[:, 0:8], start=True, stop=False)
            pe.matmul(bank[2][:, 16:24], ones, sel[:, 8:16], start=False, stop=True).then_inc(counted, 1)
            warm(0, 6)

            def gather(n, b, before_it):
                pe.wait_ge(picks_made, 7 * n + 5)
                if before_it is not None:
                    pe.wait_ge(x_updated, before_it)
                for k in range(4):
                    f = (4 * b + k) * P
                    for t in range(NT):
                        ins = pe.matmul(bank[6 + b][:, k * P:(k + 1) * P], h[:, t, f:f + P], pick[:, t, :],
                                        start=(t == 0), stop=(t == 1))
                ins.then_inc(x_gathered, 1)

            def rows_by_expert(dst, c, turn, half):
                pe.wait_ge(lo_done, u_count(c, turn))
                w = unit(c, 4)
                for k in range(4):
                    for a, b in HI_LO:
                        ins = pe.matmul(dst[:, :], (t_hi, t_lo)[a][:, 4 * half + k, 0:P], w[b][:, k, :],
                                        start=(half == 0 and k == 0 and (a, b) == (0, 0)),
                                        stop=(half == 1 and k == 3 and (a, b) == (1, 0)), skip_group_check=True)
                ins.then_inc(multiplied, 1)

            def turn_hid(m):
                pe.wait_ge(hid_made, m + 1)
                pe.wait_ge(hid_lo, m)
                for k in range(4):
                    ins = pe.transpose(bank[2][:, k * P:(k + 1) * P], hid[:, k * P:(k + 1) * P], ident)
                ins.then_inc(hid_turned, 1)

            def expert_down(c, turn, m, half, last):
                pe.wait_ge(lo_done, u_count(c, turn))
                pe.wait_ge(hid_lo, m + 1)
                w = unit(c, 2)
                for f in range(2):
                    for i in range(2):
                        for a, b in HI_LO:
                            ins = pe.matmul(bank[4 + i][:, :], (act_hi, act_lo)[a][:, (2 * half + f) * P:(2 * half + f + 1) * P],
                                            w[b][:, f, i * 512:(i + 1) * 512], start=False,
                                            stop=(last and half == 1 and f == 1 and (a, b) == (1, 0)), skip_group_check=True)
                ins.then_inc(multiplied, 1)

            def first_gate(n, turn):
                pe.wait_ge(gate_acted, n * EC + FC)
                for i in range(2):
                    pe.wait_ge(x_lo, 8 * n + 4 * (i + 1))
                    rows_by_expert(bank[0], MOE_BASE + i, turn, i)

            def expert(n, turn, ahead):
                c = MOE_BASE
                m = n * EC + FC
                clear(4)
                clear(5)
                pe.wait_ge(picks_made, 7 * n + 7)
                for t in range(NT):
                    ins = pe.transpose(bank[3][:, t * P:(t + 1) * P], pick_g[:, t, :], ident)
                ins.then_inc(g_turned, 1)
                pe.wait_ge(hid_made, m)
                for i in range(2):
                    rows_by_expert(bank[1], c + 2 + i, turn, i)
                with pe.Fori(0, EC - 1) as i:
                    a, at = c + 4, turn + i
                    pe.wait_ge(gate_acted, m + i + 1)
                    rows_by_expert(bank[0], a, at, 0)
                    turn_hid(m + i)
                    rows_by_expert(bank[0], a + 1, at, 1)
                    for k in range(2):
                        expert_down(a + 2 + k, at, m + i, k, False)
                    for k in range(2):
                        rows_by_expert(bank[1], a + 4 + k, at, k)
                if ahead:
                    gather(n + 1, 0, 4 * n + 12)
                else:
                    warm(6, 3)
                turn_hid(m + (EC - 1))
                if ahead:
                    gather(n + 1, 1, None)
                if not ahead:
                    warm(6, 4)
                for k in range(2):
                    expert_down(c + 4 + k, turn + (EC - 1), m + (EC - 1), k, True)
                if ahead:
                    first_gate(n + 1, turn + EC)
                pe.wait_ge(g_copied, n + 1)
                pe.wait_ge(y_copied_act, n + 1)
                pe.wait_ge(y_copied_vec, n + 1)
                for q in range(4):
                    t, i = q // 2, q % 2
                    if q >= 2:
                        pe.wait_ge(x_updated, 4 * n + (12 + q - 1))
                    pe.matmul(bank[6 + i][:, :], pick_gt[:, t * P:(t + 1) * P], y_exp[:, i * 512:(i + 1) * 512],
                              start=True, stop=True).then_inc(scattered, 1)

            gather(0, 0, None)
            gather(0, 1, None)
            first_gate(0, 0)
            with pe.Fori(0, NE - 1) as e:
                expert(e, e * EC, True)
            expert(NE - 1, (NE - 1) * EC, False)
            pe.wait_ge(table_made, 1)
            n_over = pe.value_load(table[0:1, 0:1], min_val=0, max_val=3)
            with pe.If(n_over > 0):
                with pe.Fori(0, n_over) as j:
                    gather(j + NE, 0, 4 * j + (12 + 4 * NE))
                    gather(j + NE, 1, None)
                    first_gate(j + NE, (j + NE) * EC)
                    expert(j + NE, (j + NE) * EC, False)


INPUTS = ["x", "norm_mix_g", "w_in", "ret_gn_g", "attn_sinks", "conv_dw_w", "conv_dw_b", "conv_ln_g", "conv_ln_b",
          "conv_pw_w", "w_out", "norm_ffn_g", "ffn_w_gate", "ffn_w_up", "ffn_w_down", "moe_router", "moe_w_gate",
          "moe_w_up", "moe_w_down", "final_norm_g"]


def kernel(**inputs):
    import concourse.bacc as bacc
    from concourse.bass_utils import run_bass_kernel_spmd

    nc = bacc.Bacc("TRN2", target_bir_lowering=False, num_devices=1)
    arrays = {f"in_{n}": np.ascontiguousarray(inputs[n]) for n in INPUTS}
    arrays["in_constants"] = shape_constants()
    t_in = {n[3:]: nc.dram_tensor(n, a.shape, mybir.dt.from_np(a.dtype), kind="ExternalInput").ap()
            for n, a in arrays.items()}
    out = nc.dram_tensor("out", (1, SEQ, DM), F32, kind="ExternalOutput").ap()
    trunk(nc, t_in, out)
    return run_bass_kernel_spmd(nc, [arrays], core_ids=[0]).results[0]["out"]
```
